# Optimizing a Trainium2 kernel written in Bass

```python
import math
import jax, jax.numpy as jnp
from jax import lax
import numpy as np

D_MODEL = 1024
BATCH = 1
SEQ = 256
DEPTH = 2

HEAD_DIM = 64
BRANCH_DIM = 512
CONV_CH = BRANCH_DIM
CONV_K = 3
ATT_HEADS = BRANCH_DIM // HEAD_DIM
ATT_DIM = ATT_HEADS * HEAD_DIM
RWKV_HEADS = BRANCH_DIM // HEAD_DIM
RWKV_DIM = RWKV_HEADS * HEAD_DIM
DECAY_LORA = 64
AAA_LORA = 64
GATE_LORA = 128
N_BRANCH = 3
MIX_DIM = CONV_CH + ATT_DIM + RWKV_DIM
MOBA_BLOCK = 256
MOBA_TOPK = 3
MOBA_Q_CHUNK = 32
ROPE_THETA = 10000.0
D_FF = 2816
N_EXPERTS = 8
EXPERT_TOPK = 2
MOE_ROWS = 256
LN_EPS = 1e-5
GN_EPS = 64e-5
DN_ALPHA = (2 * DEPTH) ** 0.25
DN_BETA = (8 * DEPTH) ** -0.25
N_DENSE = (DEPTH + 1) // 2
N_MOE = DEPTH // 2
IN_SPLITS = [CONV_CH] * 3 + [ATT_DIM] * 3 + [RWKV_DIM] * 3 + [DECAY_LORA, AAA_LORA, GATE_LORA] + [D_MODEL] * N_BRANCH
P_TOTAL = sum(IN_SPLITS)
SHIFT_DIM = 3 * RWKV_DIM + DECAY_LORA + AAA_LORA + GATE_LORA

kernel_name = "hybrid_conv_moba_rwkv7_deepnorm_moe"

def split_cols(a, sizes):
    idx = np.cumsum(sizes)[:-1].tolist()
    return jnp.split(a, idx, axis=-1)

def layer_norm(x, g, b):
    xf = x.astype(jnp.float32)
    mu = xf.mean(-1, keepdims=True)
    var = jnp.square(xf - mu).mean(-1, keepdims=True)
    return ((xf - mu) * lax.rsqrt(var + LN_EPS) * g + b).astype(x.dtype)

def token_shift(u):
    return jnp.pad(u, ((0, 0), (1, 0), (0, 0)))[:, :-1]

def rope(x, pos):
    half = HEAD_DIM // 2
    inv = ROPE_THETA ** (-jnp.arange(half, dtype=jnp.float32) / half)
    ang = pos.astype(jnp.float32)[:, None] * inv[None, :]
    cos = jnp.cos(ang)[None, :, None, :]
    sin = jnp.sin(ang)[None, :, None, :]
    x1 = x[..., :half].astype(jnp.float32)
    x2 = x[..., half:].astype(jnp.float32)
    return jnp.concatenate([x1 * cos - x2 * sin, x2 * cos + x1 * sin], -1).astype(x.dtype)

def short_conv(u, w):
    return lax.conv_general_dilated(
        u, w[:, None, :], window_strides=(1,), padding=((CONV_K - 1, 0),),
        dimension_numbers=('NWC', 'WIO', 'NWC'), feature_group_count=u.shape[-1])

def moba_attention(q, k, v):
    B, T, H, Dh = q.shape
    nb = -(-T // MOBA_BLOCK)
    tp = nb * MOBA_BLOCK
    pad = ((0, 0), (0, tp - T), (0, 0), (0, 0))
    q = jnp.pad(q, pad).transpose(0, 2, 1, 3)
    k = jnp.pad(k, pad).transpose(0, 2, 1, 3)
    v = jnp.pad(v, pad).transpose(0, 2, 1, 3)
    kb = k.reshape(B, H, nb, MOBA_BLOCK, Dh)
    vb = v.reshape(B, H, nb, MOBA_BLOCK, Dh)
    kmean = kb.astype(jnp.float32).mean(3)
    topk = min(MOBA_TOPK, nb)
    scale = Dh ** -0.5
    blk_ids = jnp.arange(nb)
    gather = jax.vmap(jax.vmap(lambda blocks, idx: blocks[idx]))

    def chunk(c):
        q0 = c * MOBA_Q_CHUNK
        qc = lax.dynamic_slice_in_dim(q, q0, MOBA_Q_CHUNK, axis=2)
        own = q0 // MOBA_BLOCK
        qpos = q0 + jnp.arange(MOBA_Q_CHUNK)
        gate = jnp.einsum('bhqd,bhnd->bhqn', qc.astype(jnp.float32), kmean)
        gate = jnp.where(blk_ids < own, gate, -jnp.inf)
        _, sel = lax.top_k(gate, topk)
        sel_ok = sel < own
        k_sel = gather(kb, sel)
        v_sel = gather(vb, sel)
        s_sel = jnp.einsum('bhqd,bhqnkd->bhqnk', qc, k_sel).astype(jnp.float32) * scale
        s_sel = jnp.where(sel_ok[..., None], s_sel, -jnp.inf)
        s_sel = s_sel.reshape(B, H, MOBA_Q_CHUNK, topk * MOBA_BLOCK)
        k_own = lax.dynamic_index_in_dim(kb, own, axis=2, keepdims=False)
        v_own = lax.dynamic_index_in_dim(vb, own, axis=2, keepdims=False)
        s_own = jnp.einsum('bhqd,bhkd->bhqk', qc, k_own).astype(jnp.float32) * scale
        kpos = own * MOBA_BLOCK + jnp.arange(MOBA_BLOCK)
        s_own = jnp.where(kpos[None, :] <= qpos[:, None], s_own, -jnp.inf)
        p = jax.nn.softmax(jnp.concatenate([s_sel, s_own], -1), axis=-1).astype(v.dtype)
        p_sel = p[..., :topk * MOBA_BLOCK].reshape(B, H, MOBA_Q_CHUNK, topk, MOBA_BLOCK)
        p_own = p[..., topk * MOBA_BLOCK:]
        return (jnp.einsum('bhqnk,bhqnkd->bhqd', p_sel, v_sel)
                + jnp.einsum('bhqk,bhkd->bhqd', p_own, v_own))

    o = lax.map(chunk, jnp.arange(tp // MOBA_Q_CHUNK))
    o = o.transpose(1, 0, 3, 2, 4).reshape(B, tp, H, Dh)
    return o[:, :T]

def delta_rule_scan(r, w, k, v, kk, a):
    B, T, H, N = r.shape
    xs = tuple(t.transpose(1, 0, 2, 3) for t in (r, w, k, v, kk, a))

    def step(S, inp):
        r_t, w_t, k_t, v_t, kk_t, a_t = inp
        sa = jnp.einsum('bhvk,bhk->bhv', S, -kk_t)
        S = S * w_t[:, :, None, :] + sa[..., None] * (kk_t * a_t)[:, :, None, :] + v_t[..., None] * k_t[:, :, None, :]
        return S, jnp.einsum('bhvk,bhk->bhv', S, r_t)

    S0 = jnp.zeros((B, H, N, N), r.dtype)
    _, y = lax.scan(step, S0, xs)
    return y.transpose(1, 0, 2, 3)

def rwkv7_time_mix(r, k, v, wl, al, gl, shift_mu, decay_w0, decay_w2, aaa_a0, aaa_w2, gate_w2,
                   k_k, k_a, r_k, gn_g, gn_b):
    B, T, _ = r.shape
    u = jnp.concatenate([r, k, v, wl, al, gl], -1).astype(jnp.float32)
    u = u + (token_shift(u) - u) * shift_mu
    r, k, v, wl, al, gl = split_cols(u, [RWKV_DIM] * 3 + [DECAY_LORA, AAA_LORA, GATE_LORA])
    w = -jax.nn.softplus(-(decay_w0 + jnp.tanh(wl) @ decay_w2)) - 0.5
    decay = jnp.exp(-jnp.exp(w))
    a = jax.nn.sigmoid(aaa_a0 + al @ aaa_w2)
    g = jax.nn.sigmoid(gl) @ gate_w2
    heads = lambda t: t.reshape(B, T, RWKV_HEADS, HEAD_DIM)
    kk = heads(k * k_k)
    kk = kk / jnp.maximum(jnp.linalg.norm(kk, axis=-1, keepdims=True), 1e-12)
    k = k * (1.0 + (a - 1.0) * k_a)
    rh, kh, vh, ah = heads(r), heads(k), heads(v), heads(a)
    y = delta_rule_scan(rh, heads(decay), kh, vh, kk, ah)
    mu = y.mean(-1, keepdims=True)
    var = jnp.square(y - mu).mean(-1, keepdims=True)
    y = ((y - mu) * lax.rsqrt(var + GN_EPS)).reshape(B, T, RWKV_DIM) * gn_g + gn_b
    y = y + ((rh * kh * r_k).sum(-1, keepdims=True) * vh).reshape(B, T, RWKV_DIM)
    return y * g

def hybrid_mixer(x, w_in, conv_w, shift_mu, decay_w0, decay_w2, aaa_a0, aaa_w2, gate_w2,
                 k_k, k_a, r_k, gn_g, gn_b, w_branch, w_out):
    B, T, _ = x.shape
    proj = x @ w_in
    (c_h, c_b, c_c, q, k, v, rr, rk, rv, wl, al, gl,
     g_conv, g_att, g_rwkv) = split_cols(proj, IN_SPLITS)
    o_conv = c_b * short_conv(c_c * c_h, conv_w)
    pos = jnp.arange(T)
    qh = rope(q.reshape(B, T, ATT_HEADS, HEAD_DIM), pos)
    kh = rope(k.reshape(B, T, ATT_HEADS, HEAD_DIM), pos)
    o_att = moba_attention(qh, kh, v.reshape(B, T, ATT_HEADS, HEAD_DIM)).reshape(B, T, ATT_DIM)
    o_rwkv = rwkv7_time_mix(rr, rk, rv, wl, al, gl, shift_mu, decay_w0, decay_w2, aaa_a0, aaa_w2,
                            gate_w2, k_k, k_a, r_k, gn_g, gn_b).astype(x.dtype)
    p_conv, p_att, p_rwkv = jnp.split(w_branch, [CONV_CH, CONV_CH + ATT_DIM], axis=0)
    merged = (jax.nn.sigmoid(g_conv) * (o_conv @ p_conv)
              + jax.nn.sigmoid(g_att) * (o_att @ p_att)
              + jax.nn.sigmoid(g_rwkv) * (o_rwkv @ p_rwkv))
    return merged @ w_out

def swiglu(x, w_gate, w_up, w_down):
    return (jax.nn.silu(x @ w_gate) * (x @ w_up)) @ w_down

def moe_swiglu(x, router_w, w_gate, w_up, w_down):
    B, T, D = x.shape
    xt = x.reshape(-1, D)
    N = xt.shape[0]
    NK = N * EXPERT_TOPK
    logits = (xt @ router_w).astype(jnp.float32)
    top_logit, top_e = lax.top_k(logits, EXPERT_TOPK)
    gate = jax.nn.softmax(top_logit, axis=-1).astype(x.dtype)
    flat_e = top_e.reshape(-1)
    flat_tok = jnp.arange(NK, dtype=jnp.int32) // EXPERT_TOPK
    flat_gate = gate.reshape(-1)
    order = jnp.argsort(flat_e)
    se = flat_e[order]
    counts = jnp.zeros((N_EXPERTS,), jnp.int32).at[flat_e].add(1)
    padded = (counts + MOE_ROWS - 1) // MOE_ROWS * MOE_ROWS
    pad_end = jnp.cumsum(padded)
    pad_start = pad_end - padded
    start = jnp.cumsum(counts) - counts
    dest = pad_start[se] + jnp.arange(NK, dtype=jnp.int32) - start[se]
    n_blocks = -(-NK // MOE_ROWS) + N_EXPERTS
    n_rows = n_blocks * MOE_ROWS
    buf_tok = jnp.zeros((n_rows,), jnp.int32).at[dest].set(flat_tok[order])
    buf_gate = jnp.zeros((n_rows,), x.dtype).at[dest].set(flat_gate[order])
    blk_start = jnp.arange(n_blocks, dtype=jnp.int32) * MOE_ROWS
    blk_e = jnp.minimum(jnp.searchsorted(pad_end, blk_start, side='right'), N_EXPERTS - 1)
    xb = xt[buf_tok].reshape(n_blocks, MOE_ROWS, D)

    def expert_block(args):
        xr, e = args
        return swiglu(xr, w_gate[e], w_up[e], w_down[e])

    yb = lax.map(expert_block, (xb, blk_e)).reshape(n_rows, D)
    out = jnp.zeros_like(xt).at[buf_tok].add(yb * buf_gate[:, None])
    return out.reshape(B, T, D)

def setup_inputs(seed: int = 0) -> dict:
    key = jax.random.key(seed)
    ks = jax.random.split(key, 32)
    n = lambda i, shape, s: jax.random.normal(ks[i], shape, jnp.float32) * s
    L = DEPTH
    return {
        "x": n(0, (BATCH, SEQ, D_MODEL), 1.0),
        "w_in": n(1, (L, D_MODEL, P_TOTAL), D_MODEL ** -0.5),
        "conv_w": n(2, (L, CONV_K, CONV_CH), CONV_K ** -0.5),
        "shift_mu": jax.random.uniform(ks[3], (L, SHIFT_DIM), jnp.float32),
        "decay_w0": jax.random.uniform(ks[4], (L, RWKV_DIM), jnp.float32, -4.0, 0.5),
        "decay_w2": n(5, (L, DECAY_LORA, RWKV_DIM), 0.1 * DECAY_LORA ** -0.5),
        "aaa_a0": n(6, (L, RWKV_DIM), 0.1),
        "aaa_w2": n(7, (L, AAA_LORA, RWKV_DIM), AAA_LORA ** -0.5),
        "gate_w2": n(8, (L, GATE_LORA, RWKV_DIM), GATE_LORA ** -0.5),
        "k_k": 1.0 + n(9, (L, RWKV_DIM), 0.1),
        "k_a": 1.0 + n(10, (L, RWKV_DIM), 0.1),
        "r_k": n(11, (L, RWKV_HEADS, HEAD_DIM), 0.1),
        "gn_g": 1.0 + n(12, (L, RWKV_DIM), 0.1),
        "gn_b": n(13, (L, RWKV_DIM), 0.02),
        "w_branch": n(14, (L, MIX_DIM, D_MODEL), BRANCH_DIM ** -0.5),
        "w_out": n(15, (L, D_MODEL, D_MODEL), D_MODEL ** -0.5 * DN_BETA),
        "ln1_g": 1.0 + n(16, (L, D_MODEL), 0.1),
        "ln1_b": n(17, (L, D_MODEL), 0.02),
        "ln2_g": 1.0 + n(18, (L, D_MODEL), 0.1),
        "ln2_b": n(19, (L, D_MODEL), 0.02),
        "ffn_w_gate": n(20, (N_DENSE, D_MODEL, D_FF), D_MODEL ** -0.5),
        "ffn_w_up": n(21, (N_DENSE, D_MODEL, D_FF), D_MODEL ** -0.5),
        "ffn_w_down": n(22, (N_DENSE, D_FF, D_MODEL), D_FF ** -0.5 * DN_BETA),
        "router_w": n(23, (N_MOE, D_MODEL, N_EXPERTS), D_MODEL ** -0.5),
        "moe_w_gate": n(24, (N_MOE, N_EXPERTS, D_MODEL, D_FF), D_MODEL ** -0.5),
        "moe_w_up": n(25, (N_MOE, N_EXPERTS, D_MODEL, D_FF), D_MODEL ** -0.5),
        "moe_w_down": n(26, (N_MOE, N_EXPERTS, D_FF, D_MODEL), D_FF ** -0.5 * DN_BETA),
    }

def reference(x, w_in, conv_w, shift_mu, decay_w0, decay_w2, aaa_a0, aaa_w2, gate_w2, k_k, k_a, r_k,
              gn_g, gn_b, w_branch, w_out, ln1_g, ln1_b, ln2_g, ln2_b, ffn_w_gate, ffn_w_up, ffn_w_down,
              router_w, moe_w_gate, moe_w_up, moe_w_down):
    for l in range(DEPTH):
        h = hybrid_mixer(x, w_in[l], conv_w[l], shift_mu[l], decay_w0[l], decay_w2[l], aaa_a0[l],
                         aaa_w2[l], gate_w2[l], k_k[l], k_a[l], r_k[l], gn_g[l], gn_b[l],
                         w_branch[l], w_out[l])
        x = layer_norm(DN_ALPHA * x + h, ln1_g[l], ln1_b[l])
        if l % 2 == 0:
            j = l // 2
            f = swiglu(x, ffn_w_gate[j], ffn_w_up[j], ffn_w_down[j])
        else:
            j = l // 2
            f = moe_swiglu(x, router_w[j], moe_w_gate[j], moe_w_up[j], moe_w_down[j])
        x = layer_norm(DN_ALPHA * x + f, ln2_g[l], ln2_b[l])
    return x


_drawn_inputs = setup_inputs


def setup_inputs(seed=0):
    import zlib

    import numpy as np

    out = dict(_drawn_inputs(seed))
    spreads = {}
    factors = {'decay_w2': 8.0, 'aaa_a0': 5.771, 'k_k': 8.0, 'k_a': 2.775, 'gn_g': 3.312, 'gn_b': 8.0}
    for name, (base, spread) in spreads.items():
        noise = np.random.default_rng([zlib.crc32(name.encode()), seed]).standard_normal(out[name].shape)
        drawn = base * np.exp(spread * noise) if base else spread * noise
        out[name] = __import__('jax').numpy.asarray(drawn.astype(out[name].dtype))
    for name, factor in factors.items():
        out[name] = (out[name] * factor).astype(out[name].dtype)
    return out
```

```python
import math
from contextlib import ExitStack

import numpy as np

import concourse.bass as bass
from concourse import mybir

F32 = mybir.dt.float32
F32R = mybir.dt.float32r
I32 = mybir.dt.int32
U32 = mybir.dt.uint32
ALU = mybir.AluOpType
ACT = mybir.ActivationFunctionType
AX = mybir.AxisListType

P = 128
T = 256
D = 1024
KD = D // P
NT = T // P
L = 2
HD = 64
BR = 512
BT = BR // P
DFF = 2816
NPAIR = DFF // (2 * P)
NE = 8
KAPPA = math.exp(-0.5)
ALPHA = (2 * L) ** 0.25
LN_EPS, GN_EPS = 1e-5, 64e-5
UN = 2048
UD = 32
LEVELS = 7
POOL_MOE = 704

C_ID, C_BLK, C_ROT, C_SI, C_LEV = 0, P, 2 * P, 3 * P, 5 * P
C_END = C_LEV + LEVELS * P
A_COS, A_SIN, A_MASK, A_END = 0, T, 2 * T, 2 * T + 3 * P
E_ONE, E_IOTA, E_I8, E_END = 0, P, 3 * P, 3 * P + NE

PAR, NPAR = {}, 0
for _name, _n in (("mu", 14), ("w0", 4), ("a0", 4), ("k_k", 4), ("k_a", 4), ("r_k", 4), ("gn_g", 4),
                  ("gn_b", 4), ("conv0", 4), ("conv1", 4), ("conv2", 4), ("ln1_g", 8), ("ln1_b", 8),
                  ("ln2_g", 8), ("ln2_b", 8)):
    PAR[_name] = NPAR
    NPAR += _n

SEGMENTS = (("rkv", 3072, 7, 7), ("conv", 0, 6, 6), ("gate0", 4864, 4, 4), ("branch0", 0, 2, 4),
            ("qkv", 1536, 6, 6), ("gate1", 5888, 4, 4), ("branch1", 1, 2, 4),
            ("gate2", 6912, 4, 4), ("branch2", 2, 2, 4), ("out", 0, 4, 0))
UNIT0 = {s[0]: sum(x[2] for x in SEGMENTS[:i]) for i, s in enumerate(SEGMENTS)}
JOB0 = {s[0]: sum(x[3] for x in SEGMENTS[:i]) for i, s in enumerate(SEGMENTS)}
MIX_UNITS = sum(s[2] for s in SEGMENTS)
MIX_JOBS = sum(s[3] for s in SEGMENTS)
FFN_UNITS = 3 * NPAIR
MOE_U0 = 2 * MIX_UNITS + FFN_UNITS
DVE_U0 = MOE_U0 - 1
END_U = MOE_U0 + NE * FFN_UNITS


def layer_unit(l):
    return l * (MIX_UNITS + FFN_UNITS)


TIMELINE = (
    ("units", "rkv", 0, 7), ("shift",),
    ("units", "conv", 0, 6), ("lora", 0), ("norm", 0), ("conv",), ("osplit", 0),
    ("units", "gate0", 0, 4), ("prep", 0), ("units", "branch0", 0, 2),
    ("scores", 0), ("units", "qkv", 0, 6),
) + tuple(("level", 0, v) for v in range(1, LEVELS)) + (
    ("chain", 0), ("finish", 0),
    ("lora", 1), ("norm", 1), ("prep", 1), ("scores", 1),
) + tuple(("level", 1, v) for v in range(1, LEVELS)) + (
    ("chain", 1), ("finish", 1), ("units", "gate1", 0, 4),
    ("attention",), ("units", "branch1", 0, 2), ("osplit", 2),
    ("units", "gate2", 0, 4), ("units", "branch2", 0, 2), ("msplit",), ("units", "out", 0, 4),
)


def trunk(nc, x, x_t, w_in, w_branch, w_out, w2, gate_w2, par, const, const_att, const_moe, ln_gb,
          router, ffn_gate, ffn_up, ffn_down, moe_gate, moe_up, moe_down, out):
    ctx = ExitStack()
    with ctx:
        place = {"at": -(-nc.sbuf_base // 64) * 64}

        def sb_at(name, shape, offset, dt=F32):
            return nc.alloc_sbuf_tensor_at(name, shape, dt, offset=offset)

        def sb(name, shape, dt=F32):
            t = sb_at(name, shape, place["at"], dt)
            place["at"] += -(-4 * math.prod(shape[1:]) // 32) * 32
            return t

        raw = [sb(f"raw{i}", [P, UN]) for i in range(3)]
        w_hi = [sb(f"w_hi{i}", [P, UN], F32R) for i in range(3)]
        w_lo = [sb(f"w_lo{i}", [P, UN], F32R) for i in range(3)]
        x_hi = sb("x_hi", [P, KD, T], F32R)
        x_lo = sb("x_lo", [P, KD, T], F32R)
        o_hi = sb("o_hi", [P, BT, T], F32R)
        o_lo = sb("o_lo", [P, BT, T], F32R)
        xtok_at = place["at"]
        merged = sb("merged", [P, KD, T])
        xtok = sb_at("xtok", [P, NT, D], xtok_at)
        cst = sb("cst", [P, C_END])
        prm = sb("prm", [P, L, NPAR])
        small = sb("small", [P, 128])
        w2_s = sb("w2_s", [P, 2, BR])
        gw2_s = sb("gw2_s", [P, BR])
        arena = place["at"]
        rkvl = sb("rkvl", [P, 14, T])
        share = sb("share", [P, 12, T])
        sgate = sb("sgate", [P, KD, T])
        t1, t2, t3, t4, t6, td = (sb(f"t_{n}", [P, 2, T]) for n in ("a", "r", "k", "g", "b", "d"))
        ar = sb("ar", [P, 4, 2, 2, P])
        sc_at = place["at"]
        sc = sb("sc", [P, 8, 4, P])
        xm = sb("xm", [P, 8, P])
        xt = sb("xt", [P, 8, P])
        mt = sb("mt", [P, 8, P])
        vtok = sb("vtok", [P, NT, 2 * P])
        bktok = sb("bktok", [P, 2, 2 * P])
        g_s = sb("g_s", [P, 4, HD])
        u_s = sb("u_s", [P, 4, HD])
        s_s = sb("s_s", [P, 2, P])
        assert place["at"] <= nc.sbuf_usable_end, (place["at"], nc.sbuf_usable_end)
        end_of_sbuf = place["at"]
        dsh = sb_at("dsh", [P, 14, T], sc_at)
        place["at"] = sc_at
        qp = sb("qp", [P, 8, T])
        pr = sb("pr", [P, 8, 3, P])
        vatt = sb("vatt", [P, NT, BR])
        cat = sb("cat", [P, A_END])
        assert place["at"] <= end_of_sbuf
        place["at"] = arena
        xf = sb("xf", [P, KD, T])
        facc = sb("facc", [P, NT, D])
        y_sb = sb("y_sb", [P, D])
        sil = sb("sil", [P, 2, NT, P])
        hid = sb("hid", [P, 2, NT, P])
        sel = sb("sel", [P, NT, P])
        selg = sb("selg", [P, NT, P])
        selgt = sb("selgt", [P, T])
        cmo = sb("cmo", [P, E_END])
        rt_s = sb("rt_s", [P, KD, NE])
        route = sb("route", [P, NT, 64])
        idx = sb("idx", [P, NT, 8], U32)
        flag = sb("flag", [P, 2], I32)
        posm = sb("posm", [P, NT, NE])
        gsel = sb("gsel", [P, NT, NE])
        assert place["at"] <= sc_at
        gb = sb_at("gb", [P, 2, D], sc_at)

        W = [nc.alloc_psum_tensor(f"W{i}", [P, 512], F32) for i in range(3)]
        Y = [nc.alloc_psum_tensor(f"Y{i}", [P, 512], F32) for i in range(4)]
        E = nc.alloc_psum_tensor("E", [P, 512], F32)
        spill = nc.dram_tensor("x_spill", (T, D), F32, kind="Internal").ap()

        ident = cst[:, C_ID:C_ID + P]
        blk = cst[:, C_BLK:C_BLK + P]
        rot = cst[:, C_ROT:C_ROT + P]
        strict = cst[:, C_SI:C_SI + P]

        def tiles(ap, n=2):
            return ap.rearrange("p (m t) -> p m t", m=n)

        def level_mask(v):
            return cst[:, C_LEV + v * P:C_LEV + (v + 1) * P].unsqueeze(1).to_broadcast([P, 4, P])

        def par_col(l, name, i):
            return prm[:, l, PAR[name] + i:PAR[name] + i + 1]

        S = {}

        def sem(name):
            if name not in S:
                S[name] = ctx.enter_context(nc.semaphore(name))
            return S[name]

        raw_full = [sem(f"raw_full{i}") for i in range(3)]
        bank_free = [sem(f"bank_free{i}") for i in range(3)]
        hi_done, lo_pool, lo_dve = sem("hi_done"), sem("lo_pool"), sem("lo_dve")
        w_used = sem("w_used")

        def wait_jobs(eng, jobs):
            for b in range(3):
                eng.wait_ge(bank_free[b], (jobs - b + 2) // 3)

        def segment_dst(kind, q):
            if kind == "rkv":
                return rkvl[:, 2 * q:2 * q + 2, :]
            if kind in ("conv", "qkv"):
                return share[:, 2 * q:2 * q + 2, :]
            return sgate[:, 2 * q:2 * q + 2, :]

        def chained(eng, name):
            s, n = sem(name), [0]

            def link(ins):
                n[0] += 1
                ins.then_inc(s, 1)
                eng.wait_ge(s, n[0])
            return link

        block = ctx.enter_context(nc.Block())

        @block.sync
        def _(sp):
            def load(u, i, first, second):
                if u >= 3:
                    split, split_dve = u - 2 + 3 * i, u - 2 - DVE_U0 + 3 * i
                    if not isinstance(i, int):
                        split, split_dve = sp.to_reg(split), sp.to_reg(split_dve)
                    sp.wait_ge(hi_done, split)
                    sp.wait_ge(lo_pool, split)
                    if u - 3 >= DVE_U0:
                        sp.wait_ge(lo_dve, split_dve)
                sp.dma_start(*first).then_inc(raw_full[u % 3], 16)
                sp.dma_start(*second).then_inc(raw_full[u % 3], 16)

            def load_cols(u, i, w, col):
                d = raw[u % 3][:].rearrange("p (k c) -> p k c", k=KD)
                s = w[:, bass.ds(col, 256)].rearrange("(k p) c -> p k c", p=P)
                load(u, i, (d[:, 0:4, :], s[:, 0:4, :]), (d[:, 4:8, :], s[:, 4:8, :]))

            def load_gate_up(u, i, wg, wu, row, col):
                d = raw[u % 3][:].rearrange("p (k c) -> p k c", k=KD)
                g, v = (w[bass.ds(row, D), bass.ds(col, P)].rearrange("(k p) c -> p k c", p=P) for w in (wg, wu))
                load(u, i, (d[:, :, 0:P], g), (d[:, :, P:2 * P], v))

            def load_rows(u, i, w, row, n=2):
                d = raw[u % 3][:].rearrange("p (k c) -> p k c", k=n)
                s = w[bass.ds(row, n * P), :].rearrange("(k p) c -> p k c", p=P)
                h = n // 2
                load(u, i, (d[:, 0:h, :], s[:, 0:h, :]), (d[:, h:n, :], s[:, h:n, :]))

            def ffn_loads(u, i, wg, wu, wd, row_in, row_hid):
                with sp.Fori(1, NPAIR) as j:
                    load_gate_up(u + 2, i + j - 1, wg, wu, row_in, 256 * j)
                    load_gate_up(u + 3, i + j - 1, wg, wu, row_in, 256 * j + P)
                    load_rows(u + 4, i + j - 1, wd, row_hid + 256 * j - 256)
                load_rows(u + 2, i + NPAIR - 1, wd, row_hid + 256 * (NPAIR - 1))

            sp.dma_start(xf[:], x_t).then_inc(sem("x_full"), 16)
            sp.dma_start(cst[:], const).then_inc(sem("cst_full"), 16)
            sp.dma_start(prm[:], par).then_inc(sem("prm_full"), 16)
            for l in range(L):
                for kind, where, n, _ in SEGMENTS:
                    u = layer_unit(l) + UNIT0[kind]
                    if kind == "out":
                        for q in range(n):
                            load_rows(u + q, 0, w_out[l], 256 * q)
                    elif kind.startswith("branch"):
                        for q in range(n):
                            load_rows(u + q, 0, w_branch[l, :, q * 512:(q + 1) * 512], where * BR, BT)
                    elif n % 3 == 0 and u >= 3:
                        with sp.Fori(0, n // 3) as i:
                            for s in range(3):
                                load_cols(u + s, i, w_in[l], where + 256 * s + 768 * i)
                    else:
                        for q in range(n):
                            load_cols(u + q, 0, w_in[l], where + 256 * q)
                u = layer_unit(l) + MIX_UNITS
                if l == 0:
                    load_gate_up(u, 0, ffn_gate, ffn_up, 0, 0)
                    load_gate_up(u + 1, 0, ffn_gate, ffn_up, 0, P)
                    ffn_loads(u, 0, ffn_gate, ffn_up, ffn_down, 0, 0)

            def expert_loads(u):
                with sp.Fori(0, NE) as e:
                    ffn_loads(u, NPAIR * e, moe_gate, moe_up, moe_down, D * e, DFF * e)
                    nxt = (e + 1) % NE
                    load_gate_up(u + 3, NPAIR * e + NPAIR - 1, moe_gate, moe_up, D * nxt, 0)
                    load_gate_up(u + 4, NPAIR * e + NPAIR - 1, moe_gate, moe_up, D * nxt, P)

            load_gate_up(MOE_U0, 0, moe_gate, moe_up, 0, 0)
            load_gate_up(MOE_U0 + 1, 0, moe_gate, moe_up, 0, P)
            expert_loads(MOE_U0)
            sp.wait_ge(sem("flag_ready"), 1)
            with sp.If(sp.value_load(flag[0:1, 0:1], min_val=0, max_val=1)):
                expert_loads(END_U)
            sp.wait_ge(sem("out_ready"), 1)
            sp.dma_start(out.rearrange("(n p) d -> p n d", p=P), xtok[:]).then_inc(sem("out_stored"), 16)
            sp.wait_ge(sem("out_stored"), 16)

        @block.tensor
        def _(pe):
            def mm3(out_ap, lhs, rhs, start, stop):
                nc.tensor.matmul(out_ap, lhs[0], rhs[1], start=start, stop=False)
                nc.tensor.matmul(out_ap, lhs[1], rhs[0], start=False, stop=False)
                return nc.tensor.matmul(out_ap, lhs[0], rhs[0], start=False, stop=stop)

            def unit_ready(u, i=0):
                pe.wait_ge(lo_pool, u + 1 + 3 * i)
                if u >= DVE_U0:
                    pe.wait_ge(lo_dve, u + 1 - DVE_U0 + 3 * i)

            def job_bank(j, i=0):
                if j >= 3:
                    pe.wait_ge(bank_free[j % 3], j // 3 + i)
                return tiles(W[j % 3][:])

            def proj_unit(u, j, i=0):
                unit_ready(u, i)
                bank = job_bank(j, i)
                wh, wl = (w[u % 3][:].rearrange("p (k c) -> p k c", k=KD) for w in (w_hi, w_lo))
                for m in range(2):
                    c = slice(m * P, (m + 1) * P)
                    for k in range(KD):
                        last = mm3(bank[:, m, :], (wh[:, k, c], wl[:, k, c]), (x_hi[:, k, :], x_lo[:, k, :]),
                                   k == 0, k == KD - 1)
                last.then_inc(w_used, 1)

            def branch_unit(l, b, u, j):
                unit_ready(u)
                pe.wait_ge(sem("o_hi_ready"), 3 * l + b + 1)
                pe.wait_ge(sem("o_lo_ready"), 3 * l + b + 1)
                wh, wl = (w[u % 3][:].rearrange("p (k c) -> p k c", k=BT) for w in (w_hi, w_lo))
                for h in range(2):
                    bank = job_bank(j + h)
                    for m in range(2):
                        c = slice((2 * h + m) * P, (2 * h + m + 1) * P)
                        for k in range(BT):
                            last = mm3(bank[:, m, :], (wh[:, k, c], wl[:, k, c]), (o_hi[:, k, :], o_lo[:, k, :]),
                                       k == 0, k == BT - 1)
                    last.then_inc(w_used if h else sem("half_done"), 1)

            def out_unit(l, q, u):
                unit_ready(u)
                if q == 0:
                    pe.wait_ge(sem("mhi_ready"), l + 1)
                    pe.wait_ge(sem("mlo_ready"), l + 1)
                wh, wl = (w[u % 3][:].rearrange("p (k c) -> p k c", k=2) for w in (w_hi, w_lo))
                for k in range(2):
                    kk = 2 * q + k
                    for t in range(NT):
                        tk = slice(t * P, (t + 1) * P)
                        for h in range(2):
                            c = slice(h * 512, (h + 1) * 512)
                            last = mm3(Y[2 * t + h][:], (x_hi[:, kk, tk], x_lo[:, kk, tk]), (wh[:, k, c], wl[:, k, c]),
                                       kk == 0, kk == KD - 1)
                return last

            def units(l, kind, a, b):
                u0, j0 = layer_unit(l) + UNIT0[kind], l * MIX_JOBS + JOB0[kind]
                if kind == "rkv" and a == 0 and l == 0:
                    pe.wait_ge(sem("x_hi_ready"), 1)
                    pe.wait_ge(sem("x_lo_ready"), 1)
                if kind == "out":
                    for q in range(a, b):
                        out_unit(l, q, u0 + q).then_inc(w_used, 1)
                elif kind.startswith("branch"):
                    for q in range(a, b):
                        branch_unit(l, int(kind[-1]), u0 + q, j0 + 2 * q)
                else:
                    q = a
                    if (b - a) // 3 >= 2 and j0 + a >= 3:
                        n = (b - a) // 3
                        with pe.Fori(0, n) as i:
                            for s in range(3):
                                proj_unit(u0 + a + s, j0 + a + s, i)
                        q = a + 3 * n
                    for q in range(q, b):
                        proj_unit(u0 + q, j0 + q)

            def transpose(out_ap, in_ap):
                return nc.tensor.transpose(out_ap, in_ap, ident)

            def lora(l, p):
                n = 2 * l + p
                pe.wait_ge(sem("w2_full"), 16 * (l + 1))
                pe.wait_ge(sem("lora_in_ready"), l + 1)
                if n:
                    pe.wait_ge(sem("pass_done"), n)
                for s, bank in ((0, Y[0]), (1, Y[1])):
                    for m in range(2):
                        c = slice((2 * p + m) * P, (2 * p + m + 1) * P)
                        last = nc.tensor.matmul(tiles(bank[:])[:, m, :], w2_s[:, s, c], rkvl[:, 12, :], start=True, stop=True)
                last.then_inc(sem("lora_done"), 1)

            def norm(l, p):
                pe.wait_ge(sem("ksq_ready"), 2 * l + p + 1)
                nc.tensor.matmul(Y[2][:], blk, td[:].rearrange("p m t -> p (m t)"), start=True, stop=True)\
                    .then_inc(sem("ss_done"), 1)

            def prep(l, p):
                n = 2 * l + p
                pe.wait_ge(sem("prep_ready"), n + 1)
                nc.tensor.matmul(Y[3][:], blk, td[:].rearrange("p m t -> p (m t)"), start=True, stop=True)\
                    .then_inc(sem("bonus_done"), 1)
                for c in range(NT):
                    for m in range(2):
                        transpose(tiles(E[:], 4)[:, 2 * c + m, :], rkvl[:, 8 + 2 * p + m, c * P:(c + 1) * P])
                for s, src in ((0, t6), (1, t3)):
                    for m in range(2):
                        last = transpose(tiles(Y[0][:], 4)[:, 2 * s + m, :], src[:, m, 0:P])
                last.then_inc(sem("tok_done"), 1)

            def scores(l, p):
                n = 2 * l + p
                pe.wait_ge(sem("tok_ready"), n + 1)
                pe.wait_ge(sem("bonus_ready"), n + 1)
                for u in range(8):
                    c, h = divmod(u, 4)
                    bank = Y[(1 + u) % 4]
                    if u >= 4:
                        pe.wait_ge(sem("score_ready"), 8 * n + u - 3)
                    rhs = ar[:, h, c].rearrange("p s t -> p (s t)")
                    nc.tensor.matmul(bank[:, 0:256], t6[:, h // 2, c * P:(c + 1) * P], rhs, start=True, stop=True)
                    nc.tensor.matmul(bank[:, 256:512], t3[:, h // 2, c * P:(c + 1) * P], rhs, start=True, stop=True)\
                        .then_inc(sem("score_done"), 1)
                untranspose(n, 0)

            def untranspose(n, v):
                for c in range(NT):
                    pe.wait_ge(sem("xt_ready"), 2 * LEVELS * n + 2 * v + c + 1)
                    for h in range(4):
                        last = transpose(tiles(Y[c][:], 4)[:, h, :], xt[:, 4 * c + h, :])
                    last.then_inc(sem("x_done"), 1)

            def level(l, p, v):
                n = 2 * l + p
                at = 2 * (LEVELS - 1) * n + 2 * (v - 1)
                for c in range(NT):
                    pe.wait_ge(sem("x_ready"), at + c + 1)
                    pe.wait_ge(sem("mt_ready"), at + c + 1)
                    for h in range(4):
                        last = nc.tensor.matmul(tiles(Y[c][:], 4)[:, h, :], mt[:, 4 * c + h, :], xm[:, 4 * c + h, :],
                                                start=True, stop=True)
                    last.then_inc(sem("mx_done"), 1)
                for c in range(NT):
                    pe.wait_ge(sem("mx_ready"), at + c + 1)
                    for h in range(4):
                        last = nc.tensor.matmul(tiles(Y[2 + c][:], 4)[:, h, :], mt[:, 4 * c + h, :], xt[:, 4 * c + h, :],
                                                start=True, stop=True)
                    last.then_inc(sem("dxt_done"), 1)
                if v < LEVELS - 1:
                    untranspose(n, v)

            def chain(l, p):
                n = 2 * l + p
                heads = [(h, h // 2, slice(h * HD, (h + 1) * HD), slice((h % 2) * HD, (h % 2 + 1) * HD)) for h in range(4)]
                pe.wait_ge(sem("xt_ready"), 2 * LEVELS * (n + 1))
                for c in range(NT):
                    if c:
                        pe.wait_ge(sem("s_ready"), n + 1)
                    for h, m, hc, half in heads:
                        last = nc.tensor.matmul(Y[0][:, hc], sc[:, 4 * c + h, 2, :], vtok[:, c, hc], start=True, stop=c == 0)
                        if c:
                            last = nc.tensor.matmul(Y[0][:, hc], ar[:, h, 1, 0, :], s_s[:, m, half], start=False, stop=True)
                    last.then_inc(sem("g_done"), 1)
                    pe.wait_ge(sem("g_ready"), 2 * n + c + 1)
                    for h, m, hc, half in heads:
                        last = nc.tensor.matmul(Y[1][:, hc], xt[:, 4 * c + h, :], g_s[:, h, :], start=True, stop=True)
                    last.then_inc(sem("u_done"), 1)
                    pe.wait_ge(sem("u_ready"), 2 * n + c + 1)
                    if c == 0:
                        for m in range(2):
                            mc = slice(m * P, (m + 1) * P)
                            nc.tensor.matmul(Y[3][:, mc], bktok[:, 0, mc], u_s[:, 2 * m:2 * m + 2, :].rearrange("p a b -> p (a b)"),
                                             start=True, stop=False)
                            last = nc.tensor.matmul(Y[3][:, mc], bktok[:, 1, mc], vtok[:, 0, mc], start=False, stop=True)
                        last.then_inc(sem("s_done"), 1)
                    for h, m, hc, half in heads:
                        o = tiles(E[:])[half, m, c * P:(c + 1) * P]
                        nc.tensor.matmul(o, vtok[:, c, hc], sc[:, 4 * c + h, 3, :], start=True, stop=False)
                        if c:
                            nc.tensor.matmul(o, s_s[:, m, half], ar[:, h, 1, 1, :], start=False, stop=False)
                        last = nc.tensor.matmul(o, u_s[:, h, :], sc[:, 4 * c + h, 1, :], start=False, stop=True)
                    last.then_inc(sem("y_done"), 1)

            def finish(l, p):
                n = 2 * l + p
                pe.wait_ge(sem("yrow_ready"), n + 1)
                nc.tensor.matmul(Y[0][:], blk, t1[:].rearrange("p m t -> p (m t)"), start=True, stop=True)\
                    .then_inc(sem("mean_done"), 1)
                pe.wait_ge(sem("gw2_full"), 16 * (l + 1))
                for m in range(2):
                    last = nc.tensor.matmul(tiles(Y[2][:])[:, m, :], gw2_s[:, (2 * p + m) * P:(2 * p + m + 1) * P],
                                            rkvl[:, 13, :], start=True, stop=True)
                last.then_inc(sem("gatemul_done"), 1)
                pe.wait_ge(sem("ysq_ready"), n + 1)
                nc.tensor.matmul(Y[1][:], blk, t2[:].rearrange("p m t -> p (m t)"), start=True, stop=True)\
                    .then_inc(sem("var_done"), 1)

            def attention(l):
                wait_jobs(pe, l * MIX_JOBS + JOB0["gate1"])
                pe.wait_ge(sem("pass_done"), 2 * l + 2)
                for s in range(4):
                    nc.tensor.matmul(Y[s][:], rot, share[:, 2 * s:2 * s + 2, :].rearrange("p m t -> p (m t)"),
                                     start=True, stop=True).then_inc(sem("rot_done"), 1)
                pe.wait_ge(sem("rope_ready"), l + 1)
                for c in range(NT):
                    for m in range(BT):
                        last = transpose(tiles(Y[c][:], 4)[:, m, :], share[:, 8 + m, c * P:(c + 1) * P])
                last.then_inc(sem("vt_done"), 1)
                for h in range(8):
                    bank = tiles(Y[(2 + h) % 4][:], 4)
                    if h == 2:
                        pe.wait_ge(sem("vatt_ready"), l + 1)
                    if h >= 4:
                        pe.wait_ge(sem("att_sc_ready"), 8 * l + h - 3)
                    nc.tensor.matmul(bank[:, 0, :], qp[:, h, 0:P], share[:, 4 + h // 2, 0:P], start=True, stop=True)
                    nc.tensor.matmul(bank[:, 1:3, :].rearrange("p a b -> p (a b)"), qp[:, h, P:T], share[:, 4 + h // 2, :],
                                     start=True, stop=True).then_inc(sem("att_sc_done"), 1)
                pe.wait_ge(sem("prob_ready"), l + 1)
                for h in range(8):
                    if h >= 3:
                        pe.wait_ge(sem("pt_ready"), 8 * l + h - 2)
                    for s in range(3):
                        last = transpose(tiles(Y[h % 3][:], 4)[:, s, :], pr[:, h, s, :])
                    last.then_inc(sem("pt_done"), 1)
                for h in range(8):
                    pe.wait_ge(sem("pt_ready"), 8 * l + h + 1)
                    o = tiles((E if h < 4 else Y[3])[:])[(h % 2) * HD:(h % 2 + 1) * HD, (h // 2) % 2, :]
                    hc = slice(h * HD, (h + 1) * HD)
                    nc.tensor.matmul(o, vatt[:, 0, hc], pr[:, h, 0:2, :].rearrange("p a b -> p (a b)"), start=True, stop=False)
                    last = nc.tensor.matmul(o[:, P:T], vatt[:, 1, hc], pr[:, h, 2, :], start=False, stop=True)
                last.then_inc(sem("att_done"), 1)

            def norm_transposes(m):
                pe.wait_ge(sem("xn_ready"), m + 1)
                for k in range(KD):
                    for t in range(NT):
                        last = transpose(tiles(Y[k // 2][:])[:, k % 2, t * P:(t + 1) * P], xtok[:, t, k * P:(k + 1) * P])
                    if k % 2:
                        last.then_inc(sem("xnt_done"), 1)

            def ffn(u, i, g, nt, x_ready):
                def gate_up(u, i, f, par_f):
                    unit_ready(u, i)
                    if not isinstance(f, int) or f >= 2:
                        pe.wait_ge(sem("hid_ready"), f - 1)
                    bank = tiles(W[par_f][:])
                    wh, wl = (w[u % 3][:].rearrange("p (k c) -> p k c", k=KD) for w in (w_hi, w_lo))
                    for t in range(nt):
                        tk = slice(t * P, (t + 1) * P)
                        for k in range(KD):
                            last = mm3(bank[:, t, :], (x_hi[:, k, tk], x_lo[:, k, tk]), (wh[:, k, :], wl[:, k, :]),
                                       k == 0, k == KD - 1)
                    last.then_inc(w_used, 1)

                def hid_transposes(g):
                    pe.wait_ge(sem("hid_ready"), 2 * g + 2)
                    for s in range(2):
                        for t in range(nt):
                            last = transpose(tiles(W[2][:], 4)[:, 2 * s + t, :], hid[:, s, t, :])
                    last.then_inc(sem("ht_done"), 1)

                def down(u, i, g, first, final):
                    unit_ready(u, i)
                    pe.wait_ge(sem("hlo_ready"), g + 1)
                    wh, wl = (w[u % 3][:].rearrange("p (k c) -> p k c", k=2) for w in (w_hi, w_lo))
                    for s in range(2):
                        for t in range(nt):
                            tk = slice(t * P, (t + 1) * P)
                            for h in range(2):
                                c = slice(h * 512, (h + 1) * 512)
                                last = mm3(Y[2 * t + h][:], (o_hi[:, s, tk], o_lo[:, s, tk]), (wh[:, s, c], wl[:, s, c]),
                                           first and s == 0, final and s == 1)
                    last.then_inc(w_used, 1)

                x_ready()
                gate_up(u, i, 2 * g, 0)
                gate_up(u + 1, i, 2 * g + 1, 1)
                gate_up(u + 2, i, 2 * g + 2, 0)
                hid_transposes(g)
                gate_up(u + 3, i, 2 * g + 3, 1)
                down(u + 4, i, g, True, False)
                with pe.Fori(2, NPAIR) as j:
                    gate_up(u + 2, i + j - 1, 2 * (g + j), 0)
                    hid_transposes(g + j - 1)
                    gate_up(u + 3, i + j - 1, 2 * (g + j) + 1, 1)
                    down(u + 4, i + j - 1, g + j - 1, False, False)
                hid_transposes(g + NPAIR - 1)
                down(u + 2, i + NPAIR - 1, g + NPAIR - 1, False, True)

            def experts(u, g, q):
                with pe.Fori(0, NE) as e:
                    pe.wait_ge(sem("sel_ready"), q + e + 1)
                    for t in range(NT):
                        transpose(E[:, t * P:(t + 1) * P], selg[:, t, :])
                    for k in range(KD):
                        for t in range(NT):
                            last = nc.tensor.matmul(tiles(Y[2 + k // 4][:], 4)[:, k % 4, :], xtok[:, t, k * P:(k + 1) * P],
                                                    sel[:, t, :], start=t == 0, stop=t == NT - 1)
                    last.then_inc(sem("rows_done"), 1)
                    ffn(u, NPAIR * e, g + NPAIR * e, 1, lambda: pe.wait_ge(sem("rows_ready"), q + e + 1))
                    pe.wait_ge(sem("yrows_ready"), q + e + 1)
                    for t, banks in ((0, (Y[2], Y[3])), (1, (E, W[2]))):
                        for h in range(2):
                            last = nc.tensor.matmul(banks[h][:], selgt[:, t * P:(t + 1) * P], y_sb[:, h * 512:(h + 1) * 512],
                                                    start=True, stop=True)
                        last.then_inc(sem("comb_done"), 1)

            pe.wait_ge(sem("cst_full"), 16)
            handlers = {"units": units, "lora": lora, "norm": norm, "prep": prep, "scores": scores, "level": level,
                        "chain": chain, "finish": finish, "attention": attention}
            for l in range(L):
                for name, *args in TIMELINE:
                    if name in handlers:
                        handlers[name](l, *args)
                norm_transposes(2 * l)
                if l == 0:
                    ffn(layer_unit(0) + MIX_UNITS, 0, 0, NT, lambda: pe.wait_ge(sem("x_lo_ready"), 5))
                    norm_transposes(1)
                    pe.wait_ge(sem("x_lo_ready"), 9)
            pe.wait_ge(sem("cmo_full"), 32)
            pe.wait_ge(sem("x_lo_ready"), 13)
            for t in range(NT):
                for k in range(KD):
                    last = nc.tensor.matmul(E[:, t * NE:(t + 1) * NE], xf[:, k, t * P:(t + 1) * P], rt_s[:, k, :],
                                            start=k == 0, stop=k == KD - 1)
            last.then_inc(sem("logits_done"), 1)
            pe.wait_ge(sem("mask_ready"), 1)
            ones, m0, m1 = cmo[:, E_ONE:E_ONE + P], route[:, 0, 40:48], route[:, 1, 40:48]
            nc.tensor.matmul(E[:, 32:40], strict, m0, start=True, stop=True)
            nc.tensor.matmul(E[:, 40:48], ones, m0, start=True, stop=False)
            nc.tensor.matmul(E[:, 40:48], strict, m1, start=False, stop=True)
            nc.tensor.matmul(E[:, 48:56], ones, m0, start=True, stop=False)
            nc.tensor.matmul(E[:, 48:56], ones, m1, start=False, stop=True).then_inc(sem("place_done"), 1)
            experts(MOE_U0, NPAIR, 0)
            with pe.If(pe.value_load(flag[0:1, 0:1], min_val=0, max_val=1)):
                experts(END_U, NPAIR * (NE + 1), NE)

        @block.scalar
        def _(act):
            link = chained(act, "act_chain")
            A = nc.scalar.activation

            def split_hi(u, i=0):
                act.wait_ge(raw_full[u % 3], UD * (u // 3 + 1 + i))
                if u >= 3:
                    act.wait_ge(w_used, u - 2 + 3 * i)
                A(w_hi[u % 3][:], raw[u % 3][:], ACT.Copy).then_inc(hi_done, 1)

            def out_of_bank(kind, q, u, j, i=0):
                act.wait_ge(w_used, u + 1 + 3 * i)
                base, func = {"r": (rkvl, ACT.Copy), "c": (share, ACT.Copy), "q": (share, ACT.Copy),
                              "g": (sgate, ACT.Sigmoid)}[kind[0]]
                dst = base[:, bass.ds(2 * q + 6 * i, 2), :] if not isinstance(i, int) else base[:, 2 * q:2 * q + 2, :]
                A(dst, tiles(W[j % 3][:]), func).then_inc(bank_free[j % 3], 1)

            def units(l, kind, a, b):
                u0, j0 = layer_unit(l) + UNIT0[kind], l * MIX_JOBS + JOB0[kind]
                if kind == "qkv":
                    act.wait_ge(sem("o_hi_ready"), 3 * l + 1)
                    act.wait_ge(sem("o_lo_ready"), 3 * l + 1)
                if kind in ("gate1", "gate2"):
                    wait_jobs(act, l * MIX_JOBS + JOB0[f"branch{int(kind[-1]) - 1}"] + 4)
                if kind == "out" or kind.startswith("branch"):
                    for q in range(a, b):
                        split_hi(u0 + q + 2)
                    return
                q = a
                if (b - a) // 3 >= 2:
                    n = (b - a) // 3
                    with act.Fori(0, n) as i:
                        for s in range(3):
                            split_hi(u0 + a + s + 2, i)
                            out_of_bank(kind, a + s, u0 + a + s, j0 + a + s, i)
                    q = a + 3 * n
                for q in range(q, b):
                    split_hi(u0 + q + 2)
                    out_of_bank(kind, q, u0 + q, j0 + q)

            def shift(l):
                act.wait_ge(sem("shift_ready"), l + 1)
                link(A(rkvl[0:64, 12, :], rkvl[0:64, 12, :], ACT.Tanh))
                A(rkvl[:, 13, :], rkvl[:, 13, :], ACT.Sigmoid).then_inc(sem("lora_in_ready"), 1)

            def lora(l, p):
                n = 2 * l + p
                act.wait_ge(sem("lora_done"), n + 1)
                if n:
                    act.wait_ge(sem("pass_done"), n)
                for m in range(2):
                    A(t1[:, m, :], tiles(Y[0][:])[:, m, :], ACT.Sigmoid, bias=par_col(l, "w0", 2 * p + m))
                for m in range(2):
                    last = A(t4[:, m, :], tiles(Y[1][:])[:, m, :], ACT.Sigmoid, bias=par_col(l, "a0", 2 * p + m))
                last.then_inc(sem("rates_ready"), 1)
                act.wait_ge(sem("decay_ready"), n + 1)
                A(t1[:], t1[:], ACT.Exp, scale=-KAPPA)
                A(t3[:], t2[:], ACT.Exp, scale=KAPPA).then_inc(sem("act_t3"), 1)
                act.wait_ge(sem("act_t3"), n + 1)
                A(t2[:], t2[:], ACT.Exp, scale=-KAPPA)
                A(small[:, 4:6], small[:, 4:6], ACT.Exp, scale=-KAPPA).then_inc(sem("exp_ready"), 1)

            def norm(l, p):
                n = 2 * l + p
                act.wait_ge(sem("ss_done"), n + 1)
                A(td[:].rearrange("p m t -> p (m t)"), Y[2][:], ACT.Sqrt).then_inc(sem("knorm_ready"), 1)

            def prep(l, p):
                n = 2 * l + p
                act.wait_ge(sem("tok_done"), n + 1)
                A(vtok[:].rearrange("p c v -> p (c v)"), E[:], ACT.Copy)
                A(bktok[:].rearrange("p c v -> p (c v)"), Y[0][:], ACT.Copy).then_inc(sem("tok_ready"), 1)

            def copy_x(n, v):
                at = 2 * (LEVELS - 1) * n + 2 * v
                for c in range(NT):
                    act.wait_ge(sem("x_done"), at + c + 1)
                    A(xm[:, 4 * c:4 * c + 4, :], tiles(Y[c][:], 4), ACT.Copy).then_inc(sem("x_ready"), 1)

            def scores(l, p):
                copy_x(2 * l + p, 0)

            def level(l, p, v):
                n = 2 * l + p
                at = 2 * (LEVELS - 1) * n + 2 * (v - 1)
                for c in range(NT):
                    act.wait_ge(sem("mx_done"), at + c + 1)
                    A(mt[:, 4 * c:4 * c + 4, :], tiles(Y[c][:], 4), ACT.Copy).then_inc(sem("mx_ready"), 1)
                if v < LEVELS - 1:
                    copy_x(n, v)

            def finish(l, p):
                n = 2 * l + p
                act.wait_ge(sem("var_done"), n + 1)
                A(t2[:].rearrange("p m t -> p (m t)"), Y[1][:], ACT.Sqrt, bias=small[:, 8:9], scale=1.0 / HD)\
                    .then_inc(sem("gn_sd_ready"), 1)
                if p == 1:
                    act.wait_ge(sem("pass_done"), n + 1)
                    act.dma_start(cat[:], const_att).then_inc(sem("cat_full"), 16)
                    if l == 0:
                        act.dma_start(w2_s[:], w2[1]).then_inc(sem("w2_full"), 16)
                        act.dma_start(gw2_s[:], gate_w2[1]).then_inc(sem("gw2_full"), 16)

            def attention(l):
                act.wait_ge(sem("vt_done"), l + 1)
                for c in range(NT):
                    last = A(vatt[:, c, :], Y[c][:], ACT.Copy)
                last.then_inc(sem("vatt_ready"), 1)
                act.wait_ge(sem("max_ready"), l + 1)
                for h in range(8):
                    A(pr[:, h, 0, :], pr[:, h, 0, :], ACT.Exp, bias=small[:, 16 + 2 * h:17 + 2 * h],
                      accum_out=small[:, 32 + 2 * h:33 + 2 * h])
                    last = A(pr[:, h, 1:3, :], pr[:, h, 1:3, :], ACT.Exp, bias=small[:, 17 + 2 * h:18 + 2 * h],
                             accum_out=small[:, 33 + 2 * h:34 + 2 * h])
                last.then_inc(sem("e_ready"), 1)
                for h in range(8):
                    act.wait_ge(sem("pt_done"), 8 * l + h + 1)
                    A(pr[:, h, :, :].rearrange("p s q -> p (s q)"), Y[h % 3][:, 0:3 * P], ACT.Copy).then_inc(sem("pt_ready"), 1)
                act.wait_ge(sem("att_done"), l + 1)
                act.wait_ge(w_used, layer_unit(l) + UNIT0["branch0"] + 2)
                A(o_hi[:, 0:2, :], tiles(E[:]), ACT.Copy)
                A(o_hi[:, 2:4, :], tiles(Y[3][:]), ACT.Copy).then_inc(sem("o_hi_ready"), 1)
                act.wait_ge(sem("o_lo_ready"), 3 * l + 2)
                act.dma_start(gb[:], ln_gb[2 * l]).then_inc(sem("gb_full"), 16)

            def osplit(l, b):
                src = share if b == 0 else rkvl
                if b == 0:
                    act.wait_ge(sem("conv_ready"), l + 1)
                else:
                    act.wait_ge(sem("pass_done"), 2 * l + 2)
                act.wait_ge(w_used, layer_unit(l) + (UNIT0["branch1"] + 2 if b else 0))
                A(o_hi[:], src[:, 0:BT, :], ACT.Copy).then_inc(sem("o_hi_ready"), 1)

            def msplit(l):
                act.wait_ge(sem("gated"), 8 * (l + 1))
                A(x_hi[:], merged[:], ACT.Copy).then_inc(sem("mhi_ready"), 1)
                act.wait_ge(sem("mlo_ready"), l + 1)
                act.wait_ge(sem("mhi_ready"), l + 1)
                if l:
                    act.wait_ge(sem("spilled"), 16)
                act.dma_start(xtok[:], (spill if l else x).rearrange("(n p) d -> p n d", p=P)).then_inc(sem("xres_full"), 16)
                if l:
                    act.dma_start(cmo[:], const_moe).then_inc(sem("cmo_full"), 16)
                    act.dma_start(rt_s[:], router).then_inc(sem("cmo_full"), 16)

            def ln_scale(m):
                act.wait_ge(sem("ln_var_ready"), m + 1)
                A(small[:, 50:52], tiles(small[:, 80:84])[:, :, 1], ACT.Sqrt, bias=small[:, 9:10]).then_inc(sem("ln_sd_ready"), 1)

            def ln_split(m):
                for k in range(4):
                    act.wait_ge(sem("xf_ready"), 4 * m + k + 1)
                    A(x_hi[:, 2 * k:2 * k + 2, :], xf[:, 2 * k:2 * k + 2, :], ACT.Copy).then_inc(sem("x_hi_ready"), 1)

            def ffn(u, i, g, nt):
                def silu(f, par_f, used):
                    act.wait_ge(w_used, used)
                    if not isinstance(f, int) or f >= 2:
                        act.wait_ge(sem("hid_ready"), f - 1)
                    A(sil[:, par_f, 0:nt, :], tiles(W[par_f][:])[:, 0:nt, 0:P], ACT.Silu).then_inc(sem("silu_ready"), 1)

                def hid_hi(g, used):
                    act.wait_ge(sem("ht_done"), g + 1)
                    act.wait_ge(w_used, used)
                    A(o_hi[:, 0:2, 0:nt * P], tiles(W[2][:])[:, :, 0:nt * P], ACT.Copy).then_inc(sem("hhi_ready"), 1)

                split_hi(u + 2, i)
                silu(2 * g, 0, u + 1 + 3 * i)
                split_hi(u + 3, i)
                silu(2 * g + 1, 1, u + 2 + 3 * i)
                with act.Fori(1, NPAIR) as j:
                    v, w = u + 3 * (i + j - 1), i + j - 1
                    split_hi(u + 4, w)
                    silu(2 * (g + j), 0, v + 3)
                    hid_hi(g + j - 1, v + 2)
                    split_hi(u + 5, w)
                    silu(2 * (g + j) + 1, 1, v + 4)
                    split_hi(u + 6, w)
                v = u + 3 * (i + NPAIR - 1)
                split_hi(u + 4, i + NPAIR - 1)
                hid_hi(g + NPAIR - 1, v + 2)

            def experts(u, g, q):
                with act.Fori(0, NE) as e:
                    act.wait_ge(sem("rows_done"), q + e + 1)
                    A(selgt[:], E[:, 0:T], ACT.Copy)
                    for s in range(2):
                        last = A(x_hi[:, 4 * s:4 * s + 4, 0:P], tiles(Y[2 + s][:], 4), ACT.Copy)
                    last.then_inc(sem("rows_hi"), 1)
                    ffn(u, NPAIR * e, g + NPAIR * e, 1)
                    act.wait_ge(w_used, u + FFN_UNITS * (e + 1))
                    for h in range(2):
                        last = A(y_sb[:, h * 512:(h + 1) * 512], Y[h][:], ACT.Copy)
                    last.then_inc(sem("yrows_ready"), 1)

            act.dma_start(w2_s[:], w2[0]).then_inc(sem("w2_full"), 16)
            act.dma_start(gw2_s[:], gate_w2[0]).then_inc(sem("gw2_full"), 16)
            act.wait_ge(sem("eps_ready"), 1)
            act.wait_ge(sem("prm_full"), 16)
            act.wait_ge(sem("x_full"), 16)
            A(x_hi[:], xf[:], ACT.Copy).then_inc(sem("x_hi_ready"), 1)
            split_hi(0)
            split_hi(1)
            handlers = {"units": units, "shift": shift, "lora": lora, "norm": norm, "prep": prep, "scores": scores,
                        "level": level, "finish": finish, "attention": attention, "osplit": osplit, "msplit": msplit}
            for l in range(L):
                for name, *args in TIMELINE:
                    if name in handlers:
                        handlers[name](l, *args)
                ln_scale(2 * l)
                ln_split(2 * l)
                if l == 0:
                    act.wait_ge(sem("xtok_ready"), 1)
                    act.dma_start(gb[:], ln_gb[1]).then_inc(sem("gb_full"), 16)
                    ffn(layer_unit(0) + MIX_UNITS, 0, 0, NT)
                    ln_scale(1)
                    ln_split(1)
                    act.wait_ge(sem("xtok_ready"), 2)
                    act.dma_start(spill.rearrange("(n p) d -> p n d", p=P), xtok[:]).then_inc(sem("spilled"), 16)
            act.wait_ge(sem("logits_done"), 1)
            act.wait_ge(sem("top_ready"), 1)
            for t in range(NT):
                last = A(route[:, t, 16:17], route[:, t, 17:18], ACT.Exp)
            last.then_inc(sem("gexp_ready"), 1)
            act.wait_ge(sem("xtok_ready"), 3)
            act.dma_start(gb[:], ln_gb[3]).then_inc(sem("gb_full"), 16)
            experts(MOE_U0, NPAIR, 0)
            act.wait_ge(sem("flag_ready"), 1)
            with act.If(act.value_load(flag[0:1, 0:1], min_val=0, max_val=1)):
                experts(END_U, NPAIR * (NE + 1), NE)
            ln_scale(3)

        @block.gpsimd
        def _(pool):
            link = chained(pool, "pool_chain")

            def split_lo(u, i=0):
                pool.wait_ge(hi_done, u + 1 + 3 * i)
                c = slice(UN - POOL_MOE if u >= DVE_U0 else 0, UN)
                nc.gpsimd.tensor_tensor(w_lo[u % 3][:, c], raw[u % 3][:, c], w_hi[u % 3][:, c].bitcast(F32), ALU.subtract)\
                    .then_inc(lo_pool, 1)

            def units(l, kind, a, b):
                u0, q = layer_unit(l) + UNIT0[kind], a
                if (b - a) // 3 >= 2:
                    with pool.Fori(0, (b - a) // 3) as i:
                        for s in range(3):
                            split_lo(u0 + a + s + 2, i)
                    q = a + (b - a) // 3 * 3
                for q in range(q, b):
                    split_lo(u0 + q + 2)

            def attention(l):
                pool.wait_ge(sem("pass_done"), 2 * l + 2)
                nc.gpsimd.memset(qp[:], 0.0).then_inc(sem("qp_zero"), 1)

            def scale_xtok(m):
                pool.wait_ge(sem("gb_full"), 16 * (m + 1))
                pool.wait_ge(sem("xnt_done"), 4 * (m + 1))
                for s, op in ((0, ALU.mult), (1, ALU.add)):
                    for t in range(NT):
                        last = nc.gpsimd.tensor_tensor(xtok[:, t, :], xtok[:, t, :], gb[:, s, :], op)
                        if s == 0 or t == 0:
                            link(last)
                last.then_inc(sem("xtok_ready"), 1)

            def ffn(u, i):
                split_lo(u + 2, i)
                split_lo(u + 3, i)
                with pool.Fori(1, NPAIR) as j:
                    for s in range(3):
                        split_lo(u + 4 + s, i + j - 1)
                split_lo(u + 4, i + NPAIR - 1)

            def experts(u):
                with pool.Fori(0, NE) as e:
                    ffn(u, NPAIR * e)

            nc.gpsimd.memset(small[:], 0.0).then_inc(sem("pool_zero"), 1)
            pool.wait_ge(sem("pool_zero"), 1)
            link(nc.gpsimd.memset(small[:, 8:9], GN_EPS))
            nc.gpsimd.memset(small[:, 9:10], LN_EPS).then_inc(sem("eps_ready"), 1)
            nc.gpsimd.memset(ar[:], 0.0).then_inc(sem("ar_zero"), 1)
            split_lo(0)
            split_lo(1)
            for l in range(L):
                for name, *args in TIMELINE:
                    if name == "units":
                        units(l, *args)
                    elif name == "attention":
                        attention(l)
                scale_xtok(2 * l)
                if l == 0:
                    ffn(layer_unit(0) + MIX_UNITS, 0)
                    scale_xtok(1)
            experts(MOE_U0)
            pool.wait_ge(sem("flag_ready"), 1)
            with pool.If(pool.value_load(flag[0:1, 0:1], min_val=0, max_val=1)):
                experts(END_U)

        @block.vector
        def _(dve):
            link = chained(dve, "dve_chain")
            V = nc.vector

            def mark(ins, name, value):
                ins.then_inc(sem(name), 1)
                dve.wait_ge(sem(name), value)

            def split_lo(u, i=0):
                dve.wait_ge(hi_done, u + 1 + 3 * i)
                c = slice(0, UN - POOL_MOE)
                V.tensor_tensor(w_lo[u % 3][:, c], raw[u % 3][:, c], w_hi[u % 3][:, c].bitcast(F32), ALU.subtract)\
                    .then_inc(lo_dve, 1)

            def units(l, kind, a, b):
                u0, j0 = layer_unit(l) + UNIT0[kind], l * MIX_JOBS + JOB0[kind]
                for q in range(a, b):
                    if u0 + q + 2 >= DVE_U0:
                        split_lo(u0 + q + 2)
                    if kind.startswith("branch"):
                        gate_unit(l, int(kind[-1]), q, u0 + q, j0 + 2 * q)

            def gate_unit(l, b, q, u, j):
                if q == 0:
                    wait_jobs(dve, l * MIX_JOBS + JOB0[f"branch{b}"])
                    if b == 0 and l:
                        dve.wait_ge(sem("spilled"), 16)
                for h in range(2):
                    if h == 0:
                        dve.wait_ge(sem("half_done"), 2 * (3 * l + b) + q + 1)
                    else:
                        dve.wait_ge(w_used, u + 1)
                    ft = slice(4 * q + 2 * h, 4 * q + 2 * h + 2)
                    free, value = bank_free[(j + h) % 3], (j + h) // 3 + 1
                    dst = td[:] if b else merged[:, ft, :]
                    V.tensor_tensor(dst, tiles(W[(j + h) % 3][:]), sgate[:, ft, :], ALU.mult).then_inc(free, 1)
                    if b:
                        dve.wait_ge(free, value)
                        mark(V.tensor_tensor(merged[:, ft, :], merged[:, ft, :], td[:], ALU.add),
                             "gated", 8 * l + 4 * (b - 1) + 2 * q + h + 1)

            def shift(l):
                wait_jobs(dve, l * MIX_JOBS + JOB0["conv"])
                link(V.tensor_tensor(dsh[:, :, 1:T], rkvl[:, :, 0:T - 1], rkvl[:, :, 1:T], ALU.subtract))
                link(V.tensor_scalar(dsh[:, :, 0:1], rkvl[:, :, 0:1], -1.0, None, ALU.mult))
                for i in range(14):
                    last = V.scalar_tensor_tensor(rkvl[:, i, :], dsh[:, i, :], par_col(l, "mu", i), rkvl[:, i, :],
                                                  ALU.mult, ALU.add)
                mark(last, "shift_ready", l + 1)

            def conv(l):
                wait_jobs(dve, l * MIX_JOBS + JOB0["gate0"])
                ch, cb, cc = share[:, 0:4, :], share[:, 4:8, :], share[:, 8:12, :]
                link(V.tensor_tensor(cc, cc, ch, ALU.mult))
                for i in range(BT):
                    V.tensor_scalar(ch[:, i, :], cc[:, i, :], par_col(l, "conv2", i), None, ALU.mult)
                for tap, back in (("conv1", 1), ("conv0", 2)):
                    link(V.engine_nop())
                    for i in range(BT):
                        V.scalar_tensor_tensor(ch[:, i, back:T], cc[:, i, 0:T - back], par_col(l, tap, i), ch[:, i, back:T],
                                               ALU.mult, ALU.add)
                link(V.engine_nop())
                mark(V.tensor_tensor(ch, ch, cb, ALU.mult), "conv_ready", l + 1)

            def lora(l, p):
                n = 2 * l + p
                dve.wait_ge(sem("rates_ready"), n + 1)
                for m in range(2):
                    for c in range(NT):
                        tc = slice(c * P, (c + 1) * P)
                        last = V.tensor_tensor_scan(t2[:, m, tc], t1[:, m, tc], t1[:, m, tc], 0.0, ALU.add, ALU.bypass)
                link(last)
                t2c = t2[:].rearrange("p m (c t) -> p (m c) t", c=NT)
                link(V.tensor_scalar(small[:, 0:4], t2c[:, :, P - 1], 0.5, None, ALU.mult))
                half = small[:, 0:4]
                V.tensor_tensor(small[:, 4:6], tiles(half)[:, :, 0], tiles(half)[:, :, 1], ALU.add)
                link(V.tensor_tensor(t2c, t2c, half.unsqueeze(2).to_broadcast([P, 4, P]), ALU.subtract))
                mark(V.tensor_tensor(t1[:], t2[:], t1[:], ALU.subtract), "decay_ready", n + 1)

            def norm(l, p):
                n = 2 * l + p
                for m in range(2):
                    last = V.tensor_scalar(t6[:, m, :], rkvl[:, 4 + 2 * p + m, :], par_col(l, "k_k", 2 * p + m), None, ALU.mult)
                link(last)
                mark(V.tensor_tensor(td[:], t6[:], t6[:], ALU.mult), "ksq_ready", n + 1)
                dve.wait_ge(sem("knorm_ready"), n + 1)
                link(V.tensor_scalar(td[:], td[:], 1e-12, None, ALU.max))
                link(V.reciprocal(td[:], td[:]))
                link(V.scalar_tensor_tensor(t6[:], t6[:], -1.0, td[:], ALU.mult, ALU.mult))

            def prep(l, p):
                n = 2 * l + p
                r, k, v = (rkvl[:, 4 * s + 2 * p:4 * s + 2 * p + 2, :] for s in range(3))
                dve.wait_ge(sem("exp_ready"), n + 1)
                if n == 0:
                    dve.wait_ge(sem("ar_zero"), 1)
                arv = ar[:].rearrange("p (m h) c s t -> p m h c s t", h=2)
                for s, a0, a1 in ((0, t6[:], t1[:]), (1, r, t2[:])):
                    for h in range(2):
                        rows = slice(h * HD, (h + 1) * HD)
                        V.tensor_tensor(arv[rows, :, h, :, s, :], a0[rows].rearrange("p m (c t) -> p m c t", c=NT),
                                        a1[rows].rearrange("p m (c t) -> p m c t", c=NT), ALU.mult)
                link(V.scalar_tensor_tensor(td[:], t6[:], -1.0, t4[:], ALU.mult, ALU.mult))
                link(V.tensor_tensor(t6[:], td[:], t3[:], ALU.mult))
                for m in range(2):
                    last = V.tensor_scalar(t4[:, m, :], t4[:, m, :], -1.0, par_col(l, "k_a", 2 * p + m), ALU.add, ALU.mult)
                link(last)
                link(V.scalar_tensor_tensor(k, t4[:], 1.0, k, ALU.add, ALU.mult))
                V.tensor_tensor(t3[:], k, t3[:], ALU.mult)
                for m in range(2):
                    last = V.scalar_tensor_tensor(td[:, m, :], r[:, m, :], par_col(l, "r_k", 2 * p + m), k[:, m, :],
                                                  ALU.mult, ALU.mult)
                mark(last, "prep_ready", n + 1)
                dve.wait_ge(sem("bonus_done"), n + 1)
                mark(V.tensor_tensor(t4[:], tiles(Y[3][:]), v, ALU.mult), "bonus_ready", n + 1)

            def mask_level(n, v, c):
                return V.tensor_tensor(mt[:, 4 * c:4 * c + 4, :], sc[:, 4 * c:4 * c + 4, 0, :], level_mask(v), ALU.mult)

            def scores(l, p):
                n = 2 * l + p
                si = cst[:, C_SI:C_SI + 2 * P].unsqueeze(1).to_broadcast([P, 2, 2 * P])
                for u in range(8):
                    dve.wait_ge(sem("score_done"), 8 * n + u + 1)
                    mark(V.tensor_tensor(sc[:, u].rearrange("p (b s) t -> p b (s t)", b=2), tiles(Y[(1 + u) % 4][:]), si, ALU.mult),
                         "score_ready", 8 * n + u + 1)
                for c in range(NT):
                    link(mask_level(n, 0, c))
                    mark(V.tensor_tensor(xt[:, 4 * c:4 * c + 4, :], mt[:, 4 * c:4 * c + 4, :],
                                         ident.unsqueeze(1).to_broadcast([P, 4, P]), ALU.add),
                         "xt_ready", 2 * LEVELS * n + c + 1)
                    mark(mask_level(n, 1, c), "mt_ready", 2 * (LEVELS - 1) * n + c + 1)

            def level(l, p, v):
                n = 2 * l + p
                for c in range(NT):
                    dve.wait_ge(sem("dxt_done"), 2 * (LEVELS - 1) * n + 2 * (v - 1) + c + 1)
                    mark(V.tensor_tensor(xt[:, 4 * c:4 * c + 4, :], xt[:, 4 * c:4 * c + 4, :], tiles(Y[2 + c][:], 4), ALU.add),
                         "xt_ready", 2 * LEVELS * n + 2 * v + c + 1)
                    if v < LEVELS - 1:
                        mark(mask_level(n, v + 1, c), "mt_ready", 2 * (LEVELS - 1) * n + 2 * v + c + 1)

            def chain(l, p):
                n = 2 * l + p
                for c in range(NT):
                    dve.wait_ge(sem("g_done"), 2 * n + c + 1)
                    mark(V.tensor_copy(g_s[:].rearrange("p a b -> p (a b)"), Y[0][:, 0:256]), "g_ready", 2 * n + c + 1)
                    dve.wait_ge(sem("u_done"), 2 * n + c + 1)
                    mark(V.tensor_copy(u_s[:].rearrange("p a b -> p (a b)"), Y[1][:, 0:256]), "u_ready", 2 * n + c + 1)
                    if c == 0:
                        dve.wait_ge(sem("s_done"), n + 1)
                        mark(V.tensor_tensor(s_s[:], tiles(Y[3][:, 0:256]), small[:, 4:6].unsqueeze(2).to_broadcast([P, 2, P]),
                                             ALU.mult), "s_ready", n + 1)

            def finish(l, p):
                n = 2 * l + p
                dve.wait_ge(sem("y_done"), 2 * n + 2)
                mark(V.tensor_copy(t1[:], tiles(E[:])), "yrow_ready", n + 1)
                dve.wait_ge(sem("mean_done"), n + 1)
                link(V.scalar_tensor_tensor(t1[:], tiles(Y[0][:]), -1.0 / HD, t1[:], ALU.mult, ALU.add))
                mark(V.tensor_tensor(t2[:], t1[:], t1[:], ALU.mult), "ysq_ready", n + 1)
                dve.wait_ge(sem("gn_sd_ready"), n + 1)
                link(V.reciprocal(t2[:], t2[:]))
                link(V.tensor_tensor(t1[:], t1[:], t2[:], ALU.mult))
                for m in range(2):
                    last = V.tensor_scalar(t1[:, m, :], t1[:, m, :], par_col(l, "gn_g", 2 * p + m),
                                           par_col(l, "gn_b", 2 * p + m), ALU.mult, ALU.add)
                link(last)
                link(V.tensor_tensor(t1[:], t1[:], t4[:], ALU.add))
                dve.wait_ge(sem("gatemul_done"), n + 1)
                mark(V.tensor_tensor(rkvl[:, 2 * p:2 * p + 2, :], t1[:], tiles(Y[2][:]), ALU.mult), "pass_done", n + 1)

            def attention(l):
                wait_jobs(dve, l * MIX_JOBS + JOB0["gate1"])
                dve.wait_ge(sem("cat_full"), 16 * (l + 1))
                dve.wait_ge(sem("qp_zero"), l + 1)
                cos, sin = (cat[:, a:a + T].unsqueeze(1).to_broadcast([P, 2, T]) for a in (A_COS, A_SIN))
                qpv = qp[:].rearrange("p (m h) t -> p m h t", h=2)
                for s in range(4):
                    src = share[:, 2 * s:2 * s + 2, :]
                    dve.wait_ge(sem("rot_done"), 4 * l + s + 1)
                    V.tensor_tensor(t1[:], tiles(Y[s][:]), sin, ALU.mult)
                    link(V.tensor_tensor(t2[:], src, cos, ALU.mult))
                    if s < 2:
                        for h in range(2):
                            rows = slice(h * HD, (h + 1) * HD)
                            last = V.tensor_tensor(qpv[rows, 2 * s:2 * s + 2, h, :], t1[rows], t2[rows], ALU.add)
                        link(last)
                    elif s == 2:
                        link(V.tensor_tensor(src, t1[:], t2[:], ALU.add))
                    else:
                        mark(V.tensor_tensor(src, t1[:], t2[:], ALU.add), "rope_ready", l + 1)
                mask = cat[:, A_MASK:A_MASK + 3 * P]
                for h in range(8):
                    dve.wait_ge(sem("att_sc_done"), 8 * l + h + 1)
                    mark(V.scalar_tensor_tensor(pr[:, h].rearrange("p s q -> p (s q)"), Y[(2 + h) % 4][:, 0:3 * P], HD ** -0.5,
                                                mask, ALU.mult, ALU.add), "att_sc_ready", 8 * l + h + 1)
                    V.reduce_max(small[:, 16 + 2 * h:17 + 2 * h], pr[:, h, 0, :], AX.X)
                    last = V.reduce_max(small[:, 17 + 2 * h:18 + 2 * h], pr[:, h, 1:3, :].rearrange("p s q -> p (s q)"), AX.X)
                link(last)
                mark(V.tensor_scalar(small[:, 16:32], small[:, 16:32], -1.0, None, ALU.mult), "max_ready", l + 1)
                dve.wait_ge(sem("e_ready"), l + 1)
                link(V.reciprocal(small[:, 32:48], small[:, 32:48]))
                inv = small[:, 32:48].rearrange("p (h q) -> p h q", q=2)
                V.tensor_tensor(pr[:, :, 0, :], pr[:, :, 0, :], inv[:, :, 0:1].to_broadcast([P, 8, P]), ALU.mult)
                late = pr[:, :, 1:3, :].rearrange("p h s q -> p h (s q)")
                mark(V.tensor_tensor(late, late, inv[:, :, 1:2].to_broadcast([P, 8, 2 * P]), ALU.mult), "prob_ready", l + 1)
                dve.wait_ge(sem("o_hi_ready"), 3 * l + 2)
                V.tensor_tensor(o_lo[:, 0:2, :], tiles(E[:]), o_hi[:, 0:2, :].bitcast(F32), ALU.subtract)
                V.tensor_tensor(o_lo[:, 2:4, :], tiles(Y[3][:]), o_hi[:, 2:4, :].bitcast(F32), ALU.subtract)\
                    .then_inc(sem("o_lo_ready"), 1)

            def osplit(l, b):
                dve.wait_ge(sem("o_hi_ready"), 3 * l + b + 1)
                V.tensor_tensor(o_lo[:], (rkvl if b else share)[:, 0:BT, :], o_hi[:].bitcast(F32), ALU.subtract)\
                    .then_inc(sem("o_lo_ready"), 1)

            def msplit(l):
                dve.wait_ge(sem("mhi_ready"), l + 1)
                V.tensor_tensor(x_lo[:], merged[:], x_hi[:].bitcast(F32), ALU.subtract).then_inc(sem("mlo_ready"), 1)

            def layer_norm(m, added):
                for t in range(NT):
                    for h in range(2):
                        part = xtok[:, t, h * 512:(h + 1) * 512]
                        last = V.scalar_tensor_tensor(part, part, ALPHA, added(t, h), ALU.mult, ALU.add)
                link(last)
                for t in range(NT):
                    for h in range(2):
                        last = V.bn_stats(small[:, 56 + 12 * t + 6 * h:62 + 12 * t + 6 * h], xtok[:, t, h * 512:(h + 1) * 512])
                link(last)
                for t in range(NT):
                    last = V.bn_aggr(small[:, 80 + 2 * t:82 + 2 * t], small[:, 56 + 12 * t:68 + 12 * t])
                mark(last, "ln_var_ready", m + 1)
                dve.wait_ge(sem("ln_sd_ready"), m + 1)
                link(V.reciprocal(small[:, 54:56], small[:, 50:52]))
                for t in range(NT):
                    last = V.tensor_scalar(xtok[:, t, :], xtok[:, t, :], small[:, 80 + 2 * t:81 + 2 * t],
                                           small[:, 54 + t:55 + t], ALU.subtract, ALU.mult)
                mark(last, "xn_ready", m + 1)

            def feature_major(m, l, which):
                for k in range(4):
                    dve.wait_ge(sem("xnt_done"), 4 * m + k + 1)
                    for kk in (2 * k, 2 * k + 1):
                        last = V.tensor_scalar(xf[:, kk, :], tiles(Y[k][:])[:, kk % 2, :], par_col(l, f"ln{which}_g", kk),
                                               par_col(l, f"ln{which}_b", kk), ALU.mult, ALU.add)
                    mark(last, "xf_ready", 4 * m + k + 1)
                for k in range(4):
                    dve.wait_ge(sem("x_hi_ready"), 4 * m + k + 2)
                    c = slice(2 * k, 2 * k + 2)
                    V.tensor_tensor(x_lo[:, c, :], xf[:, c, :], x_hi[:, c, :].bitcast(F32), ALU.subtract)\
                        .then_inc(sem("x_lo_ready"), 1)

            def ffn(u, i, g, nt, moe):
                def hidden(f, par_f, g_last):
                    dve.wait_ge(sem("silu_ready"), f + 1)
                    if not isinstance(f, int) or f >= 2:
                        dve.wait_ge(sem("ht_done"), g_last)
                    V.tensor_tensor(hid[:, par_f, 0:nt, :], sil[:, par_f, 0:nt, :], tiles(W[par_f][:])[:, 0:nt, P:2 * P],
                                    ALU.mult).then_inc(sem("hid_ready"), 1)

                def hid_lo(g):
                    dve.wait_ge(sem("hhi_ready"), g + 1)
                    V.tensor_tensor(o_lo[:, 0:2, 0:nt * P], tiles(W[2][:])[:, :, 0:nt * P],
                                    o_hi[:, 0:2, 0:nt * P].bitcast(F32), ALU.subtract).then_inc(sem("hlo_ready"), 1)

                def lo(u, i):
                    if moe:
                        split_lo(u, i)

                lo(u + 2, i)
                hidden(2 * g, 0, g)
                lo(u + 3, i)
                hidden(2 * g + 1, 1, g)
                with dve.Fori(1, NPAIR) as j:
                    lo(u + 4, i + j - 1)
                    hidden(2 * (g + j), 0, g + j)
                    hid_lo(g + j - 1)
                    lo(u + 5, i + j - 1)
                    hidden(2 * (g + j) + 1, 1, g + j)
                    lo(u + 6, i + j - 1)
                lo(u + 4, i + NPAIR - 1)
                hid_lo(g + NPAIR - 1)

            def routing():
                dve.wait_ge(sem("logits_done"), 1)
                i8 = cmo[:, E_I8:E_I8 + NE]
                for t in range(NT):
                    r = route[:, t, :]
                    link(V.tensor_copy(r[:, 0:8], E[:, t * NE:(t + 1) * NE]))
                    link(V.max(r[:, 8:16], r[:, 0:8]))
                    link(V.max_index(idx[:, t, :], r[:, 8:16], r[:, 0:8]))
                    link(V.tensor_copy(r[:, 18:20], idx[:, t, 0:2]))
                    last = V.tensor_tensor(r[:, 17:18], r[:, 9:10], r[:, 8:9], ALU.subtract)
                mark(last, "top_ready", 1)
                dve.wait_ge(sem("gexp_ready"), 1)
                for t in range(NT):
                    r = route[:, t, :]
                    link(V.tensor_scalar(r[:, 20:21], r[:, 16:17], 1.0, None, ALU.add))
                    link(V.reciprocal(r[:, 21:22], r[:, 20:21]))
                    link(V.tensor_tensor(r[:, 22:23], r[:, 16:17], r[:, 21:22], ALU.mult))
                    link(V.tensor_scalar(r[:, 24:32], i8, r[:, 18:19], None, ALU.is_equal))
                    link(V.tensor_scalar(r[:, 32:40], i8, r[:, 19:20], r[:, 22:23], ALU.is_equal, ALU.mult))
                    link(V.scalar_tensor_tensor(gsel[:, t, :], r[:, 24:32], r[:, 21:22], r[:, 32:40], ALU.mult, ALU.add))
                    last = V.scalar_tensor_tensor(r[:, 40:48], i8, r[:, 19:20], r[:, 24:32], ALU.is_equal, ALU.add)
                mark(last, "mask_ready", 1)
                dve.wait_ge(sem("place_done"), 1)
                for t in range(NT):
                    r = route[:, t, :]
                    link(V.scalar_tensor_tensor(r[:, 48:56], E[:, 32 + 8 * t:40 + 8 * t], 1.0, r[:, 40:48], ALU.add, ALU.mult))
                    link(V.tensor_scalar(posm[:, t, :], r[:, 48:56], -1.0, None, ALU.add))
                link(V.reduce_max(small[:, 48:49], E[:, 48:56], AX.X))
                mark(V.tensor_scalar(flag[:, 0:1], small[:, 48:49], P + 0.5, None, ALU.is_gt), "flag_ready", 1)

            def experts(u, g, q, chunk):
                iota = cmo[:, E_IOTA + chunk * P:E_IOTA + (chunk + 1) * P]
                with dve.Fori(0, NE) as e:
                    for t in range(NT):
                        slot, gate = posm[:, t, bass.ds(e, 1)], gsel[:, t, bass.ds(e, 1)]
                        V.tensor_scalar(sel[:, t, :], iota, slot, None, ALU.is_equal)
                        last = V.tensor_scalar(selg[:, t, :], iota, slot, gate, ALU.is_equal, ALU.mult)
                    last.then_inc(sem("sel_ready"), 1)
                    dve.wait_ge(sem("rows_hi"), q + e + 1)
                    for s in range(2):
                        c = slice(4 * s, 4 * s + 4)
                        last = V.tensor_tensor(x_lo[:, c, 0:P], tiles(Y[2 + s][:], 4), x_hi[:, c, 0:P].bitcast(F32), ALU.subtract)
                    last.then_inc(sem("rows_ready"), 1)
                    ffn(u, NPAIR * e, g + NPAIR * e, 1, True)
                    for t, banks in ((0, (Y[2], Y[3])), (1, (E, W[2]))):
                        dve.wait_ge(sem("comb_done"), 2 * (q + e) + t + 1)
                        for h in range(2):
                            part = facc[:, t, h * 512:(h + 1) * 512]
                            V.tensor_tensor(part, part, banks[h][:], ALU.add)

            dve.wait_ge(sem("x_hi_ready"), 1)
            V.tensor_tensor(x_lo[:], xf[:], x_hi[:].bitcast(F32), ALU.subtract).then_inc(sem("x_lo_ready"), 1)
            handlers = {"units": units, "shift": shift, "conv": conv, "lora": lora, "norm": norm, "prep": prep,
                        "scores": scores, "level": level, "chain": chain, "finish": finish, "attention": attention,
                        "osplit": osplit, "msplit": msplit}
            for l in range(L):
                for name, *args in TIMELINE:
                    if name in handlers:
                        handlers[name](l, *args)
                dve.wait_ge(sem("xres_full"), 16 * (l + 1))
                dve.wait_ge(w_used, layer_unit(l) + MIX_UNITS)
                layer_norm(2 * l, lambda t, h: Y[2 * t + h][:])
                feature_major(2 * l, l, 1)
                if l == 0:
                    ffn(MIX_UNITS, 0, 0, NT, False)
                    dve.wait_ge(w_used, layer_unit(1))
                    dve.wait_ge(sem("xtok_ready"), 1)
                    layer_norm(1, lambda t, h: Y[2 * t + h][:])
                    feature_major(1, 0, 2)
            routing()
            link(V.memset(facc[:], 0.0))
            dve.wait_ge(sem("xtok_ready"), 3)
            experts(MOE_U0, NPAIR, 0, 0)
            with dve.If(dve.value_load(flag[0:1, 0:1], min_val=0, max_val=1)):
                experts(END_U, NPAIR * (NE + 1), NE, 1)
            link(V.engine_nop())
            layer_norm(3, lambda t, h: facc[:, t, h * 512:(h + 1) * 512])
            dve.wait_ge(sem("gb_full"), 64)
            for t in range(NT):
                link(V.tensor_tensor(xtok[:, t, :], xtok[:, t, :], gb[:, 0, :], ALU.mult))
            V.tensor_tensor(xtok[:, 0, :], xtok[:, 0, :], gb[:, 1, :], ALU.add)
            V.tensor_tensor(xtok[:, 1, :], xtok[:, 1, :], gb[:, 1, :], ALU.add).then_inc(sem("out_ready"), 1)


def constants():
    i, j = np.arange(P)[:, None], np.arange(P)[None, :]
    rot = np.where((j % HD < HD // 2) & (i == j + HD // 2), -1.0, 0.0) + np.where((j % HD >= HD // 2) & (i == j - HD // 2), 1.0, 0.0)
    levels = [((i >> v) % 2 == 0) & ((j >> v) == (i >> v) + 1) for v in range(LEVELS)]
    general = np.concatenate([i == j, (i // HD) == (j // HD), rot, i < j, i <= j] + levels, 1)
    half = HD // 2
    inv = np.float32(10000.0) ** (-np.arange(half, dtype=np.float32) / np.float32(half))
    ang = (np.arange(T, dtype=np.float32)[None, :] * inv[:, None]).astype(np.float32)
    causal = np.where(j <= i, 0.0, -1e30)
    att = np.concatenate([np.tile(np.cos(ang), (4, 1)), np.tile(np.sin(ang), (4, 1)), causal, 0 * causal, causal], 1)
    row = np.arange(2 * P)[None, :] + 0 * i
    moe = np.concatenate([np.ones((P, P)), row, row[:, :NE]], 1)
    return [np.ascontiguousarray(c, dtype=np.float32) for c in (general, att, moe)]


def kernel(**inputs):
    import concourse.bacc as bacc
    from concourse.bass_utils import run_bass_kernel_spmd

    a = {k: np.asarray(v) for k, v in inputs.items()}

    def columns(v):
        return v.reshape(L, -1, P).transpose(0, 2, 1)

    conv = a["conv_w"]
    par = np.concatenate([columns(v) for v in (
        a["shift_mu"], a["decay_w0"], a["aaa_a0"], a["k_k"], a["k_a"], a["r_k"], a["gn_g"], a["gn_b"],
        conv[:, 0], conv[:, 1], conv[:, 2], a["ln1_g"], a["ln1_b"], a["ln2_g"], a["ln2_b"])], 2).transpose(1, 0, 2)
    w2 = np.zeros((L, P, 2, BR), np.float32)
    w2[:, 0:64, 0], w2[:, 64:128, 1] = a["decay_w2"], a["aaa_w2"]
    ln_gb = np.stack([np.stack([a[f"ln{k}_g"][l], a[f"ln{k}_b"][l]]) for l in range(L) for k in (1, 2)])
    ln_gb = np.broadcast_to(ln_gb[:, None], (2 * L, P, 2, D))
    general, att, moe = constants()
    x = a["x"].reshape(T, D)
    data = {
        "x": x, "x_t": x.T.reshape(KD, P, T).transpose(1, 0, 2), "w_in": a["w_in"], "w_branch": a["w_branch"],
        "w_out": a["w_out"], "w2": w2, "gate_w2": a["gate_w2"], "par": par, "const": general, "const_att": att,
        "const_moe": moe, "ln_gb": ln_gb, "router": a["router_w"][0].reshape(KD, P, NE).transpose(1, 0, 2),
        "ffn_gate": a["ffn_w_gate"][0], "ffn_up": a["ffn_w_up"][0], "ffn_down": a["ffn_w_down"][0],
        "moe_gate": a["moe_w_gate"].reshape(NE * D, DFF), "moe_up": a["moe_w_up"].reshape(NE * D, DFF),
        "moe_down": a["moe_w_down"].reshape(NE * DFF, D),
    }
    nc = bacc.Bacc("TRN2", target_bir_lowering=False, num_devices=1)
    arrays = {k: np.ascontiguousarray(v) for k, v in data.items()}
    aps = [nc.dram_tensor(k, v.shape, mybir.dt.from_np(v.dtype), kind="ExternalInput").ap() for k, v in arrays.items()]
    result = nc.dram_tensor("result", (T, D), F32, kind="ExternalOutput").ap()
    trunk(nc, *aps, result)
    r = run_bass_kernel_spmd(nc, [arrays], core_ids=[0])
    return r.results[0]["result"].reshape(1, T, D)
```

```python
import math
from contextlib import ExitStack

import numpy as np

import concourse.bass as bass
from concourse import mybir

F32 = mybir.dt.float32
F32R = mybir.dt.float32r
I32 = mybir.dt.int32
U32 = mybir.dt.uint32
ALU = mybir.AluOpType
ACT = mybir.ActivationFunctionType
AX = mybir.AxisListType

P = 128
T = 256
D = 1024
KD = D // P
NT = T // P
L = 2
HD = 64
BR = 512
BT = BR // P
DFF = 2816
NPAIR = DFF // (2 * P)
NE = 8
KAPPA = math.exp(-0.5)
ALPHA = (2 * L) ** 0.25
LN_EPS, GN_EPS = 1e-5, 64e-5
UN = 2048
UD = 32
LEVELS = 7
POOL_MOE = 704

C_ID, C_BLK, C_ROT, C_SI, C_LEV = 0, P, 2 * P, 3 * P, 5 * P
C_COS = C_LEV + LEVELS * P
C_SIN = C_COS + T
C_END = C_SIN + T
E_ONE, E_IOTA, E_I8, E_END = 0, P, 3 * P, 3 * P + NE

PAR, NPAR = {}, 0
for _name, _n in (("mu", 14), ("w0", 4), ("a0", 4), ("k_k", 4), ("k_a", 4), ("r_k", 4), ("gn_g", 4),
                  ("gn_b", 4), ("conv0", 4), ("conv1", 4), ("conv2", 4), ("ln1_g", 8), ("ln1_b", 8),
                  ("ln2_g", 8), ("ln2_b", 8)):
    PAR[_name] = NPAR
    NPAR += _n

SEGMENTS = (("lora", 4608, 1, 1), ("rkv", 3072, 6, 6), ("conv", 0, 6, 6), ("gate0", 4864, 4, 4), ("branch0", 0, 2, 4),
            ("qkv", 1536, 6, 6), ("gate1", 6912, 4, 4), ("branch1", 2, 2, 4),
            ("gate2", 5888, 4, 4), ("branch2", 1, 2, 4), ("out", 0, 4, 0))
UNIT0 = {s[0]: sum(x[2] for x in SEGMENTS[:i]) for i, s in enumerate(SEGMENTS)}
JOB0 = {s[0]: sum(x[3] for x in SEGMENTS[:i]) for i, s in enumerate(SEGMENTS)}
MIX_UNITS = sum(s[2] for s in SEGMENTS)
MIX_JOBS = sum(s[3] for s in SEGMENTS)
FFN_UNITS = 3 * NPAIR
MOE_U0 = 2 * MIX_UNITS + FFN_UNITS
DVE_U0 = MOE_U0 - 1
END_U = MOE_U0 + NE * FFN_UNITS


def dve_parts(u):
    return max(0, u - DVE_U0 + 1) + 1


def layer_unit(l):
    return l * (MIX_UNITS + FFN_UNITS)


TIMELINE = (
    ("units", "lora", 0, 1), ("units", "rkv", 0, 1),
    ("shift", 6), ("lora_in",),
    ("units", "rkv", 1, 2), ("shift", 0), ("lora_w", 0), ("rate_w", 0),
    ("units", "rkv", 2, 3), ("decay", 0), ("shift", 1), ("lora_a", 0), ("rate_a", 0),
    ("units", "rkv", 3, 4), ("shift", 2), ("ksq", 0), ("exps", 0), ("ss", 0), ("knorm", 0),
    ("units", "rkv", 4, 5), ("shift", 3), ("kk", 0),
    ("units", "rkv", 5, 6), ("shift", 4), ("prep", 0),
    ("units", "conv", 0, 1), ("shift", 5), ("decayed", 0), ("tok", 0), ("bonus", 0),
    ("units", "conv", 1, 2), ("scores", 0),
    ("units", "conv", 2, 3), ("level", 0, 1),
    ("units", "conv", 3, 4), ("lora_w", 1), ("rate_w", 1), ("level", 0, 2),
    ("units", "conv", 4, 5), ("decay", 1), ("lora_a", 1), ("rate_a", 1), ("level", 0, 3),
    ("units", "conv", 5, 6), ("ksq", 1), ("exps", 1), ("ss", 1), ("knorm", 1), ("level", 0, 4),
    ("units", "gate0", 0, 1), ("kk", 1), ("level", 0, 5),
    ("units", "gate0", 1, 2), ("prep", 1), ("level", 0, 6),
    ("units", "gate0", 2, 3), ("conv", 0), ("chain", 0, 0),
    ("units", "gate0", 3, 4), ("conv", 1), ("osplit", 0), ("chain", 0, 1),
    ("units", "branch0", 0, 1), ("finish", 0),
    ("units", "branch0", 1, 2), ("decayed", 1), ("tok", 1), ("bonus", 1),
    ("units", "qkv", 0, 1), ("scores", 1),
    ("units", "qkv", 1, 2), ("level", 1, 1),
    ("units", "qkv", 2, 3), ("rope", 0), ("level", 1, 2),
    ("units", "qkv", 3, 4), ("rope", 1), ("level", 1, 3),
    ("units", "qkv", 4, 5), ("rope", 2), ("level", 1, 4),
    ("units", "qkv", 5, 6), ("rope", 3), ("level", 1, 5),
    ("units", "gate1", 0, 1), ("level", 1, 6),
    ("units", "gate1", 1, 2), ("chain", 1, 0),
    ("units", "gate1", 2, 3), ("chain", 1, 1), ("finish", 1), ("osplit", 1),
    ("units", "gate1", 3, 4), ("att_scores",), ("units", "branch1", 0, 2),
    ("softmax",), ("units", "gate2", 0, 2), ("probs_t",), ("units", "gate2", 2, 4),
    ("att_out",), ("units", "branch2", 0, 1), ("msplit", 0), ("units", "branch2", 1, 2), ("msplit", 1), ("units", "out", 0, 4),
)


def trunk(nc, x, x_t, w_in, w_branch, w_out, w2, gate_w2, par, const, const_att, const_moe, ln_gb,
          router, ffn_gate, ffn_up, ffn_down, moe_gate, moe_up, moe_down, out):
    ctx = ExitStack()
    with ctx:
        place = {"at": -(-nc.sbuf_base // 64) * 64}

        def sb_at(name, shape, offset, dt=F32):
            return nc.alloc_sbuf_tensor_at(name, shape, dt, offset=offset)

        def sb(name, shape, dt=F32):
            t = sb_at(name, shape, place["at"], dt)
            place["at"] += -(-4 * math.prod(shape[1:]) // 32) * 32
            return t

        raw = [sb(f"raw{i}", [P, UN]) for i in range(3)]
        w_hi = [sb(f"w_hi{i}", [P, UN], F32R) for i in range(3)]
        w_lo = [sb(f"w_lo{i}", [P, UN], F32R) for i in range(3)]
        x_hi = sb("x_hi", [P, KD, T], F32R)
        x_lo = sb("x_lo", [P, KD, T], F32R)
        o_hi = sb("o_hi", [P, BT, T], F32R)
        o_lo = sb("o_lo", [P, BT, T], F32R)
        xtok_at = place["at"]
        merged = sb("merged", [P, KD, T])
        xtok = sb_at("xtok", [P, NT, D], xtok_at)
        cst = sb("cst", [P, C_END])
        prm = sb("prm", [P, L, NPAR])
        small = sb("small", [P, 128])
        w2_s = sb("w2_s", [P, 2, BR])
        gw2_s = sb("gw2_s", [P, BR])
        arena = place["at"]
        rkvl = sb("rkvl", [P, 14, T])
        share = sb("share", [P, 12, T])
        sgate = sb("sgate", [P, KD, T])
        t1, t2, t3, t4, t6, td = (sb(f"t_{n}", [P, 2, T]) for n in ("a", "r", "k", "g", "b", "d"))
        ar = sb("ar", [P, 4, 2, 2, P])
        sc_at = place["at"]
        sc = sb("sc", [P, 8, 4, P])
        xm = sb("xm", [P, 8, P])
        xt = sb("xt", [P, 8, P])
        mt = sb("mt", [P, 8, P])
        vtok = sb("vtok", [P, NT, 2 * P])
        bktok = sb("bktok", [P, 2, 2 * P])
        g_s = u_s = sb("gu_s", [P, 4, HD])
        s_s = sb("s_s", [P, 2, P])
        assert place["at"] <= nc.sbuf_usable_end, (place["at"], nc.sbuf_usable_end)
        end_of_sbuf = place["at"]
        dsh = sb_at("dsh", [P, 14, T], sc_at)
        place["at"] = sc_at
        qp = sb("qp", [P, 8, T])
        pr = sb("pr", [P, 8, 3, P])
        vatt = sb("vatt", [P, NT, BR])
        cat = sb("cat", [P, 3 * P])
        assert place["at"] <= end_of_sbuf
        place["at"] = arena
        xf = sb("xf", [P, KD, T])
        facc = sb("facc", [P, NT, D])
        y_sb = sb("y_sb", [P, D])
        sil = sb("sil", [P, 2, NT, P])
        hid = sb("hid", [P, 2, NT, P])
        sel = sb("sel", [P, NT, P])
        selg = sb("selg", [P, NT, P])
        selgt = sb("selgt", [P, T])
        cmo = sb("cmo", [P, E_END])
        rt_s = sb("rt_s", [P, KD, NE])
        route = sb("route", [P, NT, 64])
        idx = sb("idx", [P, NT, 8], U32)
        flag = sb("flag", [P, 2], I32)
        posm = sb("posm", [P, NT, NE])
        gsel = sb("gsel", [P, NT, NE])
        assert place["at"] <= sc_at
        gb = sb_at("gb", [P, 2, D], sc_at)

        W = [nc.alloc_psum_tensor(f"W{i}", [P, 512], F32) for i in range(3)]
        Y = [nc.alloc_psum_tensor(f"Y{i}", [P, 512], F32) for i in range(4)]
        E = nc.alloc_psum_tensor("E", [P, 512], F32)
        spill = nc.dram_tensor("x_spill", (T, D), F32, kind="Internal").ap()

        ident = cst[:, C_ID:C_ID + P]
        blk = cst[:, C_BLK:C_BLK + P]
        rot = cst[:, C_ROT:C_ROT + P]
        strict = cst[:, C_SI:C_SI + P]

        def tiles(ap, n=2):
            return ap.rearrange("p (m t) -> p m t", m=n)

        def level_mask(v):
            return cst[:, C_LEV + v * P:C_LEV + (v + 1) * P].unsqueeze(1).to_broadcast([P, 4, P])

        fin1, fin2 = (xm[:, 4 * i:4 * i + 4, :].rearrange("p (m c) t -> p m (c t)", c=2) for i in range(2))

        state_decay = [small[:, 4 + 6 * p:6 + 6 * p] for p in range(2)]

        def par_col(l, name, i):
            return prm[:, l, PAR[name] + i:PAR[name] + i + 1]

        S = {}

        def sem(name):
            if name not in S:
                S[name] = ctx.enter_context(nc.semaphore(name))
            return S[name]

        raw_full = [sem(f"raw_full{i}") for i in range(3)]
        bank_free = [sem(f"bank_free{i}") for i in range(3)]
        hi_done, lo_pool, lo_dve = sem("hi_done"), sem("lo_pool"), sem("lo_dve")
        w_used = sem("w_used")

        def wait_jobs(eng, jobs):
            for b in range(3):
                eng.wait_ge(bank_free[b], (jobs - b + 2) // 3)

        def chained(eng, name):
            s, n = sem(name), [0]

            def link(ins):
                n[0] += 1
                ins.then_inc(s, 1)
                eng.wait_ge(s, n[0])
            return link

        block = ctx.enter_context(nc.Block())

        @block.sync
        def _(sp):
            def load(u, i, first, second):
                if u >= 3:
                    split, split_dve = u - 2 + 3 * i, dve_parts(u - 3) + 3 * i
                    if not isinstance(i, int):
                        split, split_dve = sp.to_reg(split), sp.to_reg(split_dve)
                    sp.wait_ge(hi_done, split)
                    sp.wait_ge(lo_pool, split)
                    if u - 3 >= DVE_U0 or u == 3:
                        sp.wait_ge(lo_dve, split_dve)
                sp.dma_start(*first).then_inc(raw_full[u % 3], 16)
                sp.dma_start(*second).then_inc(raw_full[u % 3], 16)

            def load_cols(u, i, w, col):
                d = raw[u % 3][:].rearrange("p (k c) -> p k c", k=KD)
                s = w[:, bass.ds(col, 256)].rearrange("(k p) c -> p k c", p=P)
                load(u, i, (d[:, 0:4, :], s[:, 0:4, :]), (d[:, 4:8, :], s[:, 4:8, :]))

            def load_gate_up(u, i, wg, wu, row, col):
                d = raw[u % 3][:].rearrange("p (k c) -> p k c", k=KD)
                g, v = (w[bass.ds(row, D), bass.ds(col, P)].rearrange("(k p) c -> p k c", p=P) for w in (wg, wu))
                load(u, i, (d[:, :, 0:P], g), (d[:, :, P:2 * P], v))

            def load_rows(u, i, w, row, n=2):
                d = raw[u % 3][:].rearrange("p (k c) -> p k c", k=n)
                s = w[bass.ds(row, n * P), :].rearrange("(k p) c -> p k c", p=P)
                h = n // 2
                load(u, i, (d[:, 0:h, :], s[:, 0:h, :]), (d[:, h:n, :], s[:, h:n, :]))

            def pair_loads(u, i, wg, wu, wd, row_in, row_hid):
                with sp.Fori(1, NPAIR) as j:
                    load_gate_up(u + 2, i + j - 1, wg, wu, row_in, 256 * j)
                    load_gate_up(u + 3, i + j - 1, wg, wu, row_in, 256 * j + P)
                    load_rows(u + 4, i + j - 1, wd, row_hid + 256 * j - 256)
                load_rows(u + 2, i + NPAIR - 1, wd, row_hid + 256 * (NPAIR - 1))

            for k in range(4):
                c = slice(2 * k, 2 * k + 2)
                sp.dma_start(xf[:, c, :], x_t[:, c, :]).then_inc(sem(f"x_full{k}"), 16)
            for l in range(L):
                for kind, where, n, _ in SEGMENTS:
                    u = layer_unit(l) + UNIT0[kind]
                    if l == 0 and kind == "rkv":
                        sp.dma_start(prm[:], par).then_inc(sem("prm_full"), 16)
                        sp.dma_start(cst[:], const).then_inc(sem("cst_full"), 16)
                    if kind == "out":
                        for q in range(n):
                            load_rows(u + q, 0, w_out[l], 256 * q)
                    elif kind.startswith("branch"):
                        for q in range(n):
                            load_rows(u + q, 0, w_branch[l, :, q * 512:(q + 1) * 512], where * BR, BT)
                    elif n % 3 == 0 and u >= 3:
                        with sp.Fori(0, n // 3) as i:
                            for s in range(3):
                                load_cols(u + s, i, w_in[l], where + 256 * s + 768 * i)
                    else:
                        for q in range(n):
                            load_cols(u + q, 0, w_in[l], where + 256 * q)
                u = layer_unit(l) + MIX_UNITS
                if l == 0:
                    load_gate_up(u, 0, ffn_gate, ffn_up, 0, 0)
                    load_gate_up(u + 1, 0, ffn_gate, ffn_up, 0, P)
                    pair_loads(u, 0, ffn_gate, ffn_up, ffn_down, 0, 0)

            def expert_loads(u):
                def first_pair(v, i, row):
                    load_gate_up(v, i, moe_gate, moe_up, row, 0)
                    load_gate_up(v + 1, i, moe_gate, moe_up, row, P)

                first_pair(u, 0, 0)
                with sp.Fori(0, NE - 1) as e:
                    pair_loads(u, NPAIR * e, moe_gate, moe_up, moe_down, D * e, DFF * e)
                    first_pair(u + 3, NPAIR * e + NPAIR - 1, D * e + D)
                pair_loads(u, NPAIR * (NE - 1), moe_gate, moe_up, moe_down, D * (NE - 1), DFF * (NE - 1))

            expert_loads(MOE_U0)
            sp.wait_ge(sem("flag_ready"), 1)
            with sp.If(sp.value_load(flag[0:1, 0:1], min_val=0, max_val=1)):
                expert_loads(END_U)
            for t in range(NT):
                sp.wait_ge(sem("out_ready"), t + 1)
                sp.dma_start(out[t * P:(t + 1) * P, :], xtok[:, t, :]).then_inc(sem("out_stored"), 16)
            sp.wait_ge(sem("out_stored"), 16 * NT)

        @block.tensor
        def _(pe):
            def mm3(out_ap, lhs, rhs, start, stop):
                nc.tensor.matmul(out_ap, lhs[0], rhs[1], start=start, stop=False)
                nc.tensor.matmul(out_ap, lhs[1], rhs[0], start=False, stop=False)
                return nc.tensor.matmul(out_ap, lhs[0], rhs[0], start=False, stop=stop)

            def unit_ready(u, i=0):
                pe.wait_ge(lo_pool, u + 1 + 3 * i)
                if u >= DVE_U0 or u == 0:
                    pe.wait_ge(lo_dve, dve_parts(u) + 3 * i)

            def job_bank(j, i=0):
                if j >= 3:
                    pe.wait_ge(bank_free[j % 3], j // 3 + i)
                return tiles(W[j % 3][:])

            def x_part(m, k):
                if k % 2 == 0:
                    pe.wait_ge(sem("x_lo_ready"), 4 * m + k // 2 + 1)

            def proj_unit(u, j, fresh=None):
                i = 0
                unit_ready(u, i)
                bank = job_bank(j, i)
                wh, wl = (w[u % 3][:].rearrange("p (k c) -> p k c", k=KD) for w in (w_hi, w_lo))
                for m in range(2):
                    c = slice(m * P, (m + 1) * P)
                    for k in range(KD):
                        if fresh is not None and m == 0:
                            x_part(fresh, k)
                        last = mm3(bank[:, m, :], (wh[:, k, c], wl[:, k, c]), (x_hi[:, k, :], x_lo[:, k, :]),
                                   k == 0, k == KD - 1)
                last.then_inc(w_used, 1)

            def branch_unit(l, b, u, j):
                unit_ready(u)
                pe.wait_ge(sem("o_hi_ready"), 3 * l + b + 1)
                pe.wait_ge(sem("o_lo_ready"), 3 * l + b + 1)
                wh, wl = (w[u % 3][:].rearrange("p (k c) -> p k c", k=BT) for w in (w_hi, w_lo))
                for h in range(2):
                    bank = job_bank(j + h)
                    for m in range(2):
                        c = slice((2 * h + m) * P, (2 * h + m + 1) * P)
                        for k in range(BT):
                            last = mm3(bank[:, m, :], (wh[:, k, c], wl[:, k, c]), (o_hi[:, k, :], o_lo[:, k, :]),
                                       k == 0, k == BT - 1)
                    last.then_inc(w_used if h else sem("half_done"), 1)

            def out_unit(l, q, u):
                unit_ready(u)
                pe.wait_ge(sem("mlo_ready"), 4 * l + q + 1)
                wh, wl = (w[u % 3][:].rearrange("p (k c) -> p k c", k=2) for w in (w_hi, w_lo))
                for k in range(2):
                    kk = 2 * q + k
                    for t in range(NT):
                        tk = slice(t * P, (t + 1) * P)
                        for h in range(2):
                            c = slice(h * 512, (h + 1) * 512)
                            last = mm3(Y[2 * t + h][:], (x_hi[:, kk, tk], x_lo[:, kk, tk]), (wh[:, k, c], wl[:, k, c]),
                                       kk == 0, kk == KD - 1)
                return last

            def units(l, kind, a, b):
                u0, j0 = layer_unit(l) + UNIT0[kind], l * MIX_JOBS + JOB0[kind]
                if kind == "out":
                    for q in range(a, b):
                        out_unit(l, q, u0 + q).then_inc(w_used, 1)
                elif kind.startswith("branch"):
                    for q in range(a, b):
                        branch_unit(l, int(kind[-1]), u0 + q, j0 + 2 * q)
                else:
                    for q in range(a, b):
                        proj_unit(u0 + q, j0 + q, 2 * l if kind == "lora" else None)

            def transpose(out_ap, in_ap):
                return nc.tensor.transpose(out_ap, in_ap, ident)

            def lora_map(l, p, s):
                for m in range(2):
                    c = slice((2 * p + m) * P, (2 * p + m + 1) * P)
                    last = nc.tensor.matmul(tiles(E[:])[:, m, :], w2_s[:, s, c], rkvl[:, 12, :], start=True, stop=True)
                last.then_inc(sem("lora_done"), 1)

            def lora_w(l, p):
                n = 2 * l + p
                if n == 0:
                    pe.wait_ge(sem("cst_full"), 16)
                if p == 0:
                    pe.wait_ge(sem("w2_full"), 16 * (l + 1))
                    pe.wait_ge(sem("lora_in_ready"), l + 1)
                if n:
                    pe.wait_ge(sem("tok_ready"), n)
                lora_map(l, p, 0)

            def lora_a(l, p):
                pe.wait_ge(sem("rate_w_ready"), 2 * l + p + 1)
                lora_map(l, p, 1)

            def ss(l, p):
                pe.wait_ge(sem("rates_ready"), 2 * l + p + 1)
                pe.wait_ge(sem("ksq_ready"), 2 * l + p + 1)
                nc.tensor.matmul(E[:], blk, td[:].rearrange("p m t -> p (m t)"), start=True, stop=True)\
                    .then_inc(sem("ss_done"), 1)

            def tok(l, p):
                n = 2 * l + p
                if n:
                    pe.wait_ge(sem("pass_done"), n)
                pe.wait_ge(sem("prep_ready"), n + 1)
                pe.wait_ge(sem("knorm_ready"), n + 1)
                nc.tensor.matmul(Y[3][:], blk, td[:].rearrange("p m t -> p (m t)"), start=True, stop=True)\
                    .then_inc(sem("bonus_done"), 1)
                pe.wait_ge(sem("decayed_ready"), n + 1)
                for c in range(NT):
                    for m in range(2):
                        transpose(tiles(E[:], 4)[:, 2 * c + m, :], rkvl[:, 8 + 2 * p + m, c * P:(c + 1) * P])
                for s, src in ((0, t6), (1, t3)):
                    for m in range(2):
                        last = transpose(tiles(Y[0][:], 4)[:, 2 * s + m, :], src[:, m, 0:P])
                last.then_inc(sem("tok_done"), 1)

            def scores(l, p):
                n = 2 * l + p
                pe.wait_ge(sem("decayed_ready"), n + 1)
                pe.wait_ge(sem("tok_ready"), n + 1)
                pe.wait_ge(sem("bonus_ready"), n + 1)
                for u in range(8):
                    c, h = divmod(u, 4)
                    bank = Y[(1 + u) % 4]
                    if u >= 4:
                        pe.wait_ge(sem("score_ready"), 8 * n + u - 3)
                    rhs = ar[:, h, c].rearrange("p s t -> p (s t)")
                    nc.tensor.matmul(bank[:, 0:256], t6[:, h // 2, c * P:(c + 1) * P], rhs, start=True, stop=True)
                    nc.tensor.matmul(bank[:, 256:512], t3[:, h // 2, c * P:(c + 1) * P], rhs, start=True, stop=True)\
                        .then_inc(sem("score_done"), 1)
                untranspose(n, 0)

            def untranspose(n, v):
                for c in range(NT):
                    pe.wait_ge(sem("xt_ready"), 2 * LEVELS * n + 2 * v + c + 1)
                    for h in range(4):
                        last = transpose(tiles(Y[c][:], 4)[:, h, :], xt[:, 4 * c + h, :])
                    last.then_inc(sem("x_done"), 1)

            def level(l, p, v):
                n = 2 * l + p
                at = 2 * (LEVELS - 1) * n + 2 * (v - 1)
                for c in range(NT):
                    pe.wait_ge(sem("x_ready"), at + c + 1)
                    pe.wait_ge(sem("mt_ready"), at + c + 1)
                    for h in range(4):
                        last = nc.tensor.matmul(tiles(Y[c][:], 4)[:, h, :], mt[:, 4 * c + h, :], xm[:, 4 * c + h, :],
                                                start=True, stop=True)
                    last.then_inc(sem("mx_done"), 1)
                for c in range(NT):
                    pe.wait_ge(sem("mx_ready"), at + c + 1)
                    for h in range(4):
                        last = nc.tensor.matmul(tiles(Y[2 + c][:], 4)[:, h, :], mt[:, 4 * c + h, :], xt[:, 4 * c + h, :],
                                                start=True, stop=True)
                    last.then_inc(sem("dxt_done"), 1)
                if v < LEVELS - 1:
                    untranspose(n, v)

            def chain(l, p, c):
                n = 2 * l + p
                heads = [(h, h // 2, slice(h * HD, (h + 1) * HD), slice((h % 2) * HD, (h % 2 + 1) * HD)) for h in range(4)]
                if c == 0:
                    pe.wait_ge(sem("xt_ready"), 2 * LEVELS * (n + 1))
                else:
                    pe.wait_ge(sem("s_ready"), n + 1)
                for h, m, hc, half in heads:
                    last = nc.tensor.matmul(Y[0][:, hc], sc[:, 4 * c + h, 2, :], vtok[:, c, hc], start=True, stop=c == 0)
                    if c:
                        last = nc.tensor.matmul(Y[0][:, hc], ar[:, h, 1, 0, :], s_s[:, m, half], start=False, stop=True)
                last.then_inc(sem("g_done"), 1)
                pe.wait_ge(sem("g_ready"), 2 * n + c + 1)
                for h, m, hc, half in heads:
                    last = nc.tensor.matmul(Y[1][:, hc], xt[:, 4 * c + h, :], g_s[:, h, :], start=True, stop=True)
                last.then_inc(sem("u_done"), 1)
                pe.wait_ge(sem("u_ready"), 2 * n + c + 1)
                if c == 0:
                    for m in range(2):
                        mc = slice(m * P, (m + 1) * P)
                        nc.tensor.matmul(Y[3][:, mc], bktok[:, 0, mc], u_s[:, 2 * m:2 * m + 2, :].rearrange("p a b -> p (a b)"),
                                         start=True, stop=False)
                        last = nc.tensor.matmul(Y[3][:, mc], bktok[:, 1, mc], vtok[:, 0, mc], start=False, stop=True)
                    last.then_inc(sem("s_done"), 1)
                    pe.wait_ge(sem("knorm_ready"), 2 * l + 2)
                    if p:
                        pe.wait_ge(sem("rope_ready"), 4 * l + 4)
                for h, m, hc, half in heads:
                    o = tiles(E[:])[half, m, c * P:(c + 1) * P]
                    nc.tensor.matmul(o, vtok[:, c, hc], sc[:, 4 * c + h, 3, :], start=True, stop=False)
                    if c:
                        nc.tensor.matmul(o, s_s[:, m, half], ar[:, h, 1, 1, :], start=False, stop=False)
                    last = nc.tensor.matmul(o, u_s[:, h, :], sc[:, 4 * c + h, 1, :], start=False, stop=True)
                last.then_inc(sem("y_done"), 1)

            def finish(l, p):
                n = 2 * l + p
                pe.wait_ge(sem("yrow_ready"), n + 1)
                nc.tensor.matmul(Y[0][:], blk, fin1.rearrange("p m t -> p (m t)"), start=True, stop=True)\
                    .then_inc(sem("mean_done"), 1)
                pe.wait_ge(sem("gw2_full"), 16 * (l + 1))
                for m in range(2):
                    last = nc.tensor.matmul(tiles(Y[2][:])[:, m, :], gw2_s[:, (2 * p + m) * P:(2 * p + m + 1) * P],
                                            rkvl[:, 13, :], start=True, stop=True)
                last.then_inc(sem("gatemul_done"), 1)
                pe.wait_ge(sem("ysq_ready"), n + 1)
                nc.tensor.matmul(Y[1][:], blk, fin2.rearrange("p m t -> p (m t)"), start=True, stop=True)\
                    .then_inc(sem("var_done"), 1)

            def rope(l, s):
                wait_jobs(pe, l * MIX_JOBS + JOB0["qkv"] + s + 1)
                if s:
                    pe.wait_ge(sem("rope_ready"), 4 * l + s)
                nc.tensor.matmul(E[:], rot, share[:, 2 * s:2 * s + 2, :].rearrange("p m t -> p (m t)"),
                                 start=True, stop=True).then_inc(sem("rot_done"), 1)

            def att_scores(l):
                pe.wait_ge(sem("pass_done"), 2 * l + 2)
                for c in range(NT):
                    for m in range(BT):
                        last = transpose(tiles(Y[c][:], 4)[:, m, :], share[:, 8 + m, c * P:(c + 1) * P])
                last.then_inc(sem("vt_done"), 1)
                pe.wait_ge(sem("qp_zero"), l + 1)
                pe.wait_ge(sem("qp_ready"), l + 1)
                for h in range(8):
                    bank = tiles(Y[(2 + h) % 4][:], 4)
                    if h == 2:
                        pe.wait_ge(sem("vatt_ready"), l + 1)
                    if h >= 4:
                        pe.wait_ge(sem("att_sc_ready"), 8 * l + h - 3)
                    nc.tensor.matmul(bank[:, 0, :], qp[:, h, 0:P], share[:, 4 + h // 2, 0:P], start=True, stop=True)
                    nc.tensor.matmul(bank[:, 1:3, :].rearrange("p a b -> p (a b)"), qp[:, h, P:T], share[:, 4 + h // 2, :],
                                     start=True, stop=True).then_inc(sem("att_sc_done"), 1)

            def probs_t(l):
                pe.wait_ge(sem("prob_ready"), l + 1)
                for h in range(8):
                    if h >= 3:
                        pe.wait_ge(sem("pt_ready"), 8 * l + h - 2)
                    for s in range(3):
                        last = transpose(tiles(Y[h % 3][:], 4)[:, s, :], pr[:, h, s, :])
                    last.then_inc(sem("pt_done"), 1)

            def att_out(l):
                for h in range(8):
                    pe.wait_ge(sem("pt_ready"), 8 * l + h + 1)
                    o = tiles((E if h < 4 else Y[3])[:])[(h % 2) * HD:(h % 2 + 1) * HD, (h // 2) % 2, :]
                    hc = slice(h * HD, (h + 1) * HD)
                    nc.tensor.matmul(o, vatt[:, 0, hc], pr[:, h, 0:2, :].rearrange("p a b -> p (a b)"), start=True, stop=False)
                    last = nc.tensor.matmul(o[:, P:T], vatt[:, 1, hc], pr[:, h, 2, :], start=False, stop=True)
                last.then_inc(sem("att_done"), 1)

            def norm_transposes(m):
                for t in range(NT):
                    pe.wait_ge(sem("xn_ready"), NT * m + t + 1)
                    for k in range(KD):
                        last = transpose(tiles(Y[k // 2][:])[:, k % 2, t * P:(t + 1) * P], xtok[:, t, k * P:(k + 1) * P])
                        if k % 2 and t == NT - 1:
                            last.then_inc(sem("xnt_done"), 1)

            def gate_up(u, i, f, nt, fresh=None):
                unit_ready(u, i)
                odd, f = f
                if not isinstance(f, int) or f >= 2:
                    pe.wait_ge(sem("hid_ready"), f - 1)
                bank = tiles(W[odd][:])
                wh, wl = (w[u % 3][:].rearrange("p (k c) -> p k c", k=KD) for w in (w_hi, w_lo))
                for t in range(nt):
                    tk = slice(t * P, (t + 1) * P)
                    for k in range(KD):
                        if fresh is not None and t == 0:
                            x_part(fresh, k)
                        last = mm3(bank[:, t, :], (x_hi[:, k, tk], x_lo[:, k, tk]), (wh[:, k, :], wl[:, k, :]),
                                   k == 0, k == KD - 1)
                last.then_inc(w_used, 1)

            def hid_transposes(g, nt):
                pe.wait_ge(sem("hid_ready"), 2 * g + 2)
                for s in range(2):
                    for t in range(nt):
                        last = transpose(tiles(W[2][:], 4)[:, 2 * s + t, :], hid[:, s, t, :])
                last.then_inc(sem("ht_done"), 1)

            def down(u, i, g, nt, first, final):
                unit_ready(u, i)
                pe.wait_ge(sem("hlo_ready"), g + 1)
                wh, wl = (w[u % 3][:].rearrange("p (k c) -> p k c", k=2) for w in (w_hi, w_lo))
                for s in range(2):
                    for t in range(nt):
                        tk = slice(t * P, (t + 1) * P)
                        for h in range(2):
                            c = slice(h * 512, (h + 1) * 512)
                            last = mm3(Y[2 * t + h][:], (o_hi[:, s, tk], o_lo[:, s, tk]), (wh[:, s, c], wl[:, s, c]),
                                       first and s == 0, final and s == 1)
                last.then_inc(w_used, 1)

            def first_pair(u, i, g, nt, fresh=None):
                gate_up(u, i, (0, 2 * g), nt, fresh)
                gate_up(u + 1, i, (1, 2 * g + 1), nt)

            def middle_pairs(u, i, g, nt, n=None):
                gate_up(u + 2, i, (0, 2 * g + 2), nt)
                if n is not None:
                    pe.wait_ge(sem("selg_ready"), n + 1)
                hid_transposes(g, nt)
                gate_up(u + 3, i, (1, 2 * g + 3), nt)
                down(u + 4, i, g, nt, True, False)
                with pe.Fori(2, NPAIR) as j:
                    gate_up(u + 2, i + j - 1, (0, 2 * (g + j)), nt)
                    hid_transposes(g + j - 1, nt)
                    gate_up(u + 3, i + j - 1, (1, 2 * (g + j) + 1), nt)
                    down(u + 4, i + j - 1, g + j - 1, nt, False, False)

            def last_down(u, i, g, nt, rows_of=None):
                hid_transposes(g + NPAIR - 1, nt)
                if rows_of is not None:
                    expert_rows(rows_of)
                down(u + 2, i + NPAIR - 1, g + NPAIR - 1, nt, False, True)

            def expert_rows(n):
                pe.wait_ge(sem("sel_ready"), n + 1)
                for k in range(KD):
                    for t in range(NT):
                        last = nc.tensor.matmul(tiles(Y[2 + k // 4][:], 4)[:, k % 4, :], xtok[:, t, k * P:(k + 1) * P],
                                                sel[:, t, :], start=t == 0, stop=t == NT - 1)
                last.then_inc(sem("rows_done"), 1)

            def experts(u, g, q):
                def expert(e, follow):
                    n = q + e
                    middle_pairs(u, NPAIR * e, g + NPAIR * e, 1, n)
                    for t in range(NT):
                        last = transpose(E[:, t * P:(t + 1) * P], selg[:, t, :])
                    last.then_inc(sem("selgt_done"), 1)
                    last_down(u, NPAIR * e, g + NPAIR * e, 1, n + 1 if follow else None)
                    if follow:
                        pe.wait_ge(sem("rows_ready"), n + 2)
                        first_pair(u + FFN_UNITS, NPAIR * e, g + NPAIR * e + NPAIR, 1)
                    pe.wait_ge(sem("yrows_ready"), n + 1)
                    for t, banks in ((0, (Y[2], Y[3])), (1, (E, W[2]))):
                        for h in range(2):
                            last = nc.tensor.matmul(banks[h][:], selgt[:, t * P:(t + 1) * P], y_sb[:, h * 512:(h + 1) * 512],
                                                    start=True, stop=True)
                        last.then_inc(sem("comb_done"), 1)

                expert_rows(q)
                pe.wait_ge(sem("rows_ready"), q + 1)
                first_pair(u, 0, g, 1)
                with pe.Fori(0, NE - 1) as e:
                    expert(e, True)
                expert(NE - 1, False)

            handlers = {"units": units, "lora_w": lora_w, "lora_a": lora_a, "ss": ss, "tok": tok, "scores": scores,
                        "level": level, "chain": chain, "finish": finish, "rope": rope, "att_scores": att_scores,
                        "probs_t": probs_t, "att_out": att_out}
            for l in range(L):
                for name, *args in TIMELINE:
                    if name in handlers:
                        handlers[name](l, *args)
                norm_transposes(2 * l)
                if l == 0:
                    first_pair(MIX_UNITS, 0, 0, NT, 1)
                    middle_pairs(MIX_UNITS, 0, 0, NT)
                    last_down(MIX_UNITS, 0, 0, NT)
                    norm_transposes(1)
            pe.wait_ge(sem("cmo_full"), 32)
            pe.wait_ge(sem("xf_ready"), 12)
            for t in range(NT):
                for k in range(KD):
                    last = nc.tensor.matmul(E[:, t * NE:(t + 1) * NE], xf[:, k, t * P:(t + 1) * P], rt_s[:, k, :],
                                            start=k == 0, stop=k == KD - 1)
            last.then_inc(sem("logits_done"), 1)
            pe.wait_ge(sem("mask_ready"), 1)
            ones, m0, m1 = cmo[:, E_ONE:E_ONE + P], route[:, 0, 40:48], route[:, 1, 40:48]
            nc.tensor.matmul(E[:, 32:40], strict, m0, start=True, stop=True)
            nc.tensor.matmul(E[:, 40:48], ones, m0, start=True, stop=False)
            nc.tensor.matmul(E[:, 40:48], strict, m1, start=False, stop=True)
            nc.tensor.matmul(E[:, 48:56], ones, m0, start=True, stop=False)
            nc.tensor.matmul(E[:, 48:56], ones, m1, start=False, stop=True).then_inc(sem("place_done"), 1)
            experts(MOE_U0, NPAIR, 0)
            with pe.If(pe.value_load(flag[0:1, 0:1], min_val=0, max_val=1)):
                experts(END_U, NPAIR * (NE + 1), NE)

        @block.scalar
        def _(act):
            link = chained(act, "act_chain")
            A = nc.scalar.activation

            def split_hi(u, i=0):
                act.wait_ge(raw_full[u % 3], UD * (u // 3 + 1 + i))
                if u >= 3:
                    act.wait_ge(w_used, u - 2 + 3 * i)
                A(w_hi[u % 3][:], raw[u % 3][:], ACT.Copy).then_inc(hi_done, 1)

            def out_of_bank(kind, q, u, j):
                act.wait_ge(w_used, u + 1)
                dst = {"lora": rkvl[:, 12:14, :], "rkv": rkvl[:, 2 * q:2 * q + 2, :], "conv": share[:, 2 * q:2 * q + 2, :],
                       "qkv": share[:, 2 * q:2 * q + 2, :]}.get(kind, sgate[:, (2 * q) % KD:(2 * q) % KD + 2, :])
                A(dst, tiles(W[j % 3][:]), ACT.Sigmoid if kind.startswith("gate") else ACT.Copy)\
                    .then_inc(bank_free[j % 3], 1)

            def units(l, kind, a, b):
                u0, j0 = layer_unit(l) + UNIT0[kind], l * MIX_JOBS + JOB0[kind]
                if kind == "qkv":
                    act.wait_ge(sem("o_hi_ready"), 3 * l + 1)
                    act.wait_ge(sem("o_lo_ready"), 3 * l + 1)
                if kind in ("gate1", "gate2"):
                    wait_jobs(act, l * MIX_JOBS + JOB0[f"branch{int(kind[-1]) - 1}"] + 4)
                if kind == "out" or kind.startswith("branch"):
                    for q in range(a, b):
                        split_hi(u0 + q + 2)
                    return
                for q in range(a, b):
                    split_hi(u0 + q + 2)
                    out_of_bank(kind, q, u0 + q, j0 + q)

            def lora_in(l):
                act.wait_ge(sem("lora_shifted"), l + 1)
                link(A(rkvl[0:64, 12, :], rkvl[0:64, 12, :], ACT.Tanh))
                A(rkvl[:, 13, :], rkvl[:, 13, :], ACT.Sigmoid).then_inc(sem("lora_in_ready"), 1)

            def rate_w(l, p):
                n = 2 * l + p
                act.wait_ge(sem("lora_done"), 2 * n + 1)
                if n == 0:
                    act.wait_ge(sem("prm_full"), 16)
                if n:
                    act.wait_ge(sem("decayed_ready"), n)
                for m in range(2):
                    last = A(t1[:, m, :], tiles(E[:])[:, m, :], ACT.Sigmoid, bias=par_col(l, "w0", 2 * p + m))
                last.then_inc(sem("rate_w_ready"), 1)

            def rate_a(l, p):
                act.wait_ge(sem("lora_done"), 2 * (2 * l + p) + 2)
                for m in range(2):
                    last = A(t4[:, m, :], tiles(E[:])[:, m, :], ACT.Sigmoid, bias=par_col(l, "a0", 2 * p + m))
                last.then_inc(sem("rates_ready"), 1)

            def exps(l, p):
                n = 2 * l + p
                act.wait_ge(sem("decay_ready"), n + 1)
                A(t1[:], t1[:], ACT.Exp, scale=-KAPPA)
                A(t3[:], t2[:], ACT.Exp, scale=KAPPA).then_inc(sem("act_t3"), 1)
                act.wait_ge(sem("act_t3"), n + 1)
                A(t2[:], t2[:], ACT.Exp, scale=-KAPPA)
                A(state_decay[p], state_decay[p], ACT.Exp, scale=-KAPPA).then_inc(sem("exp_ready"), 1)

            def knorm(l, p):
                act.wait_ge(sem("ss_done"), 2 * l + p + 1)
                A(td[:].rearrange("p m t -> p (m t)"), E[:], ACT.Sqrt).then_inc(sem("knorm_ready"), 1)

            def tok(l, p):
                act.wait_ge(sem("tok_done"), 2 * l + p + 1)
                A(vtok[:].rearrange("p c v -> p (c v)"), E[:], ACT.Copy)
                A(bktok[:].rearrange("p c v -> p (c v)"), Y[0][:], ACT.Copy).then_inc(sem("tok_ready"), 1)

            def copy_x(n, v):
                at = 2 * (LEVELS - 1) * n + 2 * v
                for c in range(NT):
                    act.wait_ge(sem("x_done"), at + c + 1)
                    A(xm[:, 4 * c:4 * c + 4, :], tiles(Y[c][:], 4), ACT.Copy).then_inc(sem("x_ready"), 1)

            def scores(l, p):
                copy_x(2 * l + p, 0)

            def level(l, p, v):
                n = 2 * l + p
                at = 2 * (LEVELS - 1) * n + 2 * (v - 1)
                for c in range(NT):
                    act.wait_ge(sem("mx_done"), at + c + 1)
                    A(mt[:, 4 * c:4 * c + 4, :], tiles(Y[c][:], 4), ACT.Copy).then_inc(sem("mx_ready"), 1)
                if v < LEVELS - 1:
                    copy_x(n, v)

            def finish(l, p):
                n = 2 * l + p
                act.wait_ge(sem("var_done"), n + 1)
                A(fin2.rearrange("p m t -> p (m t)"), Y[1][:], ACT.Sqrt, bias=small[:, 8:9], scale=1.0 / HD)\
                    .then_inc(sem("gn_sd_ready"), 1)
                if p == 1:
                    act.wait_ge(sem("pass_done"), n + 1)
                    act.dma_start(cat[:], const_att).then_inc(sem("cat_full"), 16)
                    if l == 0:
                        act.dma_start(w2_s[:], w2[1]).then_inc(sem("w2_full"), 16)
                        act.dma_start(gw2_s[:], gate_w2[1]).then_inc(sem("gw2_full"), 16)

            def att_scores(l):
                qpv = qp[:].rearrange("p (m h) t -> p m h t", h=2)
                for h in range(2):
                    rows = slice(h * HD, (h + 1) * HD)
                    last = A(qpv[rows, :, h, :], share[rows, 0:BT, :], ACT.Copy)
                last.then_inc(sem("qp_ready"), 1)
                act.wait_ge(sem("vt_done"), l + 1)
                for c in range(NT):
                    last = A(vatt[:, c, :], Y[c][:], ACT.Copy)
                last.then_inc(sem("vatt_ready"), 1)

            def softmax(l):
                act.wait_ge(sem("max_ready"), l + 1)
                for h in range(8):
                    A(pr[:, h, 0, :], pr[:, h, 0, :], ACT.Exp, bias=small[:, 16 + 2 * h:17 + 2 * h],
                      accum_out=small[:, 32 + 2 * h:33 + 2 * h])
                    last = A(pr[:, h, 1:3, :], pr[:, h, 1:3, :], ACT.Exp, bias=small[:, 17 + 2 * h:18 + 2 * h],
                             accum_out=small[:, 33 + 2 * h:34 + 2 * h])
                last.then_inc(sem("e_ready"), 1)

            def probs_t(l):
                for h in range(8):
                    act.wait_ge(sem("pt_done"), 8 * l + h + 1)
                    A(pr[:, h, :, :].rearrange("p s q -> p (s q)"), Y[h % 3][:, 0:3 * P], ACT.Copy).then_inc(sem("pt_ready"), 1)

            def att_out(l):
                act.wait_ge(sem("att_done"), l + 1)
                act.wait_ge(w_used, layer_unit(l) + UNIT0["branch1"] + 2)
                A(o_hi[:, 0:2, :], tiles(E[:]), ACT.Copy)
                A(o_hi[:, 2:4, :], tiles(Y[3][:]), ACT.Copy).then_inc(sem("o_hi_ready"), 1)
                act.wait_ge(sem("o_lo_ready"), 3 * l + 3)
                act.dma_start(gb[:], ln_gb[2 * l]).then_inc(sem("gb_full"), 16)

            def osplit(l, b):
                src = share if b == 0 else rkvl
                if b == 0:
                    act.wait_ge(sem("conv_ready"), 2 * l + 2)
                else:
                    act.wait_ge(sem("pass_done"), 2 * l + 2)
                act.wait_ge(w_used, layer_unit(l) + (UNIT0["branch0"] + 2 if b else 0))
                A(o_hi[:], src[:, 0:BT, :], ACT.Copy).then_inc(sem("o_hi_ready"), 1)

            def msplit(l, half):
                for q in (2 * half, 2 * half + 1):
                    act.wait_ge(sem("gated"), 8 * l + 4 + q + 1)
                    c = slice(2 * q, 2 * q + 2)
                    A(x_hi[:, c, :], merged[:, c, :], ACT.Copy).then_inc(sem("mhi_ready"), 1)
                if half == 0:
                    return
                act.wait_ge(sem("mlo_ready"), 4 * l + 4)
                act.wait_ge(sem("mhi_ready"), 4 * l + 4)
                if l:
                    act.wait_ge(sem("spilled"), 16)
                act.dma_start(xtok[:], (spill if l else x).rearrange("(n p) d -> p n d", p=P)).then_inc(sem("xres_full"), 16)
                if l:
                    act.dma_start(cmo[:], const_moe).then_inc(sem("cmo_full"), 16)
                    act.dma_start(rt_s[:], router).then_inc(sem("cmo_full"), 16)

            def ln_scale(m):
                for t in range(NT):
                    act.wait_ge(sem("ln_var_ready"), NT * m + t + 1)
                    A(small[:, 50 + t:51 + t], small[:, 81 + 2 * t:82 + 2 * t], ACT.Sqrt, bias=small[:, 9:10])\
                        .then_inc(sem("ln_sd_ready"), 1)

            def ln_split(m):
                for k in range(4):
                    act.wait_ge(sem("xf_ready"), 4 * m + k + 1)
                    A(x_hi[:, 2 * k:2 * k + 2, :], xf[:, 2 * k:2 * k + 2, :], ACT.Copy).then_inc(sem("x_hi_ready"), 1)

            def silu(f, nt, used):
                odd, f = f
                act.wait_ge(w_used, used)
                if not isinstance(f, int) or f >= 2:
                    act.wait_ge(sem("hid_ready"), f - 1)
                A(sil[:, odd, 0:nt, :], tiles(W[odd][:])[:, 0:nt, 0:P], ACT.Silu).then_inc(sem("silu_ready"), 1)

            def hid_hi(g, nt, used):
                act.wait_ge(sem("ht_done"), g + 1)
                act.wait_ge(w_used, used)
                A(o_hi[:, 0:2, 0:nt * P], tiles(W[2][:])[:, :, 0:nt * P], ACT.Copy).then_inc(sem("hhi_ready"), 1)

            def first_pair(u, i, g, nt):
                split_hi(u + 2, i)
                silu((0, 2 * g), nt, u + 1 + 3 * i)
                split_hi(u + 3, i)
                silu((1, 2 * g + 1), nt, u + 2 + 3 * i)

            def pair(u, i, g, nt, j, ahead):
                v, w = u + 3 * (i + j - 1), i + j - 1
                split_hi(u + 4, w)
                silu((0, 2 * (g + j)), nt, v + 3)
                hid_hi(g + j - 1, nt, v + 2)
                split_hi(u + 5, w)
                silu((1, 2 * (g + j) + 1), nt, v + 4)
                if ahead:
                    split_hi(u + 6, w)

            def middle_pairs(u, i, g, nt, ahead=True):
                with act.Fori(1, NPAIR if ahead else NPAIR - 1) as j:
                    pair(u, i, g, nt, j, True)
                if not ahead:
                    pair(u, i, g, nt, NPAIR - 1, False)

            def rows_hi(n):
                act.wait_ge(sem("rows_done"), n + 1)
                for s in range(2):
                    last = A(x_hi[:, 4 * s:4 * s + 4, 0:P], tiles(Y[2 + s][:], 4), ACT.Copy)
                last.then_inc(sem("rows_hi"), 1)

            def last_down(u, i, g, nt, ahead=True, rows_of=None):
                hid_hi(g + NPAIR - 1, nt, u + 2 + 3 * (i + NPAIR - 1))
                if rows_of is not None:
                    rows_hi(rows_of)
                if ahead:
                    split_hi(u + 4, i + NPAIR - 1)

            def experts(u, g, q, cold):
                def expert(e, follow):
                    n = q + e
                    middle_pairs(u, NPAIR * e, g + NPAIR * e, 1, follow)
                    act.wait_ge(sem("selgt_done"), n + 1)
                    A(selgt[:], E[:, 0:T], ACT.Copy)
                    last_down(u, NPAIR * e, g + NPAIR * e, 1, follow, n + 1 if follow else None)
                    act.wait_ge(w_used, u + FFN_UNITS * (e + 1))
                    for h in range(2):
                        last = A(y_sb[:, h * 512:(h + 1) * 512], Y[h][:], ACT.Copy)
                    last.then_inc(sem("yrows_ready"), 1)
                    if follow:
                        first_pair(u + FFN_UNITS, NPAIR * e, g + NPAIR * e + NPAIR, 1)

                if cold:
                    split_hi(u)
                    split_hi(u + 1)
                rows_hi(q)
                first_pair(u, 0, g, 1)
                with act.Fori(0, NE - 1) as e:
                    expert(e, True)
                expert(NE - 1, False)

            act.dma_start(w2_s[:], w2[0]).then_inc(sem("w2_full"), 16)
            act.dma_start(gw2_s[:], gate_w2[0]).then_inc(sem("gw2_full"), 16)
            act.wait_ge(sem("eps_ready"), 1)
            for k in range(4):
                c = slice(2 * k, 2 * k + 2)
                act.wait_ge(sem(f"x_full{k}"), 16)
                A(x_hi[:, c, :], xf[:, c, :], ACT.Copy).then_inc(sem("x_hi_ready"), 1)
            split_hi(0)
            split_hi(1)
            handlers = {"units": units, "lora_in": lora_in, "rate_w": rate_w, "rate_a": rate_a, "exps": exps,
                        "knorm": knorm, "tok": tok, "scores": scores, "level": level, "finish": finish,
                        "att_scores": att_scores, "softmax": softmax, "probs_t": probs_t, "att_out": att_out,
                        "osplit": osplit, "msplit": msplit}
            for l in range(L):
                for name, *args in TIMELINE:
                    if name in handlers:
                        handlers[name](l, *args)
                ln_scale(2 * l)
                if l == 0:
                    ln_split(0)
                    act.wait_ge(sem("xtok_ready"), 1)
                    act.dma_start(gb[:], ln_gb[1]).then_inc(sem("gb_full"), 16)
                    first_pair(MIX_UNITS, 0, 0, NT)
                    middle_pairs(MIX_UNITS, 0, 0, NT)
                    last_down(MIX_UNITS, 0, 0, NT)
                    ln_scale(1)
                    ln_split(1)
                    act.wait_ge(sem("xtok_ready"), 2)
                    act.dma_start(spill.rearrange("(n p) d -> p n d", p=P), xtok[:]).then_inc(sem("spilled"), 16)
            act.wait_ge(sem("logits_done"), 1)
            act.wait_ge(sem("top_ready"), 1)
            for t in range(NT):
                last = A(route[:, t, 16:17], route[:, t, 17:18], ACT.Exp)
            last.then_inc(sem("gexp_ready"), 1)
            act.wait_ge(sem("xtok_ready"), 3)
            act.dma_start(gb[:], ln_gb[3]).then_inc(sem("gb_full"), 16)
            experts(MOE_U0, NPAIR, 0, False)
            act.wait_ge(sem("flag_ready"), 1)
            with act.If(act.value_load(flag[0:1, 0:1], min_val=0, max_val=1)):
                experts(END_U, NPAIR * (NE + 1), NE, True)
            ln_scale(3)

        @block.gpsimd
        def _(pool):
            link = chained(pool, "pool_chain")

            def split_lo(u, i=0):
                pool.wait_ge(hi_done, u + 1 + 3 * i)
                c = slice(UN - POOL_MOE if u >= DVE_U0 or u == 0 else 0, UN)
                nc.gpsimd.tensor_tensor(w_lo[u % 3][:, c], raw[u % 3][:, c], w_hi[u % 3][:, c].bitcast(F32), ALU.subtract)\
                    .then_inc(lo_pool, 1)

            def units(l, kind, a, b):
                for q in range(a, b):
                    split_lo(layer_unit(l) + UNIT0[kind] + q + 2)

            def scale_xtok(m):
                pool.wait_ge(sem("gb_full"), 16 * (m + 1))
                pool.wait_ge(sem("xnt_done"), 4 * (m + 1))
                for s, op in ((0, ALU.mult), (1, ALU.add)):
                    for t in range(NT):
                        last = nc.gpsimd.tensor_tensor(xtok[:, t, :], xtok[:, t, :], gb[:, s, :], op)
                        if s == 0 or t == 0:
                            link(last)
                last.then_inc(sem("xtok_ready"), 1)

            def ffn(u, i, ahead=True):
                with pool.Fori(1, NPAIR if ahead else NPAIR - 1) as j:
                    for s in range(3):
                        split_lo(u + 4 + s, i + j - 1)
                if ahead:
                    split_lo(u + 4, i + NPAIR - 1)
                else:
                    split_lo(u + 4, NPAIR - 2 + i)
                    split_lo(u + 5, NPAIR - 2 + i)

            def experts(u, cold):
                for s in range(0 if cold else 2, 4):
                    split_lo(u + s)
                with pool.Fori(0, NE - 1) as e:
                    ffn(u, NPAIR * e)
                    split_lo(u + FFN_UNITS + 2, NPAIR * e)
                    split_lo(u + FFN_UNITS + 3, NPAIR * e)
                ffn(u, NPAIR * (NE - 1), False)

            nc.gpsimd.memset(small[:], 0.0).then_inc(sem("pool_zero"), 1)
            pool.wait_ge(sem("pool_zero"), 1)
            link(nc.gpsimd.memset(small[:, 8:9], GN_EPS))
            nc.gpsimd.memset(small[:, 9:10], LN_EPS).then_inc(sem("eps_ready"), 1)
            split_lo(0)
            split_lo(1)
            nc.gpsimd.memset(ar[:], 0.0).then_inc(sem("ar_zero"), 1)
            for l in range(L):
                for name, *args in TIMELINE:
                    if name == "units":
                        units(l, *args)
                scale_xtok(2 * l)
                if l == 0:
                    split_lo(MIX_UNITS + 2)
                    split_lo(MIX_UNITS + 3)
                    ffn(MIX_UNITS, 0)
                    scale_xtok(1)
            experts(MOE_U0, False)
            pool.wait_ge(sem("flag_ready"), 1)
            with pool.If(pool.value_load(flag[0:1, 0:1], min_val=0, max_val=1)):
                experts(END_U, True)

        @block.vector
        def _(dve):
            link = chained(dve, "dve_chain")
            V = nc.vector

            def mark(ins, name, value):
                ins.then_inc(sem(name), 1)
                dve.wait_ge(sem(name), value)

            def split_lo(u, i=0):
                dve.wait_ge(hi_done, u + 1 + 3 * i)
                c = slice(0, UN - POOL_MOE)
                V.tensor_tensor(w_lo[u % 3][:, c], raw[u % 3][:, c], w_hi[u % 3][:, c].bitcast(F32), ALU.subtract)\
                    .then_inc(lo_dve, 1)

            def units(l, kind, a, b):
                u0, j0 = layer_unit(l) + UNIT0[kind], l * MIX_JOBS + JOB0[kind]
                for q in range(a, b):
                    if u0 + q + 2 >= DVE_U0:
                        split_lo(u0 + q + 2)
                    if kind.startswith("branch"):
                        gate_unit(l, int(kind[-1]), q, u0 + q, j0 + 2 * q)

            def gate_unit(l, b, q, u, j):
                if q == 0:
                    wait_jobs(dve, l * MIX_JOBS + JOB0[f"branch{b}"])
                    if b == 0 and l:
                        dve.wait_ge(sem("spilled"), 16)
                for h in range(2):
                    if h == 0:
                        dve.wait_ge(sem("half_done"), 2 * (3 * l + b) + q + 1)
                    else:
                        dve.wait_ge(w_used, u + 1)
                    ft = slice(4 * q + 2 * h, 4 * q + 2 * h + 2)
                    free, value = bank_free[(j + h) % 3], (j + h) // 3 + 1
                    dst = td[:] if b else merged[:, ft, :]
                    V.tensor_tensor(dst, tiles(W[(j + h) % 3][:]), sgate[:, ft, :], ALU.mult).then_inc(free, 1)
                    if b:
                        dve.wait_ge(free, value)
                        mark(V.tensor_tensor(merged[:, ft, :], merged[:, ft, :], td[:], ALU.add),
                             "gated", 8 * l + 4 * (b - 1) + 2 * q + h + 1)

            def shift(l, q):
                wait_jobs(dve, l * MIX_JOBS + (JOB0["lora"] if q == 6 else JOB0["rkv"] + q) + 1)
                c = slice(2 * q, 2 * q + 2)
                link(V.tensor_tensor(dsh[:, c, 1:T], rkvl[:, c, 0:T - 1], rkvl[:, c, 1:T], ALU.subtract))
                link(V.tensor_scalar(dsh[:, c, 0:1], rkvl[:, c, 0:1], -1.0, None, ALU.mult))
                for i in (2 * q, 2 * q + 1):
                    last = V.scalar_tensor_tensor(rkvl[:, i, :], dsh[:, i, :], par_col(l, "mu", i), rkvl[:, i, :],
                                                  ALU.mult, ALU.add)
                if q == 6:
                    mark(last, "lora_shifted", l + 1)
                else:
                    link(last)

            def conv(l, half):
                if half == 0:
                    wait_jobs(dve, l * MIX_JOBS + JOB0["gate0"])
                m = range(2 * half, 2 * half + 2)
                ch, cb, cc = (share[:, 4 * s + 2 * half:4 * s + 2 * half + 2, :] for s in range(3))
                link(V.tensor_tensor(cc, cc, ch, ALU.mult))
                for i in range(2):
                    last = V.tensor_scalar(ch[:, i, :], cc[:, i, :], par_col(l, "conv2", m[i]), None, ALU.mult)
                for tap, back in (("conv1", 1), ("conv0", 2)):
                    link(last)
                    for i in range(2):
                        last = V.scalar_tensor_tensor(ch[:, i, back:T], cc[:, i, 0:T - back], par_col(l, tap, m[i]),
                                                      ch[:, i, back:T], ALU.mult, ALU.add)
                link(last)
                mark(V.tensor_tensor(ch, ch, cb, ALU.mult), "conv_ready", 2 * l + half + 1)

            def decay(l, p):
                n = 2 * l + p
                dve.wait_ge(sem("rate_w_ready"), n + 1)
                for m in range(2):
                    for c in range(NT):
                        tc = slice(c * P, (c + 1) * P)
                        last = V.tensor_tensor_scan(t2[:, m, tc], t1[:, m, tc], t1[:, m, tc], 0.0, ALU.add, ALU.bypass)
                link(last)
                t2c = t2[:].rearrange("p m (c t) -> p (m c) t", c=NT)
                link(V.tensor_scalar(small[:, 0:4], t2c[:, :, P - 1], 0.5, None, ALU.mult))
                half = small[:, 0:4]
                V.tensor_tensor(state_decay[p], tiles(half)[:, :, 0], tiles(half)[:, :, 1], ALU.add)
                link(V.tensor_tensor(t2c, t2c, half.unsqueeze(2).to_broadcast([P, 4, P]), ALU.subtract))
                mark(V.tensor_tensor(t1[:], t2[:], t1[:], ALU.subtract), "decay_ready", n + 1)

            def ksq(l, p):
                for m in range(2):
                    last = V.tensor_scalar(t6[:, m, :], rkvl[:, 4 + 2 * p + m, :], par_col(l, "k_k", 2 * p + m), None, ALU.mult)
                link(last)
                mark(V.tensor_tensor(td[:], t6[:], t6[:], ALU.mult), "ksq_ready", 2 * l + p + 1)

            def kk(l, p):
                dve.wait_ge(sem("knorm_ready"), 2 * l + p + 1)
                link(V.tensor_scalar(td[:], td[:], 1e-12, None, ALU.max))
                link(V.reciprocal(td[:], td[:]))
                link(V.scalar_tensor_tensor(t6[:], t6[:], -1.0, td[:], ALU.mult, ALU.mult))

            def prep(l, p):
                n = 2 * l + p
                r, k = (rkvl[:, 4 * s + 2 * p:4 * s + 2 * p + 2, :] for s in range(2))
                dve.wait_ge(sem("exp_ready"), n + 1)
                dve.wait_ge(sem("rates_ready"), n + 1)
                V.tensor_tensor(t1[:], t6[:], t1[:], ALU.mult)
                V.tensor_tensor(t2[:], r, t2[:], ALU.mult)
                link(V.scalar_tensor_tensor(td[:], t6[:], -1.0, t4[:], ALU.mult, ALU.mult))
                link(V.tensor_tensor(t6[:], td[:], t3[:], ALU.mult))
                for m in range(2):
                    last = V.tensor_scalar(t4[:, m, :], t4[:, m, :], -1.0, par_col(l, "k_a", 2 * p + m), ALU.add, ALU.mult)
                link(last)
                link(V.scalar_tensor_tensor(k, t4[:], 1.0, k, ALU.add, ALU.mult))
                V.tensor_tensor(t3[:], k, t3[:], ALU.mult)
                for m in range(2):
                    last = V.scalar_tensor_tensor(td[:, m, :], r[:, m, :], par_col(l, "r_k", 2 * p + m), k[:, m, :],
                                                  ALU.mult, ALU.mult)
                mark(last, "prep_ready", n + 1)

            def decayed(l, p):
                n = 2 * l + p
                if n == 0:
                    dve.wait_ge(sem("ar_zero"), 1)
                arv = ar[:].rearrange("p (m h) c s t -> p m h c s t", h=2)
                for s, src in ((0, t1), (1, t2)):
                    for h in range(2):
                        rows = slice(h * HD, (h + 1) * HD)
                        last = V.tensor_copy(arv[rows, :, h, :, s, :], src[rows].rearrange("p m (c t) -> p m c t", c=NT))
                mark(last, "decayed_ready", n + 1)

            def bonus(l, p):
                n = 2 * l + p
                dve.wait_ge(sem("bonus_done"), n + 1)
                mark(V.tensor_tensor(rkvl[:, 2 * p:2 * p + 2, :], tiles(Y[3][:]), rkvl[:, 8 + 2 * p:10 + 2 * p, :], ALU.mult),
                     "bonus_ready", n + 1)

            def mask_level(n, v, c):
                return V.tensor_tensor(mt[:, 4 * c:4 * c + 4, :], sc[:, 4 * c:4 * c + 4, 0, :], level_mask(v), ALU.mult)

            def scores(l, p):
                n = 2 * l + p
                si = cst[:, C_SI:C_SI + 2 * P].unsqueeze(1).to_broadcast([P, 2, 2 * P])
                for u in range(8):
                    dve.wait_ge(sem("score_done"), 8 * n + u + 1)
                    mark(V.tensor_tensor(sc[:, u].rearrange("p (b s) t -> p b (s t)", b=2), tiles(Y[(1 + u) % 4][:]), si, ALU.mult),
                         "score_ready", 8 * n + u + 1)
                for c in range(NT):
                    link(mask_level(n, 0, c))
                    mark(V.tensor_tensor(xt[:, 4 * c:4 * c + 4, :], mt[:, 4 * c:4 * c + 4, :],
                                         ident.unsqueeze(1).to_broadcast([P, 4, P]), ALU.add),
                         "xt_ready", 2 * LEVELS * n + c + 1)
                    mark(mask_level(n, 1, c), "mt_ready", 2 * (LEVELS - 1) * n + c + 1)

            def level(l, p, v):
                n = 2 * l + p
                for c in range(NT):
                    dve.wait_ge(sem("dxt_done"), 2 * (LEVELS - 1) * n + 2 * (v - 1) + c + 1)
                    mark(V.tensor_tensor(xt[:, 4 * c:4 * c + 4, :], xt[:, 4 * c:4 * c + 4, :], tiles(Y[2 + c][:], 4), ALU.add),
                         "xt_ready", 2 * LEVELS * n + 2 * v + c + 1)
                    if v < LEVELS - 1:
                        mark(mask_level(n, v + 1, c), "mt_ready", 2 * (LEVELS - 1) * n + 2 * v + c + 1)

            def chain(l, p, c):
                n = 2 * l + p
                dve.wait_ge(sem("g_done"), 2 * n + c + 1)
                mark(V.tensor_copy(g_s[:].rearrange("p a b -> p (a b)"), Y[0][:, 0:256]), "g_ready", 2 * n + c + 1)
                dve.wait_ge(sem("u_done"), 2 * n + c + 1)
                mark(V.tensor_copy(u_s[:].rearrange("p a b -> p (a b)"), Y[1][:, 0:256]), "u_ready", 2 * n + c + 1)
                if c == 0:
                    dve.wait_ge(sem("s_done"), n + 1)
                    mark(V.tensor_tensor(s_s[:], tiles(Y[3][:, 0:256]), state_decay[p].unsqueeze(2).to_broadcast([P, 2, P]),
                                         ALU.mult), "s_ready", n + 1)

            def finish(l, p):
                n = 2 * l + p
                dst = rkvl[:, 2 * p:2 * p + 2, :]
                dve.wait_ge(sem("y_done"), 2 * n + 2)
                mark(V.tensor_copy(fin1, tiles(E[:])), "yrow_ready", n + 1)
                dve.wait_ge(sem("mean_done"), n + 1)
                link(V.scalar_tensor_tensor(fin1, tiles(Y[0][:]), -1.0 / HD, fin1, ALU.mult, ALU.add))
                mark(V.tensor_tensor(fin2, fin1, fin1, ALU.mult), "ysq_ready", n + 1)
                dve.wait_ge(sem("gn_sd_ready"), n + 1)
                link(V.reciprocal(fin2, fin2))
                link(V.tensor_tensor(fin1, fin1, fin2, ALU.mult))
                for m in range(2):
                    last = V.tensor_scalar(fin1[:, m, :], fin1[:, m, :], par_col(l, "gn_g", 2 * p + m),
                                           par_col(l, "gn_b", 2 * p + m), ALU.mult, ALU.add)
                link(last)
                link(V.tensor_tensor(fin1, fin1, dst, ALU.add))
                dve.wait_ge(sem("gatemul_done"), n + 1)
                mark(V.tensor_tensor(dst, fin1, tiles(Y[2][:]), ALU.mult), "pass_done", n + 1)

            def rope(l, s):
                src = share[:, 2 * s:2 * s + 2, :]
                cos, sin = (cst[:, a:a + T].unsqueeze(1).to_broadcast([P, 2, T]) for a in (C_COS, C_SIN))
                dve.wait_ge(sem("rot_done"), 4 * l + s + 1)
                V.tensor_tensor(t1[:], tiles(E[:]), sin, ALU.mult)
                link(V.tensor_tensor(t2[:], src, cos, ALU.mult))
                mark(V.tensor_tensor(src, t1[:], t2[:], ALU.add), "rope_ready", 4 * l + s + 1)

            def att_scores(l):
                qpv = qp[:].rearrange("p (m h) t -> p m h t", h=2)
                for h in range(2):
                    last = V.memset(qpv[(1 - h) * HD:(2 - h) * HD, :, h, :], 0.0)
                last.then_inc(sem("qp_zero"), 1)
                dve.wait_ge(sem("cat_full"), 16 * (l + 1))
                mask = cat[:]
                for h in range(8):
                    dve.wait_ge(sem("att_sc_done"), 8 * l + h + 1)
                    mark(V.scalar_tensor_tensor(pr[:, h].rearrange("p s q -> p (s q)"), Y[(2 + h) % 4][:, 0:3 * P], HD ** -0.5,
                                                mask, ALU.mult, ALU.add), "att_sc_ready", 8 * l + h + 1)
                    V.reduce_max(small[:, 16 + 2 * h:17 + 2 * h], pr[:, h, 0, :], AX.X)
                    last = V.reduce_max(small[:, 17 + 2 * h:18 + 2 * h], pr[:, h, 1:3, :].rearrange("p s q -> p (s q)"), AX.X)
                link(last)
                mark(V.tensor_scalar(small[:, 16:32], small[:, 16:32], -1.0, None, ALU.mult), "max_ready", l + 1)

            def softmax(l):
                dve.wait_ge(sem("e_ready"), l + 1)
                link(V.reciprocal(small[:, 32:48], small[:, 32:48]))
                inv = small[:, 32:48].rearrange("p (h q) -> p h q", q=2)
                V.tensor_tensor(pr[:, :, 0, :], pr[:, :, 0, :], inv[:, :, 0:1].to_broadcast([P, 8, P]), ALU.mult)
                late = pr[:, :, 1:3, :].rearrange("p h s q -> p h (s q)")
                mark(V.tensor_tensor(late, late, inv[:, :, 1:2].to_broadcast([P, 8, 2 * P]), ALU.mult), "prob_ready", l + 1)

            def att_out(l):
                dve.wait_ge(sem("o_hi_ready"), 3 * l + 3)
                V.tensor_tensor(o_lo[:, 0:2, :], tiles(E[:]), o_hi[:, 0:2, :].bitcast(F32), ALU.subtract)
                V.tensor_tensor(o_lo[:, 2:4, :], tiles(Y[3][:]), o_hi[:, 2:4, :].bitcast(F32), ALU.subtract)\
                    .then_inc(sem("o_lo_ready"), 1)

            def osplit(l, b):
                dve.wait_ge(sem("o_hi_ready"), 3 * l + b + 1)
                V.tensor_tensor(o_lo[:], (rkvl if b else share)[:, 0:BT, :], o_hi[:].bitcast(F32), ALU.subtract)\
                    .then_inc(sem("o_lo_ready"), 1)

            def msplit(l, half):
                for q in (2 * half, 2 * half + 1):
                    dve.wait_ge(sem("mhi_ready"), 4 * l + q + 1)
                    c = slice(2 * q, 2 * q + 2)
                    V.tensor_tensor(x_lo[:, c, :], merged[:, c, :], x_hi[:, c, :].bitcast(F32), ALU.subtract)\
                        .then_inc(sem("mlo_ready"), 1)

            def layer_norm(m, src, added=None):
                for t in range(NT):
                    for h in range(2):
                        part = src[:, t, h * 512:(h + 1) * 512]
                        if added:
                            link(V.scalar_tensor_tensor(part, part, ALPHA, added(t, h), ALU.mult, ALU.add))
                        last = V.bn_stats(small[:, 56 + 12 * t + 6 * h:62 + 12 * t + 6 * h], part)
                    link(last)
                    mark(V.bn_aggr(small[:, 80 + 2 * t:82 + 2 * t], small[:, 56 + 12 * t:68 + 12 * t]),
                         "ln_var_ready", NT * m + t + 1)
                for t in range(NT):
                    dve.wait_ge(sem("ln_sd_ready"), NT * m + t + 1)
                    link(V.reciprocal(small[:, 54 + t:55 + t], small[:, 50 + t:51 + t]))
                    mark(V.tensor_scalar(xtok[:, t, :], src[:, t, :], small[:, 80 + 2 * t:81 + 2 * t],
                                         small[:, 54 + t:55 + t], ALU.subtract, ALU.mult), "xn_ready", NT * m + t + 1)

            def feature_major(m, l, which):
                def lo(k):
                    dve.wait_ge(sem("x_hi_ready"), 4 * (m + 1) + k + 1)
                    c = slice(2 * k, 2 * k + 2)
                    V.tensor_tensor(x_lo[:, c, :], xf[:, c, :], x_hi[:, c, :].bitcast(F32), ALU.subtract)\
                        .then_inc(sem("x_lo_ready"), 1)

                split = m < 2
                for k in range(4):
                    dve.wait_ge(sem("xnt_done"), 4 * m + k + 1)
                    for kk in (2 * k, 2 * k + 1):
                        last = V.tensor_scalar(xf[:, kk, :], tiles(Y[k][:])[:, kk % 2, :], par_col(l, f"ln{which}_g", kk),
                                               par_col(l, f"ln{which}_b", kk), ALU.mult, ALU.add)
                    mark(last, "xf_ready", 4 * m + k + 1)
                    if split and k:
                        lo(k - 1)
                if split:
                    lo(3)

            def hidden(f, nt, transposed):
                odd, f = f
                dve.wait_ge(sem("silu_ready"), f + 1)
                if not isinstance(f, int) or f >= 2:
                    dve.wait_ge(sem("ht_done"), transposed)
                V.tensor_tensor(hid[:, odd, 0:nt, :], sil[:, odd, 0:nt, :], tiles(W[odd][:])[:, 0:nt, P:2 * P],
                                ALU.mult).then_inc(sem("hid_ready"), 1)

            def hid_lo(g, nt):
                dve.wait_ge(sem("hhi_ready"), g + 1)
                V.tensor_tensor(o_lo[:, 0:2, 0:nt * P], tiles(W[2][:])[:, :, 0:nt * P],
                                o_hi[:, 0:2, 0:nt * P].bitcast(F32), ALU.subtract).then_inc(sem("hlo_ready"), 1)

            def expert_lo(u, i, nt):
                if nt == 1:
                    split_lo(u, i)

            def first_pair(u, i, g, nt):
                expert_lo(u + 2, i, nt)
                hidden((0, 2 * g), nt, g)
                expert_lo(u + 3, i, nt)
                hidden((1, 2 * g + 1), nt, g)

            def pair(u, i, g, nt, j, ahead):
                expert_lo(u + 4, i + j - 1, nt)
                hidden((0, 2 * (g + j)), nt, g + j)
                hid_lo(g + j - 1, nt)
                expert_lo(u + 5, i + j - 1, nt)
                hidden((1, 2 * (g + j) + 1), nt, g + j)
                if ahead:
                    expert_lo(u + 6, i + j - 1, nt)

            def middle_pairs(u, i, g, nt, ahead=True):
                with dve.Fori(1, NPAIR if ahead else NPAIR - 1) as j:
                    pair(u, i, g, nt, j, True)
                if not ahead:
                    pair(u, i, g, nt, NPAIR - 1, False)

            def rows_lo(n):
                dve.wait_ge(sem("rows_hi"), n + 1)
                for s in range(2):
                    c = slice(4 * s, 4 * s + 4)
                    last = V.tensor_tensor(x_lo[:, c, 0:P], tiles(Y[2 + s][:], 4), x_hi[:, c, 0:P].bitcast(F32), ALU.subtract)
                last.then_inc(sem("rows_ready"), 1)

            def last_down(u, i, g, nt, ahead=True, rows_of=None):
                hid_lo(g + NPAIR - 1, nt)
                if rows_of is not None:
                    rows_lo(rows_of)
                if ahead:
                    expert_lo(u + 4, i + NPAIR - 1, nt)

            def routing():
                dve.wait_ge(sem("logits_done"), 1)
                i8 = cmo[:, E_I8:E_I8 + NE]
                for t in range(NT):
                    r = route[:, t, :]
                    link(V.tensor_copy(r[:, 0:8], E[:, t * NE:(t + 1) * NE]))
                    link(V.max(r[:, 8:16], r[:, 0:8]))
                    link(V.max_index(idx[:, t, :], r[:, 8:16], r[:, 0:8]))
                    link(V.tensor_copy(r[:, 18:20], idx[:, t, 0:2]))
                    last = V.tensor_tensor(r[:, 17:18], r[:, 9:10], r[:, 8:9], ALU.subtract)
                mark(last, "top_ready", 1)
                dve.wait_ge(sem("gexp_ready"), 1)
                for t in range(NT):
                    r = route[:, t, :]
                    link(V.tensor_scalar(r[:, 20:21], r[:, 16:17], 1.0, None, ALU.add))
                    link(V.reciprocal(r[:, 21:22], r[:, 20:21]))
                    link(V.tensor_tensor(r[:, 22:23], r[:, 16:17], r[:, 21:22], ALU.mult))
                    link(V.tensor_scalar(r[:, 24:32], i8, r[:, 18:19], None, ALU.is_equal))
                    link(V.tensor_scalar(r[:, 32:40], i8, r[:, 19:20], r[:, 22:23], ALU.is_equal, ALU.mult))
                    link(V.scalar_tensor_tensor(gsel[:, t, :], r[:, 24:32], r[:, 21:22], r[:, 32:40], ALU.mult, ALU.add))
                    last = V.scalar_tensor_tensor(r[:, 40:48], i8, r[:, 19:20], r[:, 24:32], ALU.is_equal, ALU.add)
                mark(last, "mask_ready", 1)
                dve.wait_ge(sem("place_done"), 1)
                for t in range(NT):
                    r = route[:, t, :]
                    link(V.scalar_tensor_tensor(r[:, 48:56], E[:, 32 + 8 * t:40 + 8 * t], 1.0, r[:, 40:48], ALU.add, ALU.mult))
                    link(V.tensor_scalar(posm[:, t, :], r[:, 48:56], -1.0, None, ALU.add))
                link(V.reduce_max(small[:, 48:49], E[:, 48:56], AX.X))
                mark(V.tensor_scalar(flag[:, 0:1], small[:, 48:49], P + 0.5, None, ALU.is_gt), "flag_ready", 1)

            def experts(u, g, q, chunk, cold):
                iota = cmo[:, E_IOTA + chunk * P:E_IOTA + (chunk + 1) * P]

                def select(e):
                    for t in range(NT):
                        last = V.tensor_scalar(sel[:, t, :], iota, posm[:, t, bass.ds(e, 1)], None, ALU.is_equal)
                    last.then_inc(sem("sel_ready"), 1)

                def expert(e, follow):
                    n = q + e
                    for t in range(NT):
                        last = V.tensor_scalar(selg[:, t, :], iota, posm[:, t, bass.ds(e, 1)], gsel[:, t, bass.ds(e, 1)],
                                               ALU.is_equal, ALU.mult)
                    last.then_inc(sem("selg_ready"), 1)
                    if follow:
                        select(e + 1)
                    middle_pairs(u, NPAIR * e, g + NPAIR * e, 1, follow)
                    last_down(u, NPAIR * e, g + NPAIR * e, 1, follow, n + 1 if follow else None)
                    if follow:
                        first_pair(u + FFN_UNITS, NPAIR * e, g + NPAIR * e + NPAIR, 1)
                    for t, banks in ((0, (Y[2], Y[3])), (1, (E, W[2]))):
                        dve.wait_ge(sem("comb_done"), 2 * n + t + 1)
                        for h in range(2):
                            part = facc[:, t, h * 512:(h + 1) * 512]
                            last = V.tensor_tensor(part, part, banks[h][:], ALU.add)
                    last.then_inc(sem("facc_ready"), 1)

                if cold:
                    split_lo(u)
                    split_lo(u + 1)
                select(0)
                rows_lo(q)
                first_pair(u, 0, g, 1)
                with dve.Fori(0, NE - 1) as e:
                    expert(e, True)
                expert(NE - 1, False)

            for k in range(4):
                dve.wait_ge(sem("x_hi_ready"), k + 1)
                c = slice(2 * k, 2 * k + 2)
                V.tensor_tensor(x_lo[:, c, :], xf[:, c, :], x_hi[:, c, :].bitcast(F32), ALU.subtract)\
                    .then_inc(sem("x_lo_ready"), 1)
            split_lo(0)
            dve.wait_ge(sem("prm_full"), 16)
            handlers = {"units": units, "shift": shift, "conv": conv, "decay": decay, "ksq": ksq, "kk": kk, "prep": prep,
                        "decayed": decayed, "bonus": bonus, "scores": scores, "level": level, "chain": chain,
                        "finish": finish, "rope": rope, "att_scores": att_scores, "softmax": softmax,
                        "att_out": att_out, "osplit": osplit, "msplit": msplit}
            for l in range(L):
                for name, *args in TIMELINE:
                    if name in handlers:
                        handlers[name](l, *args)
                dve.wait_ge(sem("xres_full"), 16 * (l + 1))
                dve.wait_ge(w_used, layer_unit(l) + MIX_UNITS)
                layer_norm(2 * l, xtok, lambda t, h: Y[2 * t + h][:])
                feature_major(2 * l, l, 1)
                if l == 0:
                    first_pair(MIX_UNITS, 0, 0, NT)
                    middle_pairs(MIX_UNITS, 0, 0, NT)
                    last_down(MIX_UNITS, 0, 0, NT)
                    dve.wait_ge(w_used, layer_unit(1))
                    dve.wait_ge(sem("xtok_ready"), 1)
                    layer_norm(1, xtok, lambda t, h: Y[2 * t + h][:])
                    feature_major(1, 0, 2)
            routing()
            dve.wait_ge(sem("xtok_ready"), 3)
            link(V.tensor_scalar(facc[:], xtok[:], ALPHA, None, ALU.mult))
            experts(MOE_U0, NPAIR, 0, 0, False)
            with dve.If(dve.value_load(flag[0:1, 0:1], min_val=0, max_val=1)):
                experts(END_U, NPAIR * (NE + 1), NE, 1, True)
            link(V.engine_nop())
            layer_norm(3, facc)
            dve.wait_ge(sem("gb_full"), 64)
            for t in range(NT):
                link(V.tensor_tensor(xtok[:, t, :], xtok[:, t, :], gb[:, 0, :], ALU.mult))
                V.tensor_tensor(xtok[:, t, :], xtok[:, t, :], gb[:, 1, :], ALU.add).then_inc(sem("out_ready"), 1)


def constants():
    i, j = np.arange(P)[:, None], np.arange(P)[None, :]
    rot = np.where((j % HD < HD // 2) & (i == j + HD // 2), -1.0, 0.0) + np.where((j % HD >= HD // 2) & (i == j - HD // 2), 1.0, 0.0)
    levels = [((i >> v) % 2 == 0) & ((j >> v) == (i >> v) + 1) for v in range(LEVELS)]
    general = np.concatenate([i == j, (i // HD) == (j // HD), rot, i < j, i <= j] + levels, 1)
    half = HD // 2
    inv = np.float32(10000.0) ** (-np.arange(half, dtype=np.float32) / np.float32(half))
    ang = (np.arange(T, dtype=np.float32)[None, :] * inv[:, None]).astype(np.float32)
    causal = np.where(j <= i, 0.0, -1e30)
    general = np.concatenate([general, np.tile(np.cos(ang), (4, 1)), np.tile(np.sin(ang), (4, 1))], 1)
    att = np.concatenate([causal, 0 * causal, causal], 1)
    row = np.arange(2 * P)[None, :] + 0 * i
    moe = np.concatenate([np.ones((P, P)), row, row[:, :NE]], 1)
    return [np.ascontiguousarray(c, dtype=np.float32) for c in (general, att, moe)]


def kernel(**inputs):
    import concourse.bacc as bacc
    from concourse.bass_utils import run_bass_kernel_spmd

    a = {k: np.asarray(v) for k, v in inputs.items()}

    def columns(v):
        return v.reshape(L, -1, P).transpose(0, 2, 1)

    conv = a["conv_w"]
    par = np.concatenate([columns(v) for v in (
        a["shift_mu"], a["decay_w0"], a["aaa_a0"], a["k_k"], a["k_a"], a["r_k"], a["gn_g"], a["gn_b"],
        conv[:, 0], conv[:, 1], conv[:, 2], a["ln1_g"], a["ln1_b"], a["ln2_g"], a["ln2_b"])], 2).transpose(1, 0, 2)
    w2 = np.zeros((L, P, 2, BR), np.float32)
    w2[:, 0:64, 0], w2[:, 64:128, 1] = a["decay_w2"], a["aaa_w2"]
    ln_gb = np.stack([np.stack([a[f"ln{k}_g"][l], a[f"ln{k}_b"][l]]) for l in range(L) for k in (1, 2)])
    ln_gb = np.broadcast_to(ln_gb[:, None], (2 * L, P, 2, D))
    general, att, moe = constants()
    x = a["x"].reshape(T, D)
    data = {
        "x": x, "x_t": x.T.reshape(KD, P, T).transpose(1, 0, 2), "w_in": a["w_in"], "w_branch": a["w_branch"],
        "w_out": a["w_out"], "w2": w2, "gate_w2": a["gate_w2"], "par": par, "const": general, "const_att": att,
        "const_moe": moe, "ln_gb": ln_gb, "router": a["router_w"][0].reshape(KD, P, NE).transpose(1, 0, 2),
        "ffn_gate": a["ffn_w_gate"][0], "ffn_up": a["ffn_w_up"][0], "ffn_down": a["ffn_w_down"][0],
        "moe_gate": a["moe_w_gate"].reshape(NE * D, DFF), "moe_up": a["moe_w_up"].reshape(NE * D, DFF),
        "moe_down": a["moe_w_down"].reshape(NE * DFF, D),
    }
    nc = bacc.Bacc("TRN2", target_bir_lowering=False, num_devices=1)
    arrays = {k: np.ascontiguousarray(v) for k, v in data.items()}
    aps = [nc.dram_tensor(k, v.shape, mybir.dt.from_np(v.dtype), kind="ExternalInput").ap() for k, v in arrays.items()]
    result = nc.dram_tensor("result", (T, D), F32, kind="ExternalOutput").ap()
    trunk(nc, *aps, result)
    r = run_bass_kernel_spmd(nc, [arrays], core_ids=[0])
    return r.results[0]["result"].reshape(1, T, D)
```

```python
import math
from contextlib import ExitStack

import numpy as np

import concourse.bass as bass
from concourse import mybir

F32 = mybir.dt.float32
F32R = mybir.dt.float32r
I32 = mybir.dt.int32
U32 = mybir.dt.uint32
ALU = mybir.AluOpType
ACT = mybir.ActivationFunctionType
AX = mybir.AxisListType

P = 128
T = 256
D = 1024
KD = D // P
NT = T // P
L = 2
HD = 64
BR = 512
BT = BR // P
DFF = 2816
NPAIR = DFF // (2 * P)
NE = 8
KAPPA = math.exp(-0.5)
ALPHA = (2 * L) ** 0.25
LN_EPS, GN_EPS = 1e-5, 64e-5
UN = 2048
UD = 32
LEVELS = 7
POOL_PART = 672

C_ID, C_BLK, C_ROT, C_SI, C_LEV = 0, P, 2 * P, 3 * P, 5 * P
C_COS = C_LEV + LEVELS * P
C_SIN = C_COS + T
C_END = C_SIN + T
E_ONE, E_IOTA, E_I8, E_END = 0, P, 3 * P, 3 * P + NE

R_TOP, R_EXP, R_IDX, R_GATE, R_ONE, R_TWO, R_MASK, R_POS, R_SUM, R_END = 0, 8, 10, 12, 16, 24, 32, 40, 48, 56

PAR, NPAR = {}, 0
for _name, _n in (("mu", 14), ("w0", 4), ("a0", 4), ("k_k", 4), ("k_a", 4), ("r_k", 4), ("gn_g", 4),
                  ("gn_b", 4), ("conv0", 4), ("conv1", 4), ("conv2", 4), ("ln1_g", 8), ("ln1_b", 8),
                  ("ln2_g", 8), ("ln2_b", 8)):
    PAR[_name] = NPAR
    NPAR += _n

SEGMENTS = (("lora", 4608, 1, 1), ("rkv", 3072, 6, 6), ("conv", 0, 6, 6), ("gate0", 4864, 4, 4), ("branch0", 0, 2, 4),
            ("qkv", 1536, 6, 6), ("gate1", 6912, 4, 4), ("branch1", 2, 2, 4),
            ("gate2", 5888, 4, 4), ("branch2", 1, 2, 4), ("out", 0, 4, 0))
UNIT0 = {s[0]: sum(x[2] for x in SEGMENTS[:i]) for i, s in enumerate(SEGMENTS)}
JOB0 = {s[0]: sum(x[3] for x in SEGMENTS[:i]) for i, s in enumerate(SEGMENTS)}
MIX_UNITS = sum(s[2] for s in SEGMENTS)
MIX_JOBS = sum(s[3] for s in SEGMENTS)
FFN_UNITS = 3 * NPAIR
MOE_U0 = 2 * MIX_UNITS + FFN_UNITS
DVE_U0 = MOE_U0 - 1
END_U = MOE_U0 + NE * FFN_UNITS


def layer_unit(l):
    return l * (MIX_UNITS + FFN_UNITS)


def dve_takes(u):
    return u == 0 or MIX_UNITS <= u < layer_unit(1) + 2 or u >= DVE_U0


def dve_parts(u):
    return 1 + min(max(0, u - MIX_UNITS + 1), FFN_UNITS + 2) + max(0, u - DVE_U0 + 1)


TIMELINE = (
    ("units", "lora", 0, 1), ("units", "rkv", 0, 1),
    ("shift", 6), ("lora_in",),
    ("units", "rkv", 1, 2), ("shift", 0), ("lora_w", 0), ("rate_w", 0),
    ("units", "rkv", 2, 3), ("decay", 0), ("shift", 1), ("lora_a", 0), ("rate_a", 0),
    ("spill",), ("units", "rkv", 3, 4), ("shift", 2), ("ksq", 0), ("exps", 0), ("ss", 0), ("knorm", 0),
    ("units", "rkv", 4, 5), ("shift", 3), ("kk", 0),
    ("units", "rkv", 5, 6), ("shift", 4), ("prep", 0),
    ("units", "conv", 0, 1), ("decayed", 0), ("shift", 5), ("tok", 0), ("bonus", 0),
    ("units", "conv", 1, 2), ("scores", 0),
    ("units", "conv", 2, 3), ("invert", 0),
    ("lora_w", 1), ("rate_w", 1), ("units", "conv", 3, 4), ("level", 0, 1),
    ("decay", 1), ("lora_a", 1), ("rate_a", 1), ("units", "conv", 4, 5), ("level", 0, 2),
    ("ksq", 1), ("exps", 1), ("units", "conv", 5, 6), ("level", 0, 3),
    ("ss", 1), ("knorm", 1), ("units", "gate0", 0, 1), ("kk", 1), ("level", 0, 4),
    ("units", "gate0", 1, 2), ("prep", 1), ("level", 0, 5),
    ("conv", 0), ("units", "gate0", 2, 3), ("level", 0, 6),
    ("chain", 0, 0), ("units", "gate0", 3, 4), ("conv", 1), ("chain", 0, 1), ("osplit", 0),
    ("units", "branch0", 0, 1), ("finish", 0),
    ("units", "branch0", 1, 2), ("decayed", 1),
    ("units", "qkv", 0, 1), ("tok", 1), ("bonus", 1),
    ("units", "qkv", 1, 2), ("scores", 1),
    ("units", "qkv", 2, 3), ("invert", 1), ("rope", 0), ("level", 1, 1),
    ("units", "qkv", 3, 4), ("rope", 1), ("level", 1, 2),
    ("units", "qkv", 4, 5), ("rope", 2), ("level", 1, 3),
    ("units", "qkv", 5, 6), ("rope", 3), ("level", 1, 4),
    ("units", "gate1", 0, 1), ("level", 1, 5), ("level", 1, 6),
    ("units", "gate1", 1, 2), ("chain", 1, 0), ("chain", 1, 1), ("finish", 1),
    ("units", "gate1", 2, 4), ("osplit", 1), ("heads",), ("units", "branch1", 0, 2),
    ("att_scores",), ("units", "gate2", 0, 1), ("softmax", 0), ("units", "gate2", 1, 2), ("softmax", 1),
    ("units", "gate2", 2, 4), ("probs_t",), ("att_out",), ("units", "branch2", 0, 1), ("msplit", 0), ("units", "branch2", 1, 2),
    ("msplit", 1), ("units", "out", 0, 4),
)


def trunk(nc, x, x_t, w_in, w_branch, w_out, w2, gate_w2, par, const, const_att, const_moe, ln_gb,
          router, ffn_gate, ffn_up, ffn_down, moe_gate, moe_up, moe_down, out):
    ctx = ExitStack()
    with ctx:
        place = {"at": -(-nc.sbuf_base // 64) * 64}

        def sb_at(name, shape, offset, dt=F32):
            return nc.alloc_sbuf_tensor_at(name, shape, dt, offset=offset)

        def sb(name, shape, dt=F32):
            t = sb_at(name, shape, place["at"], dt)
            place["at"] += -(-4 * math.prod(shape[1:]) // 32) * 32
            return t

        raw = [sb(f"raw{i}", [P, UN]) for i in range(3)]
        w_hi = [sb(f"w_hi{i}", [P, UN], F32R) for i in range(3)]
        w_lo = [sb(f"w_lo{i}", [P, UN], F32R) for i in range(3)]
        x_hi = sb("x_hi", [P, KD, T], F32R)
        x_lo = sb("x_lo", [P, KD, T], F32R)
        o_hi = sb("o_hi", [P, BT, T], F32R)
        o_lo = sb("o_lo", [P, BT, T], F32R)
        xtok_at = place["at"]
        merged = sb("merged", [P, KD, T])
        xtok = sb_at("xtok", [P, NT, D], xtok_at)
        cst = sb("cst", [P, C_END])
        prm = sb("prm", [P, L, NPAR])
        small = sb("small", [P, 128])
        w2_s = sb("w2_s", [P, 2, BR])
        gw2_s = sb("gw2_s", [P, BR])
        arena = place["at"]
        rkvl = sb("rkvl", [P, 14, T])
        share = sb("share", [P, 12, T])
        sgate = sb("sgate", [P, KD, T])
        t1, t2, t3, t4, t6, td = (sb(f"t_{n}", [P, 2, T]) for n in ("a", "r", "k", "g", "b", "d"))
        ar = sb("ar", [P, 4, 2, 2, P])
        sc_at = place["at"]
        sc = sb("sc", [P, 8, 4, P])
        xm = sb("xm", [P, 8, P])
        xt = sb("xt", [P, 8, P])
        mt = sb("mt", [P, 8, P])
        vtok = sb("vtok", [P, NT, 2 * P])
        bktok = sb("bktok", [P, 2, 2 * P])
        g_s = u_s = sb("gu_s", [P, 4, HD])
        s_s = sb("s_s", [P, 2, P])
        assert place["at"] <= nc.sbuf_usable_end, (place["at"], nc.sbuf_usable_end)
        end_of_sbuf = place["at"]
        dsh = sb_at("dsh", [P, 14, T], sc_at + 4 * 2 * D)
        place["at"] = sc_at
        qp = sb("qp", [P, 8, T])
        pr = sb("pr", [P, 8, 3, P])
        vatt = sb("vatt", [P, NT, BR])
        cat = sb("cat", [P, 3 * P])
        assert place["at"] <= end_of_sbuf
        place["at"] = arena
        xf = sb("xf", [P, KD, T])
        facc = sb("facc", [P, NT, D])
        y_hi = sb("y_hi", [P, D], F32R)
        sil = sb("sil", [P, 2, NT, P])
        hid = sb("hid", [P, 2, NT, P])
        sel = sb("sel", [P, NT, P])
        selt = sb("selt", [P, T], F32R)
        cmo = sb("cmo", [P, E_END])
        rt_s = sb("rt_s", [P, KD, NE])
        route = sb("route", [P, NT, R_END])
        idx = sb("idx", [P, NT, 8], U32)
        flag = sb("flag", [P, 2], I32)
        posm = sb("posm", [P, NT, NE])
        gsel = sb("gsel", [P, NT, NE])
        assert place["at"] <= sc_at
        gb = sb_at("gb", [P, 2, D], sc_at)
        y_lo = sb_at("y_lo", [P, D], sc_at + 4 * 2 * D, F32R)
        assert sc_at + 4 * 3 * D <= end_of_sbuf

        W = [nc.alloc_psum_tensor(f"W{i}", [P, 512], F32) for i in range(3)]
        Y = [nc.alloc_psum_tensor(f"Y{i}", [P, 512], F32) for i in range(4)]
        E = nc.alloc_psum_tensor("E", [P, 512], F32)
        spill = nc.dram_tensor("x_spill", (T, D), F32, kind="Internal").ap()

        ident = cst[:, C_ID:C_ID + P]
        blk = cst[:, C_BLK:C_BLK + P]
        rot = cst[:, C_ROT:C_ROT + P]
        strict = cst[:, C_SI:C_SI + P]

        def tiles(ap, n=2):
            return ap.rearrange("p (m t) -> p m t", m=n)

        def level_mask(v):
            return cst[:, C_LEV + v * P:C_LEV + (v + 1) * P].unsqueeze(1).to_broadcast([P, 4, P])

        fin1, fin2 = (xm[:, 4 * i:4 * i + 4, :].rearrange("p (m c) t -> p m (c t)", c=2) for i in range(2))

        state_decay = [small[:, 4 + 6 * p:6 + 6 * p] for p in range(2)]

        NB = (W[0], W[1], W[2], E)

        def par_col(l, name, i):
            return prm[:, l, PAR[name] + i:PAR[name] + i + 1]

        S = {}

        def sem(name):
            if name not in S:
                S[name] = ctx.enter_context(nc.semaphore(name))
            return S[name]

        raw_full = [sem(f"raw_full{i}") for i in range(3)]
        bank_free = [sem(f"bank_free{i}") for i in range(3)]
        hi_done, lo_pool, lo_dve = sem("hi_done"), sem("lo_pool"), sem("lo_dve")
        w_used = sem("w_used")

        def wait_jobs(eng, jobs):
            for b in range(3):
                eng.wait_ge(bank_free[b], (jobs - b + 2) // 3)

        def chained(eng, name):
            s, n = sem(name), [0]

            def link(ins):
                n[0] += 1
                ins.then_inc(s, 1)
                eng.wait_ge(s, n[0])
            return link

        block = ctx.enter_context(nc.Block())

        @block.sync
        def _(sp):
            def load(u, i, first, second):
                if u >= 3:
                    split, split_dve = u - 2 + 3 * i, dve_parts(u - 3) + 3 * i
                    if not isinstance(i, int):
                        split, split_dve = sp.to_reg(split), sp.to_reg(split_dve)
                    sp.wait_ge(hi_done, split)
                    sp.wait_ge(lo_pool, split)
                    if dve_takes(u - 3) or dve_takes(u):
                        sp.wait_ge(lo_dve, split_dve)
                sp.dma_start(*first).then_inc(raw_full[u % 3], 16)
                sp.dma_start(*second).then_inc(raw_full[u % 3], 16)

            def load_cols(u, i, w, col):
                d = raw[u % 3][:].rearrange("p (k c) -> p k c", k=KD)
                s = w[:, bass.ds(col, 256)].rearrange("(k p) c -> p k c", p=P)
                load(u, i, (d[:, 0:4, :], s[:, 0:4, :]), (d[:, 4:8, :], s[:, 4:8, :]))

            def load_gate_up(u, i, wg, wu, row, col):
                d = raw[u % 3][:].rearrange("p (k c) -> p k c", k=KD)
                g, v = (w[bass.ds(row, D), bass.ds(col, P)].rearrange("(k p) c -> p k c", p=P) for w in (wg, wu))
                load(u, i, (d[:, :, 0:P], g), (d[:, :, P:2 * P], v))

            def load_rows(u, i, w, row, n=2):
                d = raw[u % 3][:].rearrange("p (k c) -> p k c", k=n)
                s = w[bass.ds(row, n * P), :].rearrange("(k p) c -> p k c", p=P)
                h = n // 2
                load(u, i, (d[:, 0:h, :], s[:, 0:h, :]), (d[:, h:n, :], s[:, h:n, :]))

            def pair_loads(u, i, wg, wu, wd, row_in, row_hid):
                with sp.Fori(1, NPAIR) as j:
                    load_gate_up(u + 2, i + j - 1, wg, wu, row_in, 256 * j)
                    load_gate_up(u + 3, i + j - 1, wg, wu, row_in, 256 * j + P)
                    load_rows(u + 4, i + j - 1, wd, row_hid + 256 * j - 256)
                load_rows(u + 2, i + NPAIR - 1, wd, row_hid + 256 * (NPAIR - 1))

            for k in range(4):
                c = slice(2 * k, 2 * k + 2)
                sp.dma_start(xf[:, c, :], x_t[:, c, :]).then_inc(sem(f"x_full{k}"), 16)
            for l in range(L):
                for kind, where, n, _ in SEGMENTS:
                    u = layer_unit(l) + UNIT0[kind]
                    if kind == "out":
                        for q in range(n):
                            load_rows(u + q, 0, w_out[l], 256 * q)
                    elif kind.startswith("branch"):
                        for q in range(n):
                            load_rows(u + q, 0, w_branch[l, :, q * 512:(q + 1) * 512], where * BR, BT)
                    elif n % 3 == 0 and kind != "rkv":
                        with sp.Fori(0, n // 3) as i:
                            for s in range(3):
                                load_cols(u + s, i, w_in[l], where + 256 * s + 768 * i)
                    else:
                        for q in range(n):
                            load_cols(u + q, 0, w_in[l], where + 256 * q)
                            if u + q == 1:
                                sp.dma_start(prm[:], par).then_inc(sem("prm_full"), 16)
                                sp.dma_start(cst[:], const).then_inc(sem("cst_full"), 16)
                u = layer_unit(l) + MIX_UNITS
                if l == 0:
                    load_gate_up(u, 0, ffn_gate, ffn_up, 0, 0)
                    load_gate_up(u + 1, 0, ffn_gate, ffn_up, 0, P)
                    pair_loads(u, 0, ffn_gate, ffn_up, ffn_down, 0, 0)

            def expert_loads(u):
                def first_pair(v, i, row):
                    load_gate_up(v, i, moe_gate, moe_up, row, 0)
                    load_gate_up(v + 1, i, moe_gate, moe_up, row, P)

                first_pair(u, 0, 0)
                with sp.Fori(0, NE - 1) as e:
                    pair_loads(u, NPAIR * e, moe_gate, moe_up, moe_down, D * e, DFF * e)
                    first_pair(u + 3, NPAIR * e + NPAIR - 1, D * e + D)
                pair_loads(u, NPAIR * (NE - 1), moe_gate, moe_up, moe_down, D * (NE - 1), DFF * (NE - 1))

            expert_loads(MOE_U0)
            sp.wait_ge(sem("flag_ready"), 1)
            with sp.If(sp.value_load(flag[0:1, 0:1], min_val=0, max_val=1)):
                expert_loads(END_U)
            for t in range(NT):
                sp.wait_ge(sem("out_ready"), t + 1)
                sp.dma_start(out[t * P:(t + 1) * P, :], xtok[:, t, :]).then_inc(sem("out_stored"), 16)
            sp.wait_ge(sem("out_stored"), 16 * NT)

        @block.tensor
        def _(pe):
            def mm3(out_ap, lhs, rhs, start, stop):
                nc.tensor.matmul(out_ap, lhs[0], rhs[1], start=start, stop=False)
                nc.tensor.matmul(out_ap, lhs[1], rhs[0], start=False, stop=False)
                return nc.tensor.matmul(out_ap, lhs[0], rhs[0], start=False, stop=stop)

            def unit_ready(u, i=0):
                pe.wait_ge(lo_pool, u + 1 + 3 * i)
                if dve_takes(u):
                    pe.wait_ge(lo_dve, dve_parts(u) + 3 * i)

            def job_bank(j, i=0):
                if j >= 3:
                    pe.wait_ge(bank_free[j % 3], j // 3 + i)
                return tiles(W[j % 3][:])

            def x_part(m, k):
                if k % 2 == 0:
                    pe.wait_ge(sem("x_lo_ready"), 4 * m + k // 2 + 1)

            def proj_unit(u, j, fresh=None):
                i = 0
                unit_ready(u, i)
                bank = job_bank(j, i)
                wh, wl = (w[u % 3][:].rearrange("p (k c) -> p k c", k=KD) for w in (w_hi, w_lo))
                for m in range(2):
                    c = slice(m * P, (m + 1) * P)
                    for k in range(KD):
                        if fresh is not None and m == 0:
                            x_part(fresh, k)
                        last = mm3(bank[:, m, :], (wh[:, k, c], wl[:, k, c]), (x_hi[:, k, :], x_lo[:, k, :]),
                                   k == 0, k == KD - 1)
                last.then_inc(w_used, 1)

            def branch_unit(l, b, u, j):
                unit_ready(u)
                pe.wait_ge(sem("o_hi_ready"), 3 * l + b + 1)
                pe.wait_ge(sem("o_lo_ready"), 3 * l + b + 1)
                wh, wl = (w[u % 3][:].rearrange("p (k c) -> p k c", k=BT) for w in (w_hi, w_lo))
                for h in range(2):
                    bank = job_bank(j + h)
                    for m in range(2):
                        c = slice((2 * h + m) * P, (2 * h + m + 1) * P)
                        for k in range(BT):
                            last = mm3(bank[:, m, :], (wh[:, k, c], wl[:, k, c]), (o_hi[:, k, :], o_lo[:, k, :]),
                                       k == 0, k == BT - 1)
                    last.then_inc(w_used if h else sem("half_done"), 1)

            def out_unit(l, q, u):
                unit_ready(u)
                pe.wait_ge(sem("mlo_ready"), 4 * l + q + 1)
                wh, wl = (w[u % 3][:].rearrange("p (k c) -> p k c", k=2) for w in (w_hi, w_lo))
                for t in range(NT):
                    tk = slice(t * P, (t + 1) * P)
                    for k in range(2):
                        kk = 2 * q + k
                        for h in range(2):
                            c = slice(h * 512, (h + 1) * 512)
                            last = mm3(Y[2 * t + h][:], (x_hi[:, kk, tk], x_lo[:, kk, tk]), (wh[:, k, c], wl[:, k, c]),
                                       kk == 0, kk == KD - 1)
                    if t == 0 and q == 3:
                        last.then_inc(sem("sum_done"), 1)
                return last

            def units(l, kind, a, b):
                u0, j0 = layer_unit(l) + UNIT0[kind], l * MIX_JOBS + JOB0[kind]
                if kind == "out":
                    for q in range(a, b):
                        out_unit(l, q, u0 + q).then_inc(w_used, 1)
                elif kind.startswith("branch"):
                    for q in range(a, b):
                        branch_unit(l, int(kind[-1]), u0 + q, j0 + 2 * q)
                else:
                    for q in range(a, b):
                        proj_unit(u0 + q, j0 + q, 2 * l if kind == "lora" else None)

            def transpose(out_ap, in_ap):
                return nc.tensor.transpose(out_ap, in_ap, ident)

            def lora_map(l, p, s):
                for m in range(2):
                    c = slice((2 * p + m) * P, (2 * p + m + 1) * P)
                    last = nc.tensor.matmul(tiles(E[:])[:, m, :], w2_s[:, s, c], rkvl[:, 12, :], start=True, stop=True)
                last.then_inc(sem("lora_done"), 1)

            def lora_w(l, p):
                n = 2 * l + p
                if n == 0:
                    pe.wait_ge(sem("cst_full"), 16)
                if p == 0:
                    pe.wait_ge(sem("w2_full"), 16 * (l + 1))
                    pe.wait_ge(sem("lora_in_ready"), l + 1)
                if n:
                    pe.wait_ge(sem("tok_ready"), n)
                lora_map(l, p, 0)

            def lora_a(l, p):
                pe.wait_ge(sem("rate_w_ready"), 2 * l + p + 1)
                lora_map(l, p, 1)

            def ss(l, p):
                pe.wait_ge(sem("rates_ready"), 2 * l + p + 1)
                pe.wait_ge(sem("ksq_ready"), 2 * l + p + 1)
                nc.tensor.matmul(E[:], blk, td[:].rearrange("p m t -> p (m t)"), start=True, stop=True)\
                    .then_inc(sem("ss_done"), 1)

            def tok(l, p):
                n = 2 * l + p
                if n:
                    pe.wait_ge(sem("pass_done"), n)
                pe.wait_ge(sem("prep_ready"), n + 1)
                pe.wait_ge(sem("knorm_ready"), n + 1)
                nc.tensor.matmul(Y[3][:], blk, td[:].rearrange("p m t -> p (m t)"), start=True, stop=True)\
                    .then_inc(sem("bonus_done"), 1)
                pe.wait_ge(sem("decayed_ready"), n + 1)
                for c in range(NT):
                    for m in range(2):
                        transpose(tiles(E[:], 4)[:, 2 * c + m, :], rkvl[:, 8 + 2 * p + m, c * P:(c + 1) * P])
                for s, src in ((0, t6), (1, t3)):
                    for m in range(2):
                        last = transpose(tiles(Y[0][:], 4)[:, 2 * s + m, :], src[:, m, 0:P])
                last.then_inc(sem("tok_done"), 1)

            def scores(l, p):
                n = 2 * l + p
                pe.wait_ge(sem("decayed_ready"), n + 1)
                pe.wait_ge(sem("tok_ready"), n + 1)
                pe.wait_ge(sem("bonus_ready"), n + 1)
                for u in range(8):
                    c, h = divmod(u, 4)
                    bank = Y[(1 + u) % 4]
                    if u >= 4:
                        pe.wait_ge(sem("score_ready"), 8 * n + u - 3)
                    rhs = ar[:, h, c].rearrange("p s t -> p (s t)")
                    nc.tensor.matmul(bank[:, 0:256], t6[:, h // 2, c * P:(c + 1) * P], rhs, start=True, stop=True)
                    nc.tensor.matmul(bank[:, 256:512], t3[:, h // 2, c * P:(c + 1) * P], rhs, start=True, stop=True)\
                        .then_inc(sem("score_done"), 1)

            def invert(l, p):
                untranspose(2 * l + p, 0)

            def untranspose(n, v):
                for c in range(NT):
                    pe.wait_ge(sem("xt_ready"), 2 * LEVELS * n + 2 * v + c + 1)
                    for h in range(4):
                        last = transpose(tiles(Y[c][:], 4)[:, h, :], xt[:, 4 * c + h, :])
                    last.then_inc(sem("x_done"), 1)

            def level(l, p, v):
                n = 2 * l + p
                at = 2 * (LEVELS - 1) * n + 2 * (v - 1)
                for c in range(NT):
                    pe.wait_ge(sem("x_ready"), at + c + 1)
                    pe.wait_ge(sem("mt_ready"), at + c + 1)
                    for h in range(4):
                        last = nc.tensor.matmul(tiles(Y[c][:], 4)[:, h, :], mt[:, 4 * c + h, :], xm[:, 4 * c + h, :],
                                                start=True, stop=True)
                    last.then_inc(sem("mx_done"), 1)
                for c in range(NT):
                    pe.wait_ge(sem("mx_ready"), at + c + 1)
                    for h in range(4):
                        last = nc.tensor.matmul(tiles(Y[2 + c][:], 4)[:, h, :], mt[:, 4 * c + h, :], xt[:, 4 * c + h, :],
                                                start=True, stop=True)
                    last.then_inc(sem("dxt_done"), 1)
                if v < LEVELS - 1:
                    untranspose(n, v)

            def chain(l, p, c):
                n = 2 * l + p
                heads = [(h, h // 2, slice(h * HD, (h + 1) * HD), slice((h % 2) * HD, (h % 2 + 1) * HD)) for h in range(4)]
                if c == 0:
                    pe.wait_ge(sem("xt_ready"), 2 * LEVELS * (n + 1))
                else:
                    pe.wait_ge(sem("s_ready"), n + 1)
                for h, m, hc, half in heads:
                    last = nc.tensor.matmul(Y[0][:, hc], sc[:, 4 * c + h, 2, :], vtok[:, c, hc], start=True, stop=c == 0)
                    if c:
                        last = nc.tensor.matmul(Y[0][:, hc], ar[:, h, 1, 0, :], s_s[:, m, half], start=False, stop=True)
                last.then_inc(sem("g_done"), 1)
                pe.wait_ge(sem("g_ready"), 2 * n + c + 1)
                for h, m, hc, half in heads:
                    last = nc.tensor.matmul(Y[1][:, hc], xt[:, 4 * c + h, :], g_s[:, h, :], start=True, stop=True)
                last.then_inc(sem("u_done"), 1)
                pe.wait_ge(sem("u_ready"), 2 * n + c + 1)
                if c == 0:
                    for m in range(2):
                        mc = slice(m * P, (m + 1) * P)
                        nc.tensor.matmul(Y[3][:, mc], bktok[:, 0, mc], u_s[:, 2 * m:2 * m + 2, :].rearrange("p a b -> p (a b)"),
                                         start=True, stop=False)
                        last = nc.tensor.matmul(Y[3][:, mc], bktok[:, 1, mc], vtok[:, 0, mc], start=False, stop=True)
                    last.then_inc(sem("s_done"), 1)
                    pe.wait_ge(sem("knorm_ready"), 2 * l + 2)
                    if p:
                        pe.wait_ge(sem("rope_ready"), 4 * l + 4)
                for h, m, hc, half in heads:
                    o = tiles(E[:])[half, m, c * P:(c + 1) * P]
                    nc.tensor.matmul(o, vtok[:, c, hc], sc[:, 4 * c + h, 3, :], start=True, stop=False)
                    if c:
                        nc.tensor.matmul(o, s_s[:, m, half], ar[:, h, 1, 1, :], start=False, stop=False)
                    last = nc.tensor.matmul(o, u_s[:, h, :], sc[:, 4 * c + h, 1, :], start=False, stop=True)
                last.then_inc(sem("y_done"), 1)

            def finish(l, p):
                n = 2 * l + p
                pe.wait_ge(sem("yrow_ready"), n + 1)
                nc.tensor.matmul(Y[0][:], blk, fin1.rearrange("p m t -> p (m t)"), start=True, stop=True)\
                    .then_inc(sem("mean_done"), 1)
                pe.wait_ge(sem("gw2_full"), 16 * (l + 1))
                for m in range(2):
                    last = nc.tensor.matmul(tiles(Y[2][:])[:, m, :], gw2_s[:, (2 * p + m) * P:(2 * p + m + 1) * P],
                                            rkvl[:, 13, :], start=True, stop=True)
                last.then_inc(sem("gatemul_done"), 1)
                pe.wait_ge(sem("ysq_ready"), n + 1)
                nc.tensor.matmul(Y[1][:], blk, fin2.rearrange("p m t -> p (m t)"), start=True, stop=True)\
                    .then_inc(sem("var_done"), 1)

            def rope(l, s):
                wait_jobs(pe, l * MIX_JOBS + JOB0["qkv"] + s + 1)
                if s:
                    pe.wait_ge(sem("rope_ready"), 4 * l + s)
                nc.tensor.matmul(E[:], rot, share[:, 2 * s:2 * s + 2, :].rearrange("p m t -> p (m t)"),
                                 start=True, stop=True).then_inc(sem("rot_done"), 1)

            def heads(l):
                pe.wait_ge(sem("pass_done"), 2 * l + 2)
                for c in range(NT):
                    for m in range(BT):
                        last = transpose(tiles(Y[c][:], 4)[:, m, :], share[:, 8 + m, c * P:(c + 1) * P])
                last.then_inc(sem("vt_done"), 1)

            def att_scores(l):
                pe.wait_ge(sem("qp_zero"), l + 1)
                pe.wait_ge(sem("qp_ready"), l + 1)
                for h in range(8):
                    bank = tiles(Y[(2 + h) % 4][:], 4)
                    if h == 2:
                        pe.wait_ge(sem("vatt_ready"), l + 1)
                    if h >= 4:
                        pe.wait_ge(sem("att_sc_ready"), 8 * l + h - 3)
                    nc.tensor.matmul(bank[:, 0, :], qp[:, h, 0:P], share[:, 4 + h // 2, 0:P], start=True, stop=True)
                    nc.tensor.matmul(bank[:, 1:3, :].rearrange("p a b -> p (a b)"), qp[:, h, P:T], share[:, 4 + h // 2, :],
                                     start=True, stop=True).then_inc(sem("att_sc_done"), 1)

            def probs_t(l):
                pe.wait_ge(sem("prob_ready"), 2 * l + 2)
                for h in range(8):
                    if h >= 3:
                        pe.wait_ge(sem("pt_ready"), 8 * l + h - 2)
                    for s in range(3):
                        last = transpose(tiles(Y[h % 3][:], 4)[:, s, :], pr[:, h, s, :])
                    last.then_inc(sem("pt_done"), 1)

            def att_out(l):
                for h in range(8):
                    pe.wait_ge(sem("pt_ready"), 8 * l + h + 1)
                    o = tiles((E if h < 4 else Y[3])[:])[(h % 2) * HD:(h % 2 + 1) * HD, (h // 2) % 2, :]
                    hc = slice(h * HD, (h + 1) * HD)
                    nc.tensor.matmul(o, vatt[:, 0, hc], pr[:, h, 0:2, :].rearrange("p a b -> p (a b)"), start=True, stop=False)
                    last = nc.tensor.matmul(o[:, P:T], vatt[:, 1, hc], pr[:, h, 2, :], start=False, stop=True)
                    if h % 4 == 3:
                        last.then_inc(sem("att_done"), 1)

            def norm_transposes(m):
                for t in range(NT):
                    pe.wait_ge(sem("xn_ready"), NT * m + t + 1)
                    for k in range(KD):
                        last = transpose(tiles(NB[k // 2][:])[:, k % 2, t * P:(t + 1) * P], xtok[:, t, k * P:(k + 1) * P])
                        if k % 2 and t == NT - 1:
                            last.then_inc(sem("xnt_done"), 1)

            def gate_up(u, i, f, nt, fresh=None):
                unit_ready(u, i)
                odd, f = f
                if not isinstance(f, int) or f >= 2:
                    pe.wait_ge(sem("hid_ready"), f - 1)
                bank = tiles(W[odd][:])
                wh, wl = (w[u % 3][:].rearrange("p (k c) -> p k c", k=KD) for w in (w_hi, w_lo))
                for t in range(nt):
                    tk = slice(t * P, (t + 1) * P)
                    for k in range(KD):
                        if fresh is not None and t == 0:
                            x_part(fresh, k)
                        last = mm3(bank[:, t, :], (x_hi[:, k, tk], x_lo[:, k, tk]), (wh[:, k, :], wl[:, k, :]),
                                   k == 0, k == KD - 1)
                last.then_inc(w_used, 1)

            def hid_transposes(g, nt):
                pe.wait_ge(sem("hid_ready"), 2 * g + 2)
                for s in range(2):
                    for t in range(nt):
                        last = transpose(tiles(W[2][:], 4)[:, 2 * s + t, :], hid[:, s, t, :])
                last.then_inc(sem("ht_done"), 1)

            def down(u, i, g, nt, first, final):
                unit_ready(u, i)
                pe.wait_ge(sem("hlo_ready"), g + 1)
                wh, wl = (w[u % 3][:].rearrange("p (k c) -> p k c", k=2) for w in (w_hi, w_lo))
                for t in range(nt):
                    tk = slice(t * P, (t + 1) * P)
                    for s in range(2):
                        for h in range(2):
                            c = slice(h * 512, (h + 1) * 512)
                            last = mm3(Y[2 * t + h][:], (o_hi[:, s, tk], o_lo[:, s, tk]), (wh[:, s, c], wl[:, s, c]),
                                       first and s == 0, final and s == 1)
                    if final and t == 0 and nt == NT:
                        last.then_inc(sem("sum_done"), 1)
                last.then_inc(w_used, 1)

            def first_pair(u, i, g, nt, fresh=None):
                gate_up(u, i, (0, 2 * g), nt, fresh)
                gate_up(u + 1, i, (1, 2 * g + 1), nt)

            def pair(u, i, g, nt, j, before=None):
                gate_up(u + 2, i + j - 1, (0, 2 * (g + j)), nt)
                if before:
                    before()
                hid_transposes(g + j - 1, nt)
                gate_up(u + 3, i + j - 1, (1, 2 * (g + j) + 1), nt)
                down(u + 4, i + j - 1, g + j - 1, nt, isinstance(j, int) and j == 1, False)

            def middle_pairs(u, i, g, nt, n=None, follow=False):
                if n is None:
                    pair(u, i, g, nt, 1)
                    with pe.Fori(2, NPAIR) as j:
                        pair(u, i, g, nt, j)
                    return
                def transpose_sel():
                    pe.wait_ge(sem("facc_ready"), n + 1)
                    for t in range(NT):
                        last = transpose(E[:, t * P:(t + 1) * P], sel[:, t, :])
                    last.then_inc(sem("selt_done"), 1)

                pair(u, i, g, nt, 1, transpose_sel)
                with pe.Fori(2, NPAIR // 2) as j:
                    pair(u, i, g, nt, j)
                if follow:
                    pe.wait_ge(sem("sel_ready"), n + 2)
                    select_rows(0)
                with pe.Fori(NPAIR // 2, NPAIR - 1) as j:
                    pair(u, i, g, nt, j)
                if follow:
                    select_rows(1)
                pair(u, i, g, nt, NPAIR - 1)

            def last_down(u, i, g, nt):
                hid_transposes(g + NPAIR - 1, nt)
                down(u + 2, i + NPAIR - 1, g + NPAIR - 1, nt, False, True)

            def select_rows(half):
                for k in range(4):
                    kk = slice((4 * half + k) * P, (4 * half + k + 1) * P)
                    for t in range(NT):
                        last = nc.tensor.matmul(tiles(Y[2 + half][:], 4)[:, k, :], xtok[:, t, kk], sel[:, t, :],
                                                start=t == 0, stop=t == NT - 1)
                last.then_inc(sem("rows_done"), 1)

            def experts(u, g, q):
                def expert(e, follow):
                    n = q + e
                    middle_pairs(u, NPAIR * e, g + NPAIR * e, 1, n, follow)
                    last_down(u, NPAIR * e, g + NPAIR * e, 1)
                    if follow:
                        pe.wait_ge(sem("rows_ready"), n + 2)
                        first_pair(u + FFN_UNITS, NPAIR * e, g + NPAIR * e + NPAIR, 1)
                    pe.wait_ge(sem("selt_ready"), n + 1)
                    pe.wait_ge(sem("yrows_ready"), n + 1)
                    for t, banks in ((0, (Y[2], Y[3])), (1, (E, W[2]))):
                        for h in range(2):
                            to_token, c = selt[:, t * P:(t + 1) * P], slice(h * 512, (h + 1) * 512)
                            nc.tensor.matmul(banks[h][:], to_token, y_lo[:, c], start=True, stop=False)
                            last = nc.tensor.matmul(banks[h][:], to_token, y_hi[:, c], start=False, stop=True)
                        last.then_inc(sem("comb_done"), 1)

                pe.wait_ge(sem("sel_ready"), q + 1)
                select_rows(0)
                select_rows(1)
                pe.wait_ge(sem("rows_ready"), q + 1)
                first_pair(u, 0, g, 1)
                with pe.Fori(0, NE - 1) as e:
                    expert(e, True)
                expert(NE - 1, False)

            handlers = {"units": units, "lora_w": lora_w, "lora_a": lora_a, "ss": ss, "tok": tok, "scores": scores, "invert": invert,
                        "level": level, "chain": chain, "finish": finish, "rope": rope, "heads": heads, "att_scores": att_scores,
                        "probs_t": probs_t, "att_out": att_out}
            for l in range(L):
                for name, *args in TIMELINE:
                    if name in handlers:
                        handlers[name](l, *args)
                norm_transposes(2 * l)
                if l == 0:
                    first_pair(MIX_UNITS, 0, 0, NT, 1)
                    middle_pairs(MIX_UNITS, 0, 0, NT)
                    last_down(MIX_UNITS, 0, 0, NT)
                    norm_transposes(1)
            pe.wait_ge(sem("cmo_full"), 32)
            for k in range(KD):
                if k % 2 == 0:
                    pe.wait_ge(sem("xf_ready"), 9 + k // 2)
                last = nc.tensor.matmul(Y[0][0:NE, 0:T], rt_s[:, k, :], xf[:, k, :], start=k == 0, stop=k == KD - 1)
            last.then_inc(sem("router_done"), 1)
            pe.wait_ge(sem("router_ready"), 1)
            for t in range(NT):
                last = nc.tensor.transpose(Y[1][:, t * NE:(t + 1) * NE], facc[0:NE, 0, t * P:(t + 1) * P], ident[0:NE, 0:NE])
            last.then_inc(sem("logits_done"), 1)
            pe.wait_ge(sem("mask_ready"), 1)
            ones, m0, m1 = cmo[:, E_ONE:E_ONE + P], route[:, 0, R_MASK:R_MASK + NE], route[:, 1, R_MASK:R_MASK + NE]
            nc.tensor.matmul(Y[0][:, 32:40], strict, m0, start=True, stop=True)
            nc.tensor.matmul(Y[0][:, 40:48], ones, m0, start=True, stop=False)
            nc.tensor.matmul(Y[0][:, 40:48], strict, m1, start=False, stop=True)
            nc.tensor.matmul(Y[0][:, 48:56], ones, m0, start=True, stop=False)
            nc.tensor.matmul(Y[0][:, 48:56], ones, m1, start=False, stop=True).then_inc(sem("place_done"), 1)
            pe.wait_ge(sem("xtok_ready"), 3)
            experts(MOE_U0, NPAIR, 0)
            with pe.If(pe.value_load(flag[0:1, 0:1], min_val=0, max_val=1)):
                experts(END_U, NPAIR * (NE + 1), NE)

        @block.scalar
        def _(act):
            link = chained(act, "act_chain")
            A = nc.scalar.activation

            def split_hi(u, i=0):
                act.wait_ge(raw_full[u % 3], UD * (u // 3 + 1 + i))
                if u >= 3:
                    act.wait_ge(w_used, u - 2 + 3 * i)
                A(w_hi[u % 3][:], raw[u % 3][:], ACT.Copy).then_inc(hi_done, 1)

            def out_of_bank(kind, q, u, j):
                act.wait_ge(w_used, u + 1)
                dst = {"lora": rkvl[:, 12:14, :], "rkv": rkvl[:, 2 * q:2 * q + 2, :], "conv": share[:, 2 * q:2 * q + 2, :],
                       "qkv": share[:, 2 * q:2 * q + 2, :]}.get(kind, sgate[:, (2 * q) % KD:(2 * q) % KD + 2, :])
                A(dst, tiles(W[j % 3][:]), ACT.Sigmoid if kind.startswith("gate") else ACT.Copy)\
                    .then_inc(bank_free[j % 3], 1)

            def units(l, kind, a, b):
                u0, j0 = layer_unit(l) + UNIT0[kind], l * MIX_JOBS + JOB0[kind]
                if kind == "qkv":
                    act.wait_ge(sem("o_hi_ready"), 3 * l + 1)
                    act.wait_ge(sem("o_lo_ready"), 3 * l + 1)
                if kind in ("gate1", "gate2"):
                    wait_jobs(act, l * MIX_JOBS + JOB0[f"branch{int(kind[-1]) - 1}"] + 4)
                if kind == "out" or kind.startswith("branch"):
                    for q in range(a, b):
                        split_hi(u0 + q + 2)
                    return
                for q in range(a, b):
                    if kind != "lora" or l == 0:
                        split_hi(u0 + q + 2)
                    out_of_bank(kind, q, u0 + q, j0 + q)

            def spill_stream(l):
                if l:
                    act.wait_ge(sem("xtok_ready"), 2)
                    act.dma_start(spill.rearrange("(n p) d -> p n d", p=P), xtok[:]).then_inc(sem("spilled"), 16)

            def lora_in(l):
                act.wait_ge(sem("lora_shifted"), l + 1)
                link(A(rkvl[0:64, 12, :], rkvl[0:64, 12, :], ACT.Tanh))
                A(rkvl[:, 13, :], rkvl[:, 13, :], ACT.Sigmoid).then_inc(sem("lora_in_ready"), 1)

            def rate_w(l, p):
                n = 2 * l + p
                act.wait_ge(sem("lora_done"), 2 * n + 1)
                if n == 0:
                    act.wait_ge(sem("prm_full"), 16)
                if n:
                    act.wait_ge(sem("decayed_ready"), n)
                for m in range(2):
                    last = A(t1[:, m, :], tiles(E[:])[:, m, :], ACT.Sigmoid, bias=par_col(l, "w0", 2 * p + m))
                last.then_inc(sem("rate_w_ready"), 1)

            def rate_a(l, p):
                act.wait_ge(sem("lora_done"), 2 * (2 * l + p) + 2)
                for m in range(2):
                    last = A(t4[:, m, :], tiles(E[:])[:, m, :], ACT.Sigmoid, bias=par_col(l, "a0", 2 * p + m))
                last.then_inc(sem("rates_ready"), 1)

            def exps(l, p):
                n = 2 * l + p
                act.wait_ge(sem("decay_ready"), n + 1)
                A(t1[:], t1[:], ACT.Exp, scale=-KAPPA)
                A(t3[:], t2[:], ACT.Exp, scale=KAPPA).then_inc(sem("act_t3"), 1)
                act.wait_ge(sem("act_t3"), n + 1)
                A(t2[:], t2[:], ACT.Exp, scale=-KAPPA)
                A(state_decay[p], state_decay[p], ACT.Exp, scale=-KAPPA).then_inc(sem("exp_ready"), 1)

            def knorm(l, p):
                act.wait_ge(sem("ss_done"), 2 * l + p + 1)
                A(td[:].rearrange("p m t -> p (m t)"), E[:], ACT.Sqrt).then_inc(sem("knorm_ready"), 1)

            def tok(l, p):
                act.wait_ge(sem("tok_done"), 2 * l + p + 1)
                A(vtok[:].rearrange("p c v -> p (c v)"), E[:], ACT.Copy)
                A(bktok[:].rearrange("p c v -> p (c v)"), Y[0][:], ACT.Copy).then_inc(sem("tok_ready"), 1)

            def copy_x(n, v):
                at = 2 * (LEVELS - 1) * n + 2 * v
                for c in range(NT):
                    act.wait_ge(sem("x_done"), at + c + 1)
                    A(xm[:, 4 * c:4 * c + 4, :], tiles(Y[c][:], 4), ACT.Copy).then_inc(sem("x_ready"), 1)

            def invert(l, p):
                copy_x(2 * l + p, 0)

            def level(l, p, v):
                n = 2 * l + p
                at = 2 * (LEVELS - 1) * n + 2 * (v - 1)
                for c in range(NT):
                    act.wait_ge(sem("mx_done"), at + c + 1)
                    A(mt[:, 4 * c:4 * c + 4, :], tiles(Y[c][:], 4), ACT.Copy).then_inc(sem("mx_ready"), 1)
                if v < LEVELS - 1:
                    copy_x(n, v)

            def finish(l, p):
                n = 2 * l + p
                act.wait_ge(sem("var_done"), n + 1)
                A(fin2.rearrange("p m t -> p (m t)"), Y[1][:], ACT.Sqrt, bias=small[:, 8:9], scale=1.0 / HD)\
                    .then_inc(sem("gn_sd_ready"), 1)

            def heads(l):
                act.wait_ge(sem("pass_done"), 2 * l + 2)
                act.dma_start(cat[:], const_att).then_inc(sem("cat_full"), 16)
                if l == 0:
                    act.dma_start(w2_s[:], w2[1]).then_inc(sem("w2_full"), 16)
                    act.dma_start(gw2_s[:], gate_w2[1]).then_inc(sem("gw2_full"), 16)
                qpv = qp[:].rearrange("p (m h) t -> p m h t", h=2)
                for h in range(2):
                    rows = slice(h * HD, (h + 1) * HD)
                    last = A(qpv[rows, :, h, :], share[rows, 0:BT, :], ACT.Copy)
                last.then_inc(sem("qp_ready"), 1)
                act.wait_ge(sem("vt_done"), l + 1)
                for c in range(NT):
                    last = A(vatt[:, c, :], Y[c][:], ACT.Copy)
                last.then_inc(sem("vatt_ready"), 1)

            def softmax(l, half):
                act.wait_ge(sem("max_ready"), l + 1)
                for h in range(4 * half, 4 * half + 4):
                    A(pr[:, h, 0, :], pr[:, h, 0, :], ACT.Exp, bias=small[:, 16 + 2 * h:17 + 2 * h],
                      accum_out=small[:, 32 + 2 * h:33 + 2 * h])
                    last = A(pr[:, h, 1:3, :], pr[:, h, 1:3, :], ACT.Exp, bias=small[:, 17 + 2 * h:18 + 2 * h],
                             accum_out=small[:, 33 + 2 * h:34 + 2 * h])
                last.then_inc(sem("e_ready"), 1)

            def probs_t(l):
                for h in range(8):
                    act.wait_ge(sem("pt_done"), 8 * l + h + 1)
                    A(pr[:, h, :, :].rearrange("p s q -> p (s q)"), Y[h % 3][:, 0:3 * P], ACT.Copy).then_inc(sem("pt_ready"), 1)

            def att_out(l):
                act.wait_ge(w_used, layer_unit(l) + UNIT0["branch1"] + 2)
                act.wait_ge(sem("att_done"), 2 * l + 1)
                A(o_hi[:, 0:2, :], tiles(E[:]), ACT.Copy).then_inc(sem("o_half_ready"), 1)
                act.wait_ge(sem("att_done"), 2 * l + 2)
                A(o_hi[:, 2:4, :], tiles(Y[3][:]), ACT.Copy).then_inc(sem("o_hi_ready"), 1)
                act.wait_ge(sem("o_lo_ready"), 3 * l + 3)
                act.dma_start(gb[:], ln_gb[2 * l]).then_inc(sem("gb_full"), 16)

            def osplit(l, b):
                src = share if b == 0 else rkvl
                if b == 0:
                    act.wait_ge(sem("conv_ready"), 2 * l + 2)
                else:
                    act.wait_ge(sem("pass_done"), 2 * l + 2)
                act.wait_ge(w_used, layer_unit(l) + (UNIT0["branch0"] + 2 if b else 0))
                A(o_hi[:], src[:, 0:BT, :], ACT.Copy).then_inc(sem("o_hi_ready"), 1)

            def msplit(l, half):
                for q in (2 * half, 2 * half + 1):
                    act.wait_ge(sem("gated"), 8 * l + 4 + q + 1)
                    c = slice(2 * q, 2 * q + 2)
                    A(x_hi[:, c, :], merged[:, c, :], ACT.Copy).then_inc(sem("mhi_ready"), 1)
                if half == 0:
                    return
                act.wait_ge(sem("mlo_ready"), 4 * l + 4)
                act.wait_ge(sem("mhi_ready"), 4 * l + 4)
                if l:
                    act.wait_ge(sem("spilled"), 16)
                act.dma_start(xtok[:], (spill if l else x).rearrange("(n p) d -> p n d", p=P)).then_inc(sem("xres_full"), 16)
                if l:
                    act.dma_start(cmo[:], const_moe).then_inc(sem("cmo_full"), 16)
                    act.dma_start(rt_s[:], router).then_inc(sem("cmo_full"), 16)

            def ln_scale(m):
                for t in range(NT):
                    act.wait_ge(sem("ln_var_ready"), NT * m + t + 1)
                    A(small[:, 50 + t:51 + t], small[:, 81 + 2 * t:82 + 2 * t], ACT.Sqrt, bias=small[:, 9:10])\
                        .then_inc(sem("ln_sd_ready"), 1)

            def ln_split(m):
                for k in range(4):
                    act.wait_ge(sem("xf_ready"), 4 * m + k + 1)
                    A(x_hi[:, 2 * k:2 * k + 2, :], xf[:, 2 * k:2 * k + 2, :], ACT.Copy).then_inc(sem("x_hi_ready"), 1)

            def silu(f, nt, used):
                odd, f = f
                act.wait_ge(w_used, used)
                if not isinstance(f, int) or f >= 2:
                    act.wait_ge(sem("hid_ready"), f - 1)
                A(sil[:, odd, 0:nt, :], tiles(W[odd][:])[:, 0:nt, 0:P], ACT.Silu).then_inc(sem("silu_ready"), 1)

            def hid_hi(g, nt, used):
                act.wait_ge(sem("ht_done"), g + 1)
                act.wait_ge(w_used, used)
                A(o_hi[:, 0:2, 0:nt * P], tiles(W[2][:])[:, :, 0:nt * P], ACT.Copy).then_inc(sem("hhi_ready"), 1)

            def first_pair(u, i, g, nt, ahead=False):
                if not ahead:
                    split_hi(u + 2, i)
                silu((0, 2 * g), nt, u + 1 + 3 * i)
                split_hi(u + 3, i)
                silu((1, 2 * g + 1), nt, u + 2 + 3 * i)

            def pair(u, i, g, nt, j, ahead):
                v, w = u + 3 * (i + j - 1), i + j - 1
                split_hi(u + 4, w)
                silu((0, 2 * (g + j)), nt, v + 3)
                hid_hi(g + j - 1, nt, v + 2)
                split_hi(u + 5, w)
                silu((1, 2 * (g + j) + 1), nt, v + 4)
                if ahead:
                    split_hi(u + 6, w)

            def middle_pairs(u, i, g, nt, ahead=True, n=None):
                start = 1
                if n is not None:
                    pair(u, i, g, nt, 1, True)
                    act.wait_ge(sem("selt_done"), n + 1)
                    A(selt[:], E[:, 0:T], ACT.Copy).then_inc(sem("selt_ready"), 1)
                    start = 2
                with act.Fori(start, NPAIR if ahead else NPAIR - 1) as j:
                    pair(u, i, g, nt, j, True)
                if not ahead:
                    pair(u, i, g, nt, NPAIR - 1, False)

            def rows_hi(n):
                act.wait_ge(sem("rows_done"), 2 * n + 2)
                for s in range(2):
                    last = A(x_hi[:, 4 * s:4 * s + 4, 0:P], tiles(Y[2 + s][:], 4), ACT.Copy)
                last.then_inc(sem("rows_hi"), 1)

            def last_down(u, i, g, nt, ahead=True, n=None):
                hid_hi(g + NPAIR - 1, nt, u + 2 + 3 * (i + NPAIR - 1))
                if ahead and n is not None:
                    rows_hi(n + 1)
                if ahead:
                    split_hi(u + 4, i + NPAIR - 1)

            def experts(u, g, q, cold):
                def expert(e, follow):
                    n = q + e
                    middle_pairs(u, NPAIR * e, g + NPAIR * e, 1, follow, n)
                    last_down(u, NPAIR * e, g + NPAIR * e, 1, follow, n)
                    act.wait_ge(w_used, u + FFN_UNITS * (e + 1))
                    for h in range(2):
                        last = A(y_hi[:, h * 512:(h + 1) * 512], Y[h][:], ACT.Copy)
                    last.then_inc(sem("yrows_hi"), 1)
                    if follow:
                        first_pair(u + FFN_UNITS, NPAIR * e, g + NPAIR * e + NPAIR, 1)

                if cold:
                    split_hi(u)
                    split_hi(u + 1)
                rows_hi(q)
                first_pair(u, 0, g, 1)
                with act.Fori(0, NE - 1) as e:
                    expert(e, True)
                expert(NE - 1, False)

            act.wait_ge(sem("eps_ready"), 1)
            for k in range(4):
                c = slice(2 * k, 2 * k + 2)
                act.wait_ge(sem(f"x_full{k}"), 16)
                A(x_hi[:, c, :], xf[:, c, :], ACT.Copy).then_inc(sem("x_hi_ready"), 1)
            act.dma_start(w2_s[:], w2[0]).then_inc(sem("w2_full"), 16)
            act.dma_start(gw2_s[:], gate_w2[0]).then_inc(sem("gw2_full"), 16)
            split_hi(0)
            split_hi(1)
            handlers = {"units": units, "lora_in": lora_in, "rate_w": rate_w, "rate_a": rate_a, "exps": exps,
                        "knorm": knorm, "tok": tok, "invert": invert, "level": level, "finish": finish,
                        "heads": heads, "softmax": softmax, "probs_t": probs_t, "att_out": att_out,
                        "osplit": osplit, "msplit": msplit, "spill": spill_stream}
            for l in range(L):
                for name, *args in TIMELINE:
                    if name in handlers:
                        handlers[name](l, *args)
                ln_scale(2 * l)
                if l == 0:
                    split_hi(MIX_UNITS + 2)
                    ln_split(0)
                    first_pair(MIX_UNITS, 0, 0, NT, True)
                    middle_pairs(MIX_UNITS, 0, 0, NT)
                    act.wait_ge(sem("xtok_ready"), 1)
                    act.dma_start(gb[:], ln_gb[1]).then_inc(sem("gb_full"), 16)
                    last_down(MIX_UNITS, 0, 0, NT)
                    ln_scale(1)
                    split_hi(layer_unit(1) + 2)
                    ln_split(1)
            act.wait_ge(sem("router_done"), 1)
            A(facc[0:NE, 0, 0:T], Y[0][0:NE, 0:T], ACT.Copy).then_inc(sem("router_ready"), 1)
            act.wait_ge(sem("top_ready"), 1)
            A(route[:, :, R_EXP:R_EXP + 1], route[:, :, R_EXP:R_EXP + 1], ACT.Exp).then_inc(sem("gexp_ready"), 1)
            act.wait_ge(sem("xtok_ready"), 3)
            act.dma_start(gb[:], ln_gb[3]).then_inc(sem("gb_full"), 16)
            experts(MOE_U0, NPAIR, 0, False)
            act.wait_ge(sem("flag_ready"), 1)
            with act.If(act.value_load(flag[0:1, 0:1], min_val=0, max_val=1)):
                experts(END_U, NPAIR * (NE + 1), NE, True)
            ln_scale(3)

        @block.gpsimd
        def _(pool):
            link = chained(pool, "pool_chain")

            def split_lo(u, i=0):
                pool.wait_ge(hi_done, u + 1 + 3 * i)
                c = slice(UN - POOL_PART if dve_takes(u) else 0, UN)
                nc.gpsimd.tensor_tensor(w_lo[u % 3][:, c], raw[u % 3][:, c], w_hi[u % 3][:, c].bitcast(F32), ALU.subtract)\
                    .then_inc(lo_pool, 1)

            def units(l, kind, a, b):
                for q in range(a, b):
                    split_lo(layer_unit(l) + UNIT0[kind] + q + 2)

            def scale_xtok(m, t):
                pool.wait_ge(sem("gb_full"), 16 * (m + 1))
                pool.wait_ge(sem("xnt_done"), 4 * (m + 1))
                link(nc.gpsimd.tensor_tensor(xtok[:, t, :], xtok[:, t, :], gb[:, 0, :], ALU.mult))
                last = nc.gpsimd.tensor_tensor(xtok[:, t, :], xtok[:, t, :], gb[:, 1, :], ALU.add)
                if t == NT - 1:
                    last.then_inc(sem("xtok_ready"), 1)
                else:
                    link(last)

            def ffn(u, i, ahead=True):
                with pool.Fori(1, NPAIR if ahead else NPAIR - 1) as j:
                    for s in range(3):
                        split_lo(u + 4 + s, i + j - 1)
                if ahead:
                    split_lo(u + 4, i + NPAIR - 1)
                else:
                    split_lo(u + 4, NPAIR - 2 + i)
                    split_lo(u + 5, NPAIR - 2 + i)

            def experts(u, cold):
                for s in range(0 if cold else 2, 4):
                    split_lo(u + s)
                with pool.Fori(0, NE - 1) as e:
                    ffn(u, NPAIR * e)
                    split_lo(u + FFN_UNITS + 2, NPAIR * e)
                    split_lo(u + FFN_UNITS + 3, NPAIR * e)
                ffn(u, NPAIR * (NE - 1), False)

            nc.gpsimd.memset(small[:], 0.0).then_inc(sem("pool_zero"), 1)
            pool.wait_ge(sem("pool_zero"), 1)
            link(nc.gpsimd.memset(small[:, 8:9], GN_EPS))
            nc.gpsimd.memset(small[:, 9:10], LN_EPS).then_inc(sem("eps_ready"), 1)
            split_lo(0)
            split_lo(1)
            nc.gpsimd.memset(ar[:], 0.0).then_inc(sem("ar_zero"), 1)
            for l in range(L):
                for name, *args in TIMELINE:
                    if name == "units":
                        units(l, *args)
                        if l and args[0] == "lora":
                            scale_xtok(1, 0)
                        if l and args[:2] == ["rkv", 0]:
                            scale_xtok(1, 1)
                if l == 0:
                    split_lo(MIX_UNITS + 2)
                    scale_xtok(0, 0)
                    split_lo(MIX_UNITS + 3)
                    scale_xtok(0, 1)
                    ffn(MIX_UNITS, 0)
                else:
                    scale_xtok(2, 0)
                    scale_xtok(2, 1)
            experts(MOE_U0, False)
            pool.wait_ge(sem("flag_ready"), 1)
            with pool.If(pool.value_load(flag[0:1, 0:1], min_val=0, max_val=1)):
                experts(END_U, True)

        @block.vector
        def _(dve):
            link = chained(dve, "dve_chain")
            V = nc.vector

            def mark(ins, name, value):
                ins.then_inc(sem(name), 1)
                dve.wait_ge(sem(name), value)

            def split_lo(u, i=0):
                dve.wait_ge(hi_done, u + 1 + 3 * i)
                c = slice(0, UN - POOL_PART)
                V.tensor_tensor(w_lo[u % 3][:, c], raw[u % 3][:, c], w_hi[u % 3][:, c].bitcast(F32), ALU.subtract)\
                    .then_inc(lo_dve, 1)

            def units(l, kind, a, b):
                u0, j0 = layer_unit(l) + UNIT0[kind], l * MIX_JOBS + JOB0[kind]
                for q in range(a, b):
                    if dve_takes(u0 + q + 2):
                        split_lo(u0 + q + 2)
                    if kind.startswith("branch"):
                        gate_unit(l, int(kind[-1]), q, u0 + q, j0 + 2 * q)

            def gate_unit(l, b, q, u, j):
                if q == 0:
                    wait_jobs(dve, l * MIX_JOBS + JOB0[f"branch{b}"])
                    if b == 0 and l:
                        dve.wait_ge(sem("spilled"), 16)
                for h in range(2):
                    if h == 0:
                        dve.wait_ge(sem("half_done"), 2 * (3 * l + b) + q + 1)
                    else:
                        dve.wait_ge(w_used, u + 1)
                    ft = slice(4 * q + 2 * h, 4 * q + 2 * h + 2)
                    free, value = bank_free[(j + h) % 3], (j + h) // 3 + 1
                    dst = td[:] if b else merged[:, ft, :]
                    V.tensor_tensor(dst, tiles(W[(j + h) % 3][:]), sgate[:, ft, :], ALU.mult).then_inc(free, 1)
                    if b:
                        dve.wait_ge(free, value)
                        mark(V.tensor_tensor(merged[:, ft, :], merged[:, ft, :], td[:], ALU.add),
                             "gated", 8 * l + 4 * (b - 1) + 2 * q + h + 1)

            def shift(l, q):
                wait_jobs(dve, l * MIX_JOBS + (JOB0["lora"] if q == 6 else JOB0["rkv"] + q) + 1)
                c = slice(2 * q, 2 * q + 2)
                link(V.tensor_tensor(dsh[:, c, 1:T], rkvl[:, c, 0:T - 1], rkvl[:, c, 1:T], ALU.subtract))
                link(V.tensor_scalar(dsh[:, c, 0:1], rkvl[:, c, 0:1], -1.0, None, ALU.mult))
                for i in (2 * q, 2 * q + 1):
                    last = V.scalar_tensor_tensor(rkvl[:, i, :], dsh[:, i, :], par_col(l, "mu", i), rkvl[:, i, :],
                                                  ALU.mult, ALU.add)
                if q == 6:
                    mark(last, "lora_shifted", l + 1)
                else:
                    link(last)

            def conv(l, half):
                if half == 0:
                    wait_jobs(dve, l * MIX_JOBS + JOB0["gate0"])
                m = range(2 * half, 2 * half + 2)
                ch, cb, cc = (share[:, 4 * s + 2 * half:4 * s + 2 * half + 2, :] for s in range(3))
                link(V.tensor_tensor(cc, cc, ch, ALU.mult))
                for i in range(2):
                    last = V.tensor_scalar(ch[:, i, :], cc[:, i, :], par_col(l, "conv2", m[i]), None, ALU.mult)
                for tap, back in (("conv1", 1), ("conv0", 2)):
                    link(last)
                    for i in range(2):
                        last = V.scalar_tensor_tensor(ch[:, i, back:T], cc[:, i, 0:T - back], par_col(l, tap, m[i]),
                                                      ch[:, i, back:T], ALU.mult, ALU.add)
                link(last)
                mark(V.tensor_tensor(ch, ch, cb, ALU.mult), "conv_ready", 2 * l + half + 1)

            def decay(l, p):
                n = 2 * l + p
                dve.wait_ge(sem("rate_w_ready"), n + 1)
                for m in range(2):
                    for c in range(NT):
                        tc = slice(c * P, (c + 1) * P)
                        last = V.tensor_tensor_scan(t2[:, m, tc], t1[:, m, tc], t1[:, m, tc], 0.0, ALU.add, ALU.bypass)
                link(last)
                t2c = t2[:].rearrange("p m (c t) -> p (m c) t", c=NT)
                link(V.tensor_scalar(small[:, 0:4], t2c[:, :, P - 1], 0.5, None, ALU.mult))
                half = small[:, 0:4]
                V.tensor_tensor(state_decay[p], tiles(half)[:, :, 0], tiles(half)[:, :, 1], ALU.add)
                link(V.tensor_tensor(t2c, t2c, half.unsqueeze(2).to_broadcast([P, 4, P]), ALU.subtract))
                mark(V.tensor_tensor(t1[:], t2[:], t1[:], ALU.subtract), "decay_ready", n + 1)

            def ksq(l, p):
                for m in range(2):
                    last = V.tensor_scalar(t6[:, m, :], rkvl[:, 4 + 2 * p + m, :], par_col(l, "k_k", 2 * p + m), None, ALU.mult)
                link(last)
                mark(V.tensor_tensor(td[:], t6[:], t6[:], ALU.mult), "ksq_ready", 2 * l + p + 1)

            def kk(l, p):
                dve.wait_ge(sem("knorm_ready"), 2 * l + p + 1)
                link(V.tensor_scalar(td[:], td[:], 1e-12, None, ALU.max))
                link(V.reciprocal(td[:], td[:]))
                link(V.scalar_tensor_tensor(t6[:], t6[:], -1.0, td[:], ALU.mult, ALU.mult))

            def prep(l, p):
                n = 2 * l + p
                r, k = (rkvl[:, 4 * s + 2 * p:4 * s + 2 * p + 2, :] for s in range(2))
                dve.wait_ge(sem("exp_ready"), n + 1)
                dve.wait_ge(sem("rates_ready"), n + 1)
                V.tensor_tensor(t1[:], t6[:], t1[:], ALU.mult)
                V.tensor_tensor(t2[:], r, t2[:], ALU.mult)
                link(V.scalar_tensor_tensor(td[:], t6[:], -1.0, t4[:], ALU.mult, ALU.mult))
                link(V.tensor_tensor(t6[:], td[:], t3[:], ALU.mult))
                for m in range(2):
                    last = V.tensor_scalar(t4[:, m, :], t4[:, m, :], -1.0, par_col(l, "k_a", 2 * p + m), ALU.add, ALU.mult)
                link(last)
                link(V.scalar_tensor_tensor(k, t4[:], 1.0, k, ALU.add, ALU.mult))
                V.tensor_tensor(t3[:], k, t3[:], ALU.mult)
                for m in range(2):
                    last = V.scalar_tensor_tensor(td[:, m, :], r[:, m, :], par_col(l, "r_k", 2 * p + m), k[:, m, :],
                                                  ALU.mult, ALU.mult)
                mark(last, "prep_ready", n + 1)

            def decayed(l, p):
                n = 2 * l + p
                if n == 0:
                    dve.wait_ge(sem("ar_zero"), 1)
                arv = ar[:].rearrange("p (m h) c s t -> p m h c s t", h=2)
                for s, src in ((0, t1), (1, t2)):
                    for h in range(2):
                        rows = slice(h * HD, (h + 1) * HD)
                        last = V.tensor_copy(arv[rows, :, h, :, s, :], src[rows].rearrange("p m (c t) -> p m c t", c=NT))
                mark(last, "decayed_ready", n + 1)

            def bonus(l, p):
                n = 2 * l + p
                dve.wait_ge(sem("bonus_done"), n + 1)
                mark(V.tensor_tensor(rkvl[:, 2 * p:2 * p + 2, :], tiles(Y[3][:]), rkvl[:, 8 + 2 * p:10 + 2 * p, :], ALU.mult),
                     "bonus_ready", n + 1)

            def mask_level(n, v, c):
                return V.tensor_tensor(mt[:, 4 * c:4 * c + 4, :], sc[:, 4 * c:4 * c + 4, 0, :], level_mask(v), ALU.mult)

            def scores(l, p):
                n = 2 * l + p
                if n == 2:
                    dve.wait_ge(sem("xtok_ready"), 2)
                si = cst[:, C_SI:C_SI + 2 * P].unsqueeze(1).to_broadcast([P, 2, 2 * P])
                for u in range(8):
                    dve.wait_ge(sem("score_done"), 8 * n + u + 1)
                    mark(V.tensor_tensor(sc[:, u].rearrange("p (b s) t -> p b (s t)", b=2), tiles(Y[(1 + u) % 4][:]), si, ALU.mult),
                         "score_ready", 8 * n + u + 1)

            def invert(l, p):
                n = 2 * l + p
                for c in range(NT):
                    link(mask_level(n, 0, c))
                    mark(V.tensor_tensor(xt[:, 4 * c:4 * c + 4, :], mt[:, 4 * c:4 * c + 4, :],
                                         ident.unsqueeze(1).to_broadcast([P, 4, P]), ALU.add),
                         "xt_ready", 2 * LEVELS * n + c + 1)
                for c in range(NT):
                    mark(mask_level(n, 1, c), "mt_ready", 2 * (LEVELS - 1) * n + c + 1)

            def level(l, p, v):
                n = 2 * l + p
                for c in range(NT):
                    dve.wait_ge(sem("dxt_done"), 2 * (LEVELS - 1) * n + 2 * (v - 1) + c + 1)
                    mark(V.tensor_tensor(xt[:, 4 * c:4 * c + 4, :], xt[:, 4 * c:4 * c + 4, :], tiles(Y[2 + c][:], 4), ALU.add),
                         "xt_ready", 2 * LEVELS * n + 2 * v + c + 1)
                if v < LEVELS - 1:
                    for c in range(NT):
                        mark(mask_level(n, v + 1, c), "mt_ready", 2 * (LEVELS - 1) * n + 2 * v + c + 1)

            def chain(l, p, c):
                n = 2 * l + p
                dve.wait_ge(sem("g_done"), 2 * n + c + 1)
                mark(V.tensor_copy(g_s[:].rearrange("p a b -> p (a b)"), Y[0][:, 0:256]), "g_ready", 2 * n + c + 1)
                dve.wait_ge(sem("u_done"), 2 * n + c + 1)
                mark(V.tensor_copy(u_s[:].rearrange("p a b -> p (a b)"), Y[1][:, 0:256]), "u_ready", 2 * n + c + 1)
                if c == 0:
                    dve.wait_ge(sem("s_done"), n + 1)
                    mark(V.tensor_tensor(s_s[:], tiles(Y[3][:, 0:256]), state_decay[p].unsqueeze(2).to_broadcast([P, 2, P]),
                                         ALU.mult), "s_ready", n + 1)

            def finish(l, p):
                n = 2 * l + p
                dst = rkvl[:, 2 * p:2 * p + 2, :]
                dve.wait_ge(sem("y_done"), 2 * n + 2)
                mark(V.tensor_copy(fin1, tiles(E[:])), "yrow_ready", n + 1)
                dve.wait_ge(sem("mean_done"), n + 1)
                link(V.scalar_tensor_tensor(fin1, tiles(Y[0][:]), -1.0 / HD, fin1, ALU.mult, ALU.add))
                mark(V.tensor_tensor(fin2, fin1, fin1, ALU.mult), "ysq_ready", n + 1)
                dve.wait_ge(sem("gn_sd_ready"), n + 1)
                link(V.reciprocal(fin2, fin2))
                link(V.tensor_tensor(fin1, fin1, fin2, ALU.mult))
                for m in range(2):
                    last = V.tensor_scalar(fin1[:, m, :], fin1[:, m, :], par_col(l, "gn_g", 2 * p + m),
                                           par_col(l, "gn_b", 2 * p + m), ALU.mult, ALU.add)
                link(last)
                link(V.tensor_tensor(fin1, fin1, dst, ALU.add))
                dve.wait_ge(sem("gatemul_done"), n + 1)
                mark(V.tensor_tensor(dst, fin1, tiles(Y[2][:]), ALU.mult), "pass_done", n + 1)

            def rope(l, s):
                src = share[:, 2 * s:2 * s + 2, :]
                cos, sin = (cst[:, a:a + T].unsqueeze(1).to_broadcast([P, 2, T]) for a in (C_COS, C_SIN))
                dve.wait_ge(sem("rot_done"), 4 * l + s + 1)
                V.tensor_tensor(t1[:], tiles(E[:]), sin, ALU.mult)
                link(V.tensor_tensor(t2[:], src, cos, ALU.mult))
                mark(V.tensor_tensor(src, t1[:], t2[:], ALU.add), "rope_ready", 4 * l + s + 1)

            def heads(l):
                qpv = qp[:].rearrange("p (m h) t -> p m h t", h=2)
                for h in range(2):
                    last = V.memset(qpv[(1 - h) * HD:(2 - h) * HD, :, h, :], 0.0)
                last.then_inc(sem("qp_zero"), 1)

            def att_scores(l):
                dve.wait_ge(sem("cat_full"), 16 * (l + 1))
                mask = cat[:]
                for h in range(8):
                    dve.wait_ge(sem("att_sc_done"), 8 * l + h + 1)
                    mark(V.scalar_tensor_tensor(pr[:, h].rearrange("p s q -> p (s q)"), Y[(2 + h) % 4][:, 0:3 * P], HD ** -0.5,
                                                mask, ALU.mult, ALU.add), "att_sc_ready", 8 * l + h + 1)
                    V.reduce_max(small[:, 16 + 2 * h:17 + 2 * h], pr[:, h, 0, :], AX.X)
                    last = V.reduce_max(small[:, 17 + 2 * h:18 + 2 * h], pr[:, h, 1:3, :].rearrange("p s q -> p (s q)"), AX.X)
                link(last)
                mark(V.tensor_scalar(small[:, 16:32], small[:, 16:32], -1.0, None, ALU.mult), "max_ready", l + 1)

            def softmax(l, half):
                dve.wait_ge(sem("e_ready"), 2 * l + half + 1)
                total, hh = small[:, 32 + 8 * half:40 + 8 * half], slice(4 * half, 4 * half + 4)
                link(V.reciprocal(total, total))
                inv = total.rearrange("p (h q) -> p h q", q=2)
                V.tensor_tensor(pr[:, hh, 0, :], pr[:, hh, 0, :], inv[:, :, 0:1].to_broadcast([P, 4, P]), ALU.mult)
                late = pr[:, hh, 1:3, :].rearrange("p h s q -> p h (s q)")
                mark(V.tensor_tensor(late, late, inv[:, :, 1:2].to_broadcast([P, 4, 2 * P]), ALU.mult), "prob_ready", 2 * l + half + 1)

            def att_out(l):
                dve.wait_ge(sem("o_half_ready"), l + 1)
                V.tensor_tensor(o_lo[:, 0:2, :], tiles(E[:]), o_hi[:, 0:2, :].bitcast(F32), ALU.subtract)
                dve.wait_ge(sem("o_hi_ready"), 3 * l + 3)
                V.tensor_tensor(o_lo[:, 2:4, :], tiles(Y[3][:]), o_hi[:, 2:4, :].bitcast(F32), ALU.subtract)\
                    .then_inc(sem("o_lo_ready"), 1)

            def osplit(l, b):
                dve.wait_ge(sem("o_hi_ready"), 3 * l + b + 1)
                V.tensor_tensor(o_lo[:], (rkvl if b else share)[:, 0:BT, :], o_hi[:].bitcast(F32), ALU.subtract)\
                    .then_inc(sem("o_lo_ready"), 1)

            def msplit(l, half):
                for q in (2 * half, 2 * half + 1):
                    dve.wait_ge(sem("mhi_ready"), 4 * l + q + 1)
                    c = slice(2 * q, 2 * q + 2)
                    V.tensor_tensor(x_lo[:, c, :], merged[:, c, :], x_hi[:, c, :].bitcast(F32), ALU.subtract)\
                        .then_inc(sem("mlo_ready"), 1)

            def layer_norm(m, src, added=None, used=0):
                def moments(t, h):
                    if added and h == 0:
                        if t == 0:
                            dve.wait_ge(sem("sum_done"), m + 1)
                        else:
                            dve.wait_ge(w_used, used)
                    part = src[:, t, h * 512:(h + 1) * 512]
                    if added:
                        link(V.scalar_tensor_tensor(part, part, ALPHA, added(t, h), ALU.mult, ALU.add))
                    link(V.bn_stats(small[:, 56 + 12 * t + 6 * h:62 + 12 * t + 6 * h], part))
                    if h:
                        mark(V.bn_aggr(small[:, 80 + 2 * t:82 + 2 * t], small[:, 56 + 12 * t:68 + 12 * t]),
                             "ln_var_ready", NT * m + t + 1)

                def finish_out(t):
                    x_t = xtok[:, t, :]
                    link(V.scalar_tensor_tensor(x_t, src[:, t, :], small[:, 80 + 2 * t:81 + 2 * t], gb[:, 0, :],
                                                ALU.subtract, ALU.mult))
                    dve.wait_ge(sem("ln_sd_ready"), NT * m + t + 1)
                    link(V.reciprocal(small[:, 54 + t:55 + t], small[:, 50 + t:51 + t]))
                    V.scalar_tensor_tensor(x_t, x_t, small[:, 54 + t:55 + t], gb[:, 1, :], ALU.mult, ALU.add)\
                        .then_inc(sem("out_ready"), 1)

                def normalise(t):
                    if not added:
                        finish_out(t)
                        return
                    dve.wait_ge(sem("ln_sd_ready"), NT * m + t + 1)
                    link(V.reciprocal(small[:, 54 + t:55 + t], small[:, 50 + t:51 + t]))
                    mark(V.tensor_scalar(xtok[:, t, :], src[:, t, :], small[:, 80 + 2 * t:81 + 2 * t],
                                         small[:, 54 + t:55 + t], ALU.subtract, ALU.mult), "xn_ready", NT * m + t + 1)

                moments(0, 0)
                moments(0, 1)
                moments(1, 0)
                normalise(0)
                moments(1, 1)
                normalise(1)

            def feature_major(m, l, which):
                def lo(k):
                    dve.wait_ge(sem("x_hi_ready"), 4 * (m + 1) + k + 1)
                    c = slice(2 * k, 2 * k + 2)
                    V.tensor_tensor(x_lo[:, c, :], xf[:, c, :], x_hi[:, c, :].bitcast(F32), ALU.subtract)\
                        .then_inc(sem("x_lo_ready"), 1)

                split = m < 2
                for k in range(4):
                    dve.wait_ge(sem("xnt_done"), 4 * m + k + 1)
                    for kk in (2 * k, 2 * k + 1):
                        last = V.tensor_scalar(xf[:, kk, :], tiles(NB[k][:])[:, kk % 2, :], par_col(l, f"ln{which}_g", kk),
                                               par_col(l, f"ln{which}_b", kk), ALU.mult, ALU.add)
                    mark(last, "xf_ready", 4 * m + k + 1)
                    if split and k:
                        lo(k - 1)
                if split:
                    lo(3)

            def hidden(f, nt, transposed):
                odd, f = f
                dve.wait_ge(sem("silu_ready"), f + 1)
                if not isinstance(f, int) or f >= 2:
                    dve.wait_ge(sem("ht_done"), transposed)
                V.tensor_tensor(hid[:, odd, 0:nt, :], sil[:, odd, 0:nt, :], tiles(W[odd][:])[:, 0:nt, P:2 * P],
                                ALU.mult).then_inc(sem("hid_ready"), 1)

            def hid_lo(g, nt):
                dve.wait_ge(sem("hhi_ready"), g + 1)
                V.tensor_tensor(o_lo[:, 0:2, 0:nt * P], tiles(W[2][:])[:, :, 0:nt * P],
                                o_hi[:, 0:2, 0:nt * P].bitcast(F32), ALU.subtract).then_inc(sem("hlo_ready"), 1)

            def first_pair(u, i, g, nt):
                split_lo(u + 2, i)
                hidden((0, 2 * g), nt, g)
                split_lo(u + 3, i)
                hidden((1, 2 * g + 1), nt, g)

            def pair(u, i, g, nt, j, ahead):
                split_lo(u + 4, i + j - 1)
                hidden((0, 2 * (g + j)), nt, g + j)
                hid_lo(g + j - 1, nt)
                split_lo(u + 5, i + j - 1)
                hidden((1, 2 * (g + j) + 1), nt, g + j)
                if ahead:
                    split_lo(u + 6, i + j - 1)

            def middle_pairs(u, i, g, nt, ahead=True, e=None, choose=None):
                start = 1
                if e is not None:
                    pair(u, i, g, nt, 1, True)
                    if ahead:
                        choose(e)
                    start = 2
                with dve.Fori(start, NPAIR if ahead else NPAIR - 1) as j:
                    pair(u, i, g, nt, j, True)
                if not ahead:
                    pair(u, i, g, nt, NPAIR - 1, False)

            def rows_lo(n):
                dve.wait_ge(sem("rows_hi"), n + 1)
                for s in range(2):
                    c = slice(4 * s, 4 * s + 4)
                    last = V.tensor_tensor(x_lo[:, c, 0:P], tiles(Y[2 + s][:], 4), x_hi[:, c, 0:P].bitcast(F32), ALU.subtract)
                last.then_inc(sem("rows_ready"), 1)

            def last_down(u, i, g, nt, ahead=True, n=None):
                hid_lo(g + NPAIR - 1, nt)
                if ahead and n is not None:
                    rows_lo(n + 1)
                if ahead:
                    split_lo(u + 4, i + NPAIR - 1)

            def routing():
                dve.wait_ge(sem("logits_done"), 1)
                i8 = cmo[:, E_I8:E_I8 + NE].unsqueeze(1).to_broadcast([P, NT, NE])

                def cols(a, n=NE):
                    return route[:, :, a:a + n]

                def each(a):
                    return cols(a, 1).to_broadcast([P, NT, NE])

                for t in range(NT):
                    last = V.max(route[:, t, R_TOP:R_TOP + 8], Y[1][:, t * NE:(t + 1) * NE])
                link(last)
                for t in range(NT):
                    last = V.max_index(idx[:, t, :], route[:, t, R_TOP:R_TOP + 8], Y[1][:, t * NE:(t + 1) * NE])
                V.tensor_tensor(cols(R_EXP, 1), cols(R_TOP + 1, 1), cols(R_TOP, 1), ALU.subtract).then_inc(sem("top_ready"), 1)
                dve.wait_ge(sem("top_ready"), 1)
                link(V.tensor_copy(cols(R_IDX, 2), idx[:, :, 0:2]))
                V.tensor_tensor(cols(R_ONE), i8, each(R_IDX), ALU.is_equal)
                link(V.tensor_tensor(cols(R_TWO), i8, each(R_IDX + 1), ALU.is_equal))
                mark(V.tensor_tensor(cols(R_MASK), cols(R_ONE), cols(R_TWO), ALU.add), "mask_ready", 1)
                dve.wait_ge(sem("gexp_ready"), 1)
                link(V.tensor_scalar(cols(R_GATE, 1), cols(R_EXP, 1), 1.0, None, ALU.add))
                link(V.reciprocal(cols(R_GATE, 1), cols(R_GATE, 1)))
                link(V.tensor_tensor(cols(R_GATE + 1, 1), cols(R_EXP, 1), cols(R_GATE, 1), ALU.mult))
                V.tensor_tensor(cols(R_ONE), cols(R_ONE), each(R_GATE), ALU.mult)
                link(V.tensor_tensor(cols(R_TWO), cols(R_TWO), each(R_GATE + 1), ALU.mult))
                V.tensor_tensor(gsel[:], cols(R_ONE), cols(R_TWO), ALU.add)
                dve.wait_ge(sem("place_done"), 1)
                place = Y[0][:, 32:48].rearrange("p (t e) -> p t e", t=NT)
                link(V.scalar_tensor_tensor(cols(R_POS), place, 1.0, cols(R_MASK), ALU.add, ALU.mult))
                link(V.tensor_scalar(posm[:], cols(R_POS), -1.0, None, ALU.add))
                link(V.reduce_max(small[:, 48:49], Y[0][:, 48:56], AX.X))
                mark(V.tensor_scalar(flag[:, 0:1], small[:, 48:49], P + 0.5, None, ALU.is_gt), "flag_ready", 1)

            def experts(u, g, q, chunk, cold):
                iota = cmo[:, E_IOTA + chunk * P:E_IOTA + (chunk + 1) * P]

                def select(e):
                    for t in range(NT):
                        last = V.tensor_scalar(sel[:, t, :], iota, posm[:, t, bass.ds(e, 1)], None, ALU.is_equal)
                    last.then_inc(sem("sel_ready"), 1)

                def choose(e):
                    dve.wait_ge(sem("selt_done"), q + e + 1)
                    select(e + 1)

                def expert(e, follow):
                    n = q + e
                    middle_pairs(u, NPAIR * e, g + NPAIR * e, 1, follow, e, choose)
                    last_down(u, NPAIR * e, g + NPAIR * e, 1, follow, n)
                    dve.wait_ge(sem("yrows_hi"), n + 1)
                    for h in range(2):
                        c = slice(h * 512, (h + 1) * 512)
                        last = V.tensor_tensor(y_lo[:, c], Y[h][:], y_hi[:, c].bitcast(F32), ALU.subtract)
                    last.then_inc(sem("yrows_ready"), 1)
                    if follow:
                        first_pair(u + FFN_UNITS, NPAIR * e, g + NPAIR * e + NPAIR, 1)
                    for t, banks in ((0, (Y[2], Y[3])), (1, (E, W[2]))):
                        dve.wait_ge(sem("comb_done"), 2 * n + t + 1)
                        for h in range(2):
                            part = facc[:, t, h * 512:(h + 1) * 512]
                            last = V.scalar_tensor_tensor(part, banks[h][:], gsel[:, t, bass.ds(e, 1)], part, ALU.mult, ALU.add)
                    last.then_inc(sem("facc_ready"), 1)

                if cold:
                    split_lo(u)
                    split_lo(u + 1)
                select(0)
                if not cold:
                    dve.wait_ge(sem("xtok_ready"), 3)
                    mark(V.tensor_scalar(facc[:], xtok[:], ALPHA, None, ALU.mult), "facc_ready", 1)
                rows_lo(q)
                first_pair(u, 0, g, 1)
                with dve.Fori(0, NE - 1) as e:
                    expert(e, True)
                expert(NE - 1, False)

            for k in range(4):
                dve.wait_ge(sem("x_hi_ready"), k + 1)
                c = slice(2 * k, 2 * k + 2)
                V.tensor_tensor(x_lo[:, c, :], xf[:, c, :], x_hi[:, c, :].bitcast(F32), ALU.subtract)\
                    .then_inc(sem("x_lo_ready"), 1)
            split_lo(0)
            dve.wait_ge(sem("prm_full"), 16)
            handlers = {"units": units, "shift": shift, "conv": conv, "decay": decay, "ksq": ksq, "kk": kk, "prep": prep,
                        "decayed": decayed, "bonus": bonus, "scores": scores, "invert": invert, "level": level, "chain": chain,
                        "finish": finish, "rope": rope, "heads": heads, "att_scores": att_scores, "softmax": softmax,
                        "att_out": att_out, "osplit": osplit, "msplit": msplit}
            for l in range(L):
                for name, *args in TIMELINE:
                    if name in handlers:
                        handlers[name](l, *args)
                dve.wait_ge(sem("xres_full"), 16 * (l + 1))
                layer_norm(2 * l, xtok, lambda t, h: Y[2 * t + h][:], layer_unit(l) + MIX_UNITS)
                feature_major(2 * l, l, 1)
                if l == 0:
                    first_pair(MIX_UNITS, 0, 0, NT)
                    middle_pairs(MIX_UNITS, 0, 0, NT)
                    last_down(MIX_UNITS, 0, 0, NT)
                    dve.wait_ge(sem("xtok_ready"), 1)
                    layer_norm(1, xtok, lambda t, h: Y[2 * t + h][:], layer_unit(1))
                    feature_major(1, 0, 2)
            routing()
            experts(MOE_U0, NPAIR, 0, 0, False)
            with dve.If(dve.value_load(flag[0:1, 0:1], min_val=0, max_val=1)):
                experts(END_U, NPAIR * (NE + 1), NE, 1, True)
            link(V.engine_nop())
            dve.wait_ge(sem("gb_full"), 64)
            layer_norm(3, facc)


def constants():
    i, j = np.arange(P)[:, None], np.arange(P)[None, :]
    rot = np.where((j % HD < HD // 2) & (i == j + HD // 2), -1.0, 0.0) + np.where((j % HD >= HD // 2) & (i == j - HD // 2), 1.0, 0.0)
    levels = [((i >> v) % 2 == 0) & ((j >> v) == (i >> v) + 1) for v in range(LEVELS)]
    general = np.concatenate([i == j, (i // HD) == (j // HD), rot, i < j, i <= j] + levels, 1)
    half = HD // 2
    inv = np.float32(10000.0) ** (-np.arange(half, dtype=np.float32) / np.float32(half))
    ang = (np.arange(T, dtype=np.float32)[None, :] * inv[:, None]).astype(np.float32)
    causal = np.where(j <= i, 0.0, -1e30)
    general = np.concatenate([general, np.tile(np.cos(ang), (4, 1)), np.tile(np.sin(ang), (4, 1))], 1)
    att = np.concatenate([causal, 0 * causal, causal], 1)
    row = np.arange(2 * P)[None, :] + 0 * i
    moe = np.concatenate([np.ones((P, P)), row, row[:, :NE]], 1)
    return [np.ascontiguousarray(c, dtype=np.float32) for c in (general, att, moe)]


def kernel(**inputs):
    import concourse.bacc as bacc
    from concourse.bass_utils import run_bass_kernel_spmd

    a = {k: np.asarray(v) for k, v in inputs.items()}

    def columns(v):
        return v.reshape(L, -1, P).transpose(0, 2, 1)

    conv = a["conv_w"]
    par = np.concatenate([columns(v) for v in (
        a["shift_mu"], a["decay_w0"], a["aaa_a0"], a["k_k"], a["k_a"], a["r_k"], a["gn_g"], a["gn_b"],
        conv[:, 0], conv[:, 1], conv[:, 2], a["ln1_g"], a["ln1_b"], a["ln2_g"], a["ln2_b"])], 2).transpose(1, 0, 2)
    w2 = np.zeros((L, P, 2, BR), np.float32)
    w2[:, 0:64, 0], w2[:, 64:128, 1] = a["decay_w2"], a["aaa_w2"]
    ln_gb = np.stack([np.stack([a[f"ln{k}_g"][l], a[f"ln{k}_b"][l]]) for l in range(L) for k in (1, 2)])
    ln_gb = np.broadcast_to(ln_gb[:, None], (2 * L, P, 2, D))
    general, att, moe = constants()
    x = a["x"].reshape(T, D)
    data = {
        "x": x, "x_t": x.T.reshape(KD, P, T).transpose(1, 0, 2), "w_in": a["w_in"], "w_branch": a["w_branch"],
        "w_out": a["w_out"], "w2": w2, "gate_w2": a["gate_w2"], "par": par, "const": general, "const_att": att,
        "const_moe": moe, "ln_gb": ln_gb, "router": a["router_w"][0].reshape(KD, P, NE).transpose(1, 0, 2),
        "ffn_gate": a["ffn_w_gate"][0], "ffn_up": a["ffn_w_up"][0], "ffn_down": a["ffn_w_down"][0],
        "moe_gate": a["moe_w_gate"].reshape(NE * D, DFF), "moe_up": a["moe_w_up"].reshape(NE * D, DFF),
        "moe_down": a["moe_w_down"].reshape(NE * DFF, D),
    }
    nc = bacc.Bacc("TRN2", target_bir_lowering=False, num_devices=1)
    arrays = {k: np.ascontiguousarray(v) for k, v in data.items()}
    aps = [nc.dram_tensor(k, v.shape, mybir.dt.from_np(v.dtype), kind="ExternalInput").ap() for k, v in arrays.items()]
    result = nc.dram_tensor("result", (T, D), F32, kind="ExternalOutput").ap()
    trunk(nc, *aps, result)
    r = run_bass_kernel_spmd(nc, [arrays], core_ids=[0])
    return r.results[0]["result"].reshape(1, T, D)
```
